# Optimizing a Trainium2 kernel written in Bass

```python
import jax, jax.numpy as jnp
from jax import lax
import numpy as np

D_MODEL = 1024
BATCH = 1
SEQ = 512
DEPTH = 2

ATT_WIDTH = D_MODEL // 2
ATT_DIM = 64
ATT_HEADS = ATT_WIDTH // ATT_DIM
ATT_KV_HEADS = 2
KV_WIDTH = ATT_KV_HEADS * ATT_DIM
ROPE_DIM = ATT_DIM // 4
ROPE_THETA = 500000.0
CMP_BLOCK = 32
CMP_STRIDE = 16
SEL_BLOCK = 64
SEL_TOPK = 16
WINDOW = 512
Q_BLOCK = 128
FORCE_BONUS = 1.0e4
M_WIDTH = D_MODEL - ATT_WIDTH
M_HEADS = 4
M_DIM = M_WIDTH // M_HEADS
M_CHUNK = 64
M_CONV = 4
D_FF = ((8 * D_MODEL // 3 + 127) // 128) * 128
FFN_CONV = 3
RMS_EPS = 1e-6
IN_SIZES = (ATT_WIDTH, KV_WIDTH, KV_WIDTH, KV_WIDTH, KV_WIDTH, KV_WIDTH, KV_WIDTH,
            3 * ATT_HEADS, 2 * M_WIDTH, M_WIDTH, 2 * M_HEADS, M_WIDTH)
IN_COLS = sum(IN_SIZES)

kernel_name = 'hybrid_nsa_mlstm_convffn_adaln'

def rms_norm(x, g):
    x32 = x.astype(jnp.float32)
    y = x32 * lax.rsqrt(jnp.mean(x32 * x32, axis=-1, keepdims=True) + RMS_EPS)
    return y.astype(x.dtype) * g

def head_rms_norm(x, g, n_heads):
    B, S, W = x.shape
    x32 = x.reshape(B, S, n_heads, W // n_heads).astype(jnp.float32)
    y = x32 * lax.rsqrt(jnp.mean(x32 * x32, axis=-1, keepdims=True) + RMS_EPS)
    return y.reshape(B, S, W).astype(x.dtype) * g

def rope_tables(positions):
    inv_freq = ROPE_THETA ** (-jnp.arange(0, ROPE_DIM, 2, dtype=jnp.float32) / ROPE_DIM)
    ang = positions.astype(jnp.float32)[..., None] * inv_freq
    return jnp.cos(ang)[:, :, None, :], jnp.sin(ang)[:, :, None, :]

def apply_rope(x, cos, sin):
    half = ROPE_DIM // 2
    x1 = x[..., :half].astype(jnp.float32)
    x2 = x[..., half:ROPE_DIM].astype(jnp.float32)
    rot = jnp.concatenate([x1 * cos - x2 * sin, x1 * sin + x2 * cos], axis=-1).astype(x.dtype)
    return jnp.concatenate([rot, x[..., ROPE_DIM:]], axis=-1)

def causal_dwconv(x, w, b):
    K = w.shape[0]
    S = x.shape[1]
    xp = jnp.pad(x, ((0, 0), (K - 1, 0), (0, 0)))
    y = b
    for k in range(K):
        y = y + xp[:, k:k + S] * w[k]
    return y

def masked_softmax(s, mask):
    s = jnp.where(mask, s, -jnp.inf)
    m = jnp.max(s, axis=-1, keepdims=True)
    m = jnp.where(jnp.isfinite(m), m, 0.0)
    p = jnp.exp(s - m)
    d = jnp.sum(p, axis=-1, keepdims=True)
    return p / jnp.where(d > 0, d, 1.0)

def compress(k, pos, w1, w2):
    B, S, G, D = k.shape
    n_cmp = (S - CMP_BLOCK) // CMP_STRIDE + 1
    idx = jnp.arange(n_cmp)[:, None] * CMP_STRIDE + jnp.arange(CMP_BLOCK)[None, :]
    blocks = k[:, idx] + pos[:, None, :]
    flat = blocks.transpose(0, 1, 3, 2, 4).reshape(B, n_cmp, G, CMP_BLOCK * D)
    return jax.nn.silu(flat @ w1) @ w2

def selection_overlap(seq_len):
    n_cmp = (seq_len - CMP_BLOCK) // CMP_STRIDE + 1
    n_sel = seq_len // SEL_BLOCK
    c_start = jnp.arange(n_cmp)[:, None] * CMP_STRIDE
    s_start = jnp.arange(n_sel)[None, :] * SEL_BLOCK
    ov = (c_start <= s_start + SEL_BLOCK - 1) & (c_start + CMP_BLOCK - 1 >= s_start)
    return ov.astype(jnp.float32)

def nsa_attention(q, k_cmp, v_cmp, k_slc, v_slc, k_win, v_win, gates, overlap):
    B, S, H, D = q.shape
    G = k_slc.shape[2]
    R = H // G
    n_cmp = k_cmp.shape[1]
    n_sel = S // SEL_BLOCK
    k_top = min(SEL_TOPK, n_sel)
    scale = D ** -0.5
    f32 = jnp.float32
    cmp_end = jnp.arange(n_cmp) * CMP_STRIDE + CMP_BLOCK - 1
    ks_blocks = k_slc.reshape(B, n_sel, SEL_BLOCK, G, D).transpose(0, 3, 1, 2, 4)
    vs_blocks = v_slc.reshape(B, n_sel, SEL_BLOCK, G, D).transpose(0, 3, 1, 2, 4)
    kw_pad = jnp.pad(k_win, ((0, 0), (WINDOW, 0), (0, 0), (0, 0)))
    vw_pad = jnp.pad(v_win, ((0, 0), (WINDOW, 0), (0, 0), (0, 0)))
    v_cmp32 = v_cmp.astype(f32)
    bi = jnp.arange(B)[:, None, None, None]
    gi = jnp.arange(G)[None, :, None, None]
    jsel = jnp.arange(n_sel)

    def block(qb):
        t0 = qb * Q_BLOCK
        tpos = t0 + jnp.arange(Q_BLOCK)
        qblk = lax.dynamic_slice_in_dim(q, t0, Q_BLOCK, axis=1).reshape(B, Q_BLOCK, G, R, D)
        gblk = lax.dynamic_slice_in_dim(gates, t0, Q_BLOCK, axis=1).reshape(B, Q_BLOCK, G, R, 3).astype(f32)
        s_c = jnp.einsum('bqgrd,bngd->bgrqn', qblk, k_cmp).astype(f32) * scale
        p_c = masked_softmax(s_c, cmp_end[None, :] <= tpos[:, None])
        o_cmp = jnp.einsum('bgrqn,bngd->bqgrd', p_c, v_cmp32)
        imp = jnp.einsum('bgrqn,nj->bgqj', p_c, overlap)
        j_cur = tpos // SEL_BLOCK
        valid = jsel[None, :] * SEL_BLOCK <= tpos[:, None]
        forced = (jsel[None, :] == 0) | (jsel[None, :] == j_cur[:, None]) | (jsel[None, :] == j_cur[:, None] - 1)
        score = jnp.where(valid, imp + jnp.where(forced, FORCE_BONUS, 0.0), -jnp.inf)
        top_vals, sel_idx = lax.top_k(score, k_top)
        k_sel = ks_blocks[bi, gi, sel_idx]
        v_sel = vs_blocks[bi, gi, sel_idx]
        s_s = jnp.einsum('bqgrd,bgqkld->bgrqkl', qblk, k_sel).astype(f32) * scale
        kpos = sel_idx[..., None] * SEL_BLOCK + jnp.arange(SEL_BLOCK)
        m_s = jnp.isfinite(top_vals)[..., None] & (kpos <= tpos[:, None, None])
        p_s = masked_softmax(s_s.reshape(B, G, R, Q_BLOCK, k_top * SEL_BLOCK),
                             m_s.reshape(B, G, 1, Q_BLOCK, k_top * SEL_BLOCK))
        o_slc = jnp.einsum('bgrqm,bgqmd->bqgrd', p_s,
                           v_sel.reshape(B, G, Q_BLOCK, k_top * SEL_BLOCK, D).astype(f32))
        k_w = lax.dynamic_slice_in_dim(kw_pad, t0, Q_BLOCK + WINDOW, axis=1)
        v_w = lax.dynamic_slice_in_dim(vw_pad, t0, Q_BLOCK + WINDOW, axis=1)
        wpos = t0 - WINDOW + jnp.arange(Q_BLOCK + WINDOW)
        m_w = (wpos[None, :] <= tpos[:, None]) & (wpos[None, :] > tpos[:, None] - WINDOW) & (wpos[None, :] >= 0)
        s_w = jnp.einsum('bqgrd,bkgd->bgrqk', qblk, k_w).astype(f32) * scale
        p_w = masked_softmax(s_w, m_w)
        o_win = jnp.einsum('bgrqk,bkgd->bqgrd', p_w, v_w.astype(f32))
        o = gblk[..., 0:1] * o_cmp + gblk[..., 1:2] * o_slc + gblk[..., 2:3] * o_win
        return o.reshape(B, Q_BLOCK, H * D).astype(q.dtype)

    out = lax.map(block, jnp.arange(S // Q_BLOCK))
    return out.transpose(1, 0, 2, 3).reshape(B, S, H * D)

def mlstm_chunkwise(q, k, v, i_pre, f_pre):
    B, S, H, D = q.shape
    L = M_CHUNK
    nc = S // L
    f32 = jnp.float32

    def chunks(a):
        return a.astype(f32).reshape(B, nc, L, H, -1).transpose(1, 0, 3, 2, 4)

    qc = chunks(q)
    kc = chunks(k) * (D ** -0.5)
    vc = chunks(v)
    ic = chunks(i_pre[..., None])[..., 0]
    lf = jax.nn.log_sigmoid(chunks(f_pre[..., None])[..., 0])
    causal = jnp.tril(jnp.ones((L, L), dtype=bool))

    def step(carry, inp):
        C, n, m = carry
        qt, kt, vt, it, ft = inp
        b = jnp.cumsum(ft, axis=-1)
        dmat = jnp.where(causal, b[..., :, None] - b[..., None, :] + it[..., None, :], -jnp.inf)
        inter = b + m[..., None]
        mt = jnp.maximum(inter, jnp.max(dmat, axis=-1))
        w_intra = jnp.exp(dmat - mt[..., None])
        w_inter = jnp.exp(inter - mt)
        qk = jnp.einsum('bhtd,bhsd->bhts', qt, kt) * w_intra
        num = w_inter[..., None] * jnp.einsum('bhtd,bhde->bhte', qt, C) + jnp.einsum('bhts,bhse->bhte', qk, vt)
        den = w_inter * jnp.einsum('bhtd,bhd->bht', qt, n) + jnp.sum(qk, axis=-1)
        h = num / jnp.maximum(jnp.abs(den), jnp.exp(-mt))[..., None]
        bL = b[..., -1]
        a_s = bL[..., None] - b + it
        m_new = jnp.maximum(bL + m, jnp.max(a_s, axis=-1))
        ws = jnp.exp(a_s - m_new[..., None])
        decay = jnp.exp(bL + m - m_new)
        C_new = decay[..., None, None] * C + jnp.einsum('bhsd,bhse->bhde', kt * ws[..., None], vt)
        n_new = decay[..., None] * n + jnp.einsum('bhs,bhsd->bhd', ws, kt)
        return (C_new, n_new, m_new), h

    init = (jnp.zeros((B, H, D, D), f32), jnp.zeros((B, H, D), f32), jnp.full((B, H), -1e30, f32))
    _, h = lax.scan(step, init, (qc, kc, vc, ic, lf))
    return h.transpose(1, 0, 3, 2, 4).reshape(B, S, H, D).astype(q.dtype)

def token_mixer(h, cos, sin, overlap, w_in, cmp_pos, cmp_w1, cmp_w2, att_norm_g,
                m_conv_w, m_conv_b, m_gate_b, m_norm_g, w_out):
    B, S, _ = h.shape
    splits = [int(i) for i in np.cumsum(IN_SIZES)[:-1]]
    q, kc, vc, ks, vs, kw, vw, g_att, m_qk, m_v, m_if, m_o = jnp.split(h @ w_in, splits, axis=-1)
    q = apply_rope(q.reshape(B, S, ATT_HEADS, ATT_DIM), cos, sin)
    kc = apply_rope(kc.reshape(B, S, ATT_KV_HEADS, ATT_DIM), cos, sin)
    ks = apply_rope(ks.reshape(B, S, ATT_KV_HEADS, ATT_DIM), cos, sin)
    kw = apply_rope(kw.reshape(B, S, ATT_KV_HEADS, ATT_DIM), cos, sin)
    vc = vc.reshape(B, S, ATT_KV_HEADS, ATT_DIM)
    vs = vs.reshape(B, S, ATT_KV_HEADS, ATT_DIM)
    vw = vw.reshape(B, S, ATT_KV_HEADS, ATT_DIM)
    k_cmp = compress(kc, cmp_pos[0], cmp_w1[0], cmp_w2[0])
    v_cmp = compress(vc, cmp_pos[1], cmp_w1[1], cmp_w2[1])
    gates = jax.nn.sigmoid(g_att).reshape(B, S, ATT_HEADS, 3)
    att = nsa_attention(q, k_cmp, v_cmp, ks, vs, kw, vw, gates, overlap)
    att = head_rms_norm(att, att_norm_g, ATT_HEADS)
    mq, mk = jnp.split(jax.nn.silu(causal_dwconv(m_qk, m_conv_w, m_conv_b)), 2, axis=-1)
    m_if = m_if + m_gate_b
    hm = mlstm_chunkwise(mq.reshape(B, S, M_HEADS, M_DIM), mk.reshape(B, S, M_HEADS, M_DIM),
                         m_v.reshape(B, S, M_HEADS, M_DIM), m_if[..., :M_HEADS], m_if[..., M_HEADS:])
    hm = jax.nn.sigmoid(m_o) * hm.reshape(B, S, M_WIDTH)
    hm = head_rms_norm(hm, m_norm_g, M_HEADS)
    return jnp.concatenate([att, hm], axis=-1) @ w_out

def conv_ffn(h, w_up, conv_w, conv_b, w_down):
    a = causal_dwconv(h @ w_up[:, :D_FF], conv_w, conv_b)
    v = h @ w_up[:, D_FF:]
    return (jax.nn.silu(a) * v) @ w_down

def setup_inputs(seed: int = 0) -> dict:
    key = jax.random.key(seed)
    ks = jax.random.split(key, 24)
    n = jax.random.normal
    L_ = DEPTH
    x = n(ks[0], (BATCH, SEQ, D_MODEL), jnp.float32)
    c = n(ks[1], (BATCH, D_MODEL), jnp.float32)
    offset = jax.random.randint(ks[2], (BATCH, 1), 0, 4096, dtype=jnp.int32)
    positions = offset + jnp.arange(SEQ, dtype=jnp.int32)[None, :]
    f_bias = jnp.linspace(3.0, 6.0, M_HEADS, dtype=jnp.float32)[None, :] + 0.1 * n(ks[3], (L_, M_HEADS))
    i_bias = 0.1 * n(ks[4], (L_, M_HEADS))
    return {
        'x': x,
        'c': c,
        'positions': positions,
        'norm1_g': 1.0 + 0.05 * n(ks[5], (L_, D_MODEL)),
        'norm2_g': 1.0 + 0.05 * n(ks[6], (L_, D_MODEL)),
        'ada_w': n(ks[7], (L_, D_MODEL, 6 * D_MODEL)) * (0.5 * D_MODEL ** -0.5),
        'ada_b': 0.02 * n(ks[8], (L_, 6 * D_MODEL)),
        'w_in': n(ks[9], (L_, D_MODEL, IN_COLS)) * D_MODEL ** -0.5,
        'cmp_pos': 0.1 * n(ks[10], (L_, 2, CMP_BLOCK, ATT_DIM)),
        'cmp_w1': n(ks[11], (L_, 2, CMP_BLOCK * ATT_DIM, ATT_DIM)) * (CMP_BLOCK * ATT_DIM) ** -0.5,
        'cmp_w2': n(ks[12], (L_, 2, ATT_DIM, ATT_DIM)) * ATT_DIM ** -0.5,
        'att_norm_g': 1.0 + 0.05 * n(ks[13], (L_, ATT_WIDTH)),
        'm_conv_w': n(ks[14], (L_, M_CONV, 2 * M_WIDTH)) * M_CONV ** -0.5,
        'm_conv_b': 0.02 * n(ks[15], (L_, 2 * M_WIDTH)),
        'm_gate_b': jnp.concatenate([i_bias, f_bias], axis=-1),
        'm_norm_g': 1.0 + 0.05 * n(ks[16], (L_, M_WIDTH)),
        'w_out': n(ks[17], (L_, D_MODEL, D_MODEL)) * D_MODEL ** -0.5,
        'ffn_up': n(ks[18], (L_, D_MODEL, 2 * D_FF)) * D_MODEL ** -0.5,
        'ffn_conv_w': n(ks[19], (L_, FFN_CONV, D_FF)) * FFN_CONV ** -0.5,
        'ffn_conv_b': 0.02 * n(ks[20], (L_, D_FF)),
        'ffn_down': n(ks[21], (L_, D_FF, D_MODEL)) * D_FF ** -0.5,
        'final_g': 1.0 + 0.05 * n(ks[22], (D_MODEL,)),
    }

def reference(x, c, positions, norm1_g, norm2_g, ada_w, ada_b, w_in, cmp_pos, cmp_w1, cmp_w2,
              att_norm_g, m_conv_w, m_conv_b, m_gate_b, m_norm_g, w_out, ffn_up, ffn_conv_w,
              ffn_conv_b, ffn_down, final_g):
    cos, sin = rope_tables(positions)
    overlap = selection_overlap(x.shape[1])
    c_act = jax.nn.silu(c)
    for l in range(DEPTH):
        mod = c_act @ ada_w[l] + ada_b[l]
        sh1, sc1, g1, sh2, sc2, g2 = [m[:, None, :] for m in jnp.split(mod, 6, axis=-1)]
        h = rms_norm(x, norm1_g[l]) * (1.0 + sc1) + sh1
        x = x + g1 * token_mixer(h, cos, sin, overlap, w_in[l], cmp_pos[l], cmp_w1[l], cmp_w2[l],
                                 att_norm_g[l], m_conv_w[l], m_conv_b[l], m_gate_b[l], m_norm_g[l], w_out[l])
        h = rms_norm(x, norm2_g[l]) * (1.0 + sc2) + sh2
        x = x + g2 * conv_ffn(h, ffn_up[l], ffn_conv_w[l], ffn_conv_b[l], ffn_down[l])
    return rms_norm(x, final_g)


_drawn_inputs = setup_inputs


def setup_inputs(seed=0):
    import zlib

    import numpy as np

    out = dict(_drawn_inputs(seed))
    spreads = {}
    factors = {'norm2_g': 2.8, 'att_norm_g': 3.295, 'm_conv_b': 8.0, 'm_norm_g': 3.756, 'ffn_conv_b': 8.0}
    for name, (base, spread) in spreads.items():
        noise = np.random.default_rng([zlib.crc32(name.encode()), seed]).standard_normal(out[name].shape)
        drawn = base * np.exp(spread * noise) if base else spread * noise
        out[name] = __import__('jax').numpy.asarray(drawn.astype(out[name].dtype))
    for name, factor in factors.items():
        out[name] = (out[name] * factor).astype(out[name].dtype)
    return out
```

```python
from contextlib import ExitStack

import numpy as np
import concourse.bass as bass
from concourse import mybir

dt = mybir.dt
F32, F32R, BF16 = dt.float32, dt.float32r, dt.bfloat16
ALU = mybir.AluOpType
ACT = mybir.ActivationFunctionType
AX = mybir.AxisListType

P = 128
D = 1024
T = 512
L = 2
KD = D // P
TT = T // P
F = 2816
KF = F // P
NH, DH, NG = 8, 64, 2
R = NH // NG
MH, MD = 4, 128
MC, FC = 4, 3
HALF = 8
CB, CS = 32, 16
NC = (T - CB) // CS + 1
NCP = NC + 1
IN_COLS = 3360
EPS = 1e-6
NEG = -1e30
TINY = 1e-30
MSCALE = float(np.float32(MD ** -0.5))

C_Q, C_KC, C_VC, C_KS, C_VS, C_KW, C_VW, C_G = 0, 512, 640, 768, 896, 1024, 1152, 1280
C_MQK, C_MV, C_IF, C_MO = 1304, 2328, 2840, 2848
NGATE = 24

N1, N2, AB, MW, MB = 0, 8, 16, 64, 96
FW, FB, MG, CP = 104, 170, 192, 200
NPAR = 232
CROW, FROW = L * NPAR, L * NPAR + KD
NROW = FROW + KD

U_QKV, U_MQK, U_MV, U_MO, U_OUT, U_UP, U_DOWN, UNITS = 0, 6, 10, 12, 14, 18, 40, 52
SLOT = 2048
RAW, HI = 3, 2
AUNITS = 24
DOWN_K = [(0, 8), (8, 15), (15, 22)]
BODY = 6
LOOPED = KF // BODY * BODY
CREDIT = 2

PJ_MQK, PJ_MV, PJ_MO, PJ = 12, 20, 24, 28
PB = 5
TOKC = 1280
W_OFF = [0, 512, 896, 1152]
W_ALL = 1280


def slot_need(u):
    return u - 2 if u >= RAW else (0, -2, -1)[u]


def build(nc, x, c, positions, norm1_g, norm2_g, ada_w, ada_b, w_in, cmp_pos, cmp_w1, cmp_w2,
          att_norm_g, m_conv_w, m_conv_b, m_gate_b, m_norm_g, w_out, ffn_up, ffn_conv_w,
          ffn_conv_b, ffn_down, final_g, out):
    ctx = ExitStack()
    with ctx:
        cursor = [16512]

        def place(name, shape, dtype=F32, at=None):
            size = int(np.prod(shape[1:])) * (2 if dtype == BF16 else 4)
            if at is None:
                at = cursor[0]
                cursor[0] += (size + 31) // 32 * 32
            return nc.alloc_sbuf_tensor_at(name, shape, dtype, offset=at)

        xT = place("xT", [P, KD, T])
        h_hi = place("h_hi", [P, KD, T], F32R)
        h_lo = place("h_lo", [P, KD, T], F32R)
        raw_at = cursor[0]
        w_raw = place("w_raw", [P, RAW, SLOT])
        w_lo = place("w_lo", [P, RAW, SLOT], F32R, at=raw_at)
        w_hi = place("w_hi", [P, HI, SLOT], F32R)
        rstd = place("rstd", [P, T])
        sqacc = place("sqacc", [P, T])
        hm_at = cursor[0]
        hm = place("hm", [P, 2, T])
        ident = place("ident", [P, P])
        identb = place("identb", [P, P], BF16)
        tri = place("tri", [P, P], BF16)
        triT = place("triT", [P, P], BF16)
        ones = place("ones", [P, P])
        eps = place("eps", [P, 1])
        par_all = place("par_all", [P, NROW])
        par = place("par", [P, NPAR])
        cact = place("cact", [P, KD])
        mod = place("mod", [P, 48])
        am = place("am", [P, 2, KD])
        cos = place("cos", [P, TT, HALF])
        sin = place("sin", [P, TT, HALF])
        cmask = place("cmask", [P, TT, NCP])
        gate_b = place("gate_b", [MH, L, 2])
        ada_at = cursor[0]
        a_raw = place("a_raw", [P, 2, SLOT])
        union = cursor[0]
        hid_hi = place("hid_hi", [P, KF, T], F32R)
        hid_lo = place("hid_lo", [P, KF, T], F32R)
        end = cursor[0]

        class Region:
            def __init__(self, at, stop):
                self.at, self.stop = at, stop

            def place(self, name, shape, dtype=F32):
                size = (int(np.prod(shape[1:])) * 4 + 31) // 32 * 32
                t = place(name, shape, dtype, at=self.at)
                self.at += size
                assert self.at <= self.stop, (name, self.at - self.stop)
                return t

        mix = Region(union, end)
        tok_at = mix.at
        tok = mix.place("tok", [P, TT, TOKC])
        mixt = place("mixt", [P, TT, D], at=tok_at)
        v_sw = mix.place("v_sw", [P, TT, 2, NG, DH + 1])
        v_m = mix.place("v_m", [P, TT, MH, MD + 1])
        so = mix.place("so", [P, TT, T])
        mqk = mix.place("mqk", [P, 2 * MH, T])
        qT = mix.place("qT", [P, R, T])
        kT = mix.place("kT", [P, 2, T])
        arow = mix.place("arow", [MH, T])
        late = mix.at
        xab = mix.place("xab", [P, 4, 2, CS // 2 * NCP])
        w1 = mix.place("w1", [P, 2, CB // 2, DH])
        probs = place("probs", [P, 2, 2, T], at=late)
        probsT = place("probsT", [P, 2, 2, TT, P], at=late + 2 * 2 * T * 4)
        mw = place("mw", [P, 2, T], at=late)
        mws = place("mws", [P, 2, W_ALL], at=late + 2 * T * 4)
        gif = mix.place("gif", [P, TT, NGATE + 2 * MH])
        xtok = place("xtok", [P, TT, D], at=tok_at)
        prow = place("prow", [P, 4, P], at=late)
        pos_i = place("pos_i", [P, TT], dt.int32, at=late + 4096)
        ang = place("ang", [P, TT, HALF], at=late + 4096 + 64)
        angn = place("angn", [P, TT, HALF], at=late + 4096 + 64 + 128)
        posf = place("posf", [P, TT], at=late + 4096 + 64 + 256)
        invf = place("invf", [P, HALF], at=late + 4096 + 64 + 288)
        otok = place("otok", [P, TT, D], at=tok_at)

        att = Region(ada_at, union)
        o_sw = att.place("o_sw", [P, 2, NH, 2, DH + 1])
        t1 = att.place("t1", [P, NH, DH])
        gat = att.place("gat", [P, TT, NGATE])
        csc = place("csc", [P, TT, NH, NCP], at=hm_at)
        hidk = att.place("hidk", [DH, NG, NCP])
        hidv = att.place("hidv", [DH, NG, 4, NCP])
        kcmp = att.place("kcmp", [P, NG, NCP])
        vcmp = att.place("vcmp", [P, NG, R, DH])
        w2 = att.place("w2", [DH, 2, DH])
        cmx = att.place("cmx", [P, TT, NH])
        csum = att.place("csum", [P, TT, NH])
        nmx = att.place("nmx", [P, 2, 2])
        coef = att.place("coef", [P, NH, 2])
        acol = att.place("acol", [P, 2, TT, MH])
        den = att.place("den", [P, 2, 2])
        ssq = att.place("ssq", [P, TT, NH + MH])
        ssq2 = att.place("ssq2", [P, TT, NH + MH])
        ib, fb, fe, brow = (place(n, [MH, T], at=ada_at + i * 4 * T)
                            for i, n in enumerate(("ib", "fb", "fe", "brow")))
        mrow = fe
        pT = place("pT", [P, TT, 2, P], at=late + 2 * 2 * T * 4)
        sqj = place("sqj", [P, MD], at=late + 2 * T * 4 + 2 * W_ALL * 4)

        ffn = Region(ada_at, union)
        fy = ffn.place("fy", [P, 2, T])
        ft = ffn.place("ft", [P, 2, T])

        psum = ctx.enter_context(nc.psum_tensor("psum", [P, 8, T], F32))
        bank = [psum[:, i, :] for i in range(8)]

        def sem(name):
            return ctx.enter_context(nc.semaphore(name))

        s_w = [sem(f"s_w{i}") for i in range(RAW)]
        s_a = [sem(f"s_a{i}") for i in range(2)]
        s_cw = sem("s_cw")
        s_x, s_par, s_pos, s_out = sem("s_x"), sem("s_par"), sem("s_pos"), sem("s_out")
        s_const, s_ang, s_sin = sem("s_const"), sem("s_ang"), sem("s_sin")
        s_prT, s_pall, s_cact, s_xT = sem("s_prT"), sem("s_pall"), sem("s_cact"), sem("s_xT")
        s_hi, s_lo, s_used = sem("s_hi"), sem("s_lo"), sem("s_used")
        s_aused, s_mod = sem("s_aused"), sem("s_mod")
        s_sqa, s_sql, s_ss, s_rt = sem("s_sqa"), sem("s_sql"), sem("s_ss"), sem("s_rt")
        s_hm, s_hhi, s_hlo = sem("s_hm"), sem("s_hhi"), sem("s_hlo")
        s_proj = sem("s_proj")
        s_pev, s_mvev, s_moev = sem("s_pev"), sem("s_mvev"), sem("s_moev")
        s_vone = sem("s_vone")
        s_cv1, s_cv2, s_cv3 = sem("s_cv1"), sem("s_cv2"), sem("s_cv3")
        s_rope = sem("s_rope")
        s_ift, s_ib, s_ln, s_rows, s_col, s_acol = (sem(n) for n in
                                                    ("s_ift", "s_ib", "s_ln", "s_rows", "s_col", "s_acol"))
        s_tp, s_tq, s_tk = sem("s_tp"), sem("s_tq"), sem("s_tk")
        s_hid, s_hids, s_cmp, s_cmpev = sem("s_hid"), sem("s_hids"), sem("s_cmp"), sem("s_cmpev")
        s_cS, s_csub, s_cexp, s_cT, s_cTev, s_cO, s_cev = (sem(n) for n in (
            "s_cS", "s_csub", "s_cexp", "s_cT", "s_cTev", "s_cO", "s_cev"))
        s_gat = sem("s_gat")
        s_S, s_nm, s_exp, s_T, s_ta, s_td, s_PV = (sem(n) for n in (
            "s_S", "s_nm", "s_exp", "s_T", "s_ta", "s_td", "s_PV"))
        s_oev, s_coef, s_comb, s_asq = sem("s_oev"), sem("s_coef"), sem("s_comb"), sem("s_asq")
        s_mS, s_mW, s_mWS = sem("s_mS"), sem("s_mW"), sem("s_mWS")
        s_mO, s_mev = sem("s_mO"), sem("s_mev")
        s_rt2, s_rh, s_mixa, s_mixm = sem("s_rt2"), sem("s_rh"), sem("s_mixa"), sem("s_mixm")
        s_mT, s_mhi, s_mlo = sem("s_mT"), sem("s_mhi"), sem("s_mlo")
        s_xu = sem("s_xu")
        s_y1, s_y2, s_z, s_fv, s_fhi, s_flo = (sem(n) for n in (
            "s_y1", "s_y2", "s_z", "s_fv", "s_fhi", "s_flo"))
        s_fin, s_yT, s_yev = sem("s_fin"), sem("s_yT"), sem("s_yev")

        block = ctx.enter_context(nc.Block())

        def pair(i):
            return bank[2 * i], bank[2 * i + 1]

        def unit_used(eng, l, u):
            eng.wait_ge(s_used, l * UNITS + (u + 1 + CREDIT))

        def projected(eng, l, i):
            if PJ_MQK <= i < PJ_MV:
                return unit_used(eng, l, U_MQK + (i - PJ_MQK) // 2)
            group = i // TT if i < PJ_MQK else (i - PJ_MV) // TT + 3
            unit = 2 * group + 1 if i < PJ_MQK else U_MV + 2 * (group - 3) + 1
            if i % TT < TT - 1:
                eng.wait_ge(s_proj, l * 5 * (TT - 1) + group * (TT - 1) + i % TT + 1)
            else:
                unit_used(eng, l, unit)

        loads, row = [], 0
        for src in [rows for l in range(L) for rows in (
                norm1_g[l].rearrange("(r q) -> r q", q=P), norm2_g[l].rearrange("(r q) -> r q", q=P),
                ada_b[l].rearrange("(r q) -> r q", q=P),
                m_conv_w[l].rearrange("w (r q) -> (w r) q", q=P), m_conv_b[l].rearrange("(r q) -> r q", q=P),
                ffn_conv_w[l].rearrange("w (r q) -> (w r) q", q=P),
                ffn_conv_b[l].rearrange("(r q) -> r q", q=P),
                att_norm_g[l].rearrange("(r q) -> r q", q=P), m_norm_g[l].rearrange("(r q) -> r q", q=P),
                cmp_pos[l].rearrange("i (c s) d -> (i c) (s d)", s=2))] + [
                c.rearrange("o (r q) -> (o r) q", q=P), final_g.rearrange("(r q) -> r q", q=P)]:
            done = 0
            while done < src.shape[0]:
                take = min(src.shape[0] - done, P - row % P)
                loads.append((row, take, src[done:done + take, :]))
                done, row = done + take, row + take
        assert row == NROW

        @block.sync
        def _(sp):
            for t in range(TT):
                sp.dma_start(xtok[:, t, :], x[0, t * P:(t + 1) * P, :]).then_inc(s_x, 16)
            sp.dma_start(gate_b[:], m_gate_b.rearrange("l (t h) -> h l t", t=2),
                         allow_slow_non_contiguous=True).then_inc(s_pos, 16)

            def load(l, u, parts):
                sp.wait_ge(s_used, l * UNITS + slot_need(u) + CREDIT)
                for dst, src in parts:
                    sp.dma_start(dst, src).then_inc(s_w[u % RAW], 16)

            def slot(u, k, n):
                return w_raw[:, u % RAW, 0:k * n].rearrange("p (k n) -> p k n", k=k)

            def load_rows(l, u, w, col, n):
                half = (u % 2) * 4
                src = w.rearrange("l (k p) n -> l p k n", p=P)
                for i in range(2):
                    yield (slot(u, 4, n)[:, 2 * i:2 * i + 2, :],
                           src[l, :, half + 2 * i:half + 2 * i + 2, col:col + n])

            def load_cols(l, u, w, col, k0, k1):
                src = w.rearrange("l (k p) n -> l p k n", p=P)
                mid = (k1 - k0) // 2
                for a, b in ((0, mid), (mid, k1 - k0)):
                    yield slot(u, k1 - k0, 256)[:, a:b, :], src[l, :, k0 + a:k0 + b, col:col + 256]

            def load_ada(l, j):
                if j != 20:
                    sp.wait_ge(s_aused, l * AUNITS + j - 1 + CREDIT)
                else:
                    sp.wait_ge(s_mT, l * KD + KD)
                sp.dma_start(a_raw[:, j % 2, :].rearrange("p (k n) -> p k n", k=KD),
                             ada_w.rearrange("l (k p) n -> l p k n", p=P)[l, :, :, j * 256:(j + 1) * 256])\
                    .then_inc(s_a[j % 2], 16)

            def load_w_in(l, u):
                if u < 4:
                    load(l, u, load_rows(l, u, w_in, (u // 2) * 512, 512))
                elif u < 6:
                    half = (u % 2) * 4
                    src = w_in.rearrange("l (k p) n -> l p k n", p=P)
                    dst = slot(u, 4, 288)
                    load(l, u, [(dst[:, :, 0:280], src[l, :, half:half + 4, 1024:1304]),
                                (dst[:, :, 280:288], src[l, :, half:half + 4, C_IF:C_IF + 8])])
                elif u < U_MV:
                    load(l, u, load_cols(l, u, w_in, C_MQK + (u - U_MQK) * 256, 0, KD))
                elif u < U_MO:
                    load(l, u, load_rows(l, u, w_in, C_MV, 512))
                else:
                    load(l, u, load_rows(l, u, w_in, C_MO, 512))

            def load_up(l, u, j):
                src = ffn_up.rearrange("l (k p) n -> l p k n", p=P)
                dst = w_raw[:, u % RAW, :].rearrange("p (k n) -> p k n", k=KD)
                load(l, u, [(dst[:, :, 0:P], src[l, :, :, bass.ds(j * P, P)]),
                            (dst[:, :, P:2 * P], src[l, :, :, bass.ds(j * P + F, P)])])

            with sp.Fori(0, L) as l:
                load_ada(l, 0)
                load_ada(l, 1)
                for u in range(RAW):
                    load_w_in(l, u)
                for j in range(2, 10):
                    load_ada(l, j)
                sp.wait_ge(s_used, l * UNITS + CREDIT)
                for i in range(2):
                    sp.dma_start(w1[:, i, :, :], cmp_w1.rearrange("l i (c p) j -> l p i c j", p=P)[l, :, i])\
                        .then_inc(s_cw, 16)
                for u in range(RAW, U_OUT):
                    load_w_in(l, u)
                    if u + 7 < 20:
                        load_ada(l, u + 7)
                sp.wait_ge(s_aused, l * AUNITS + 20 + CREDIT)
                sp.dma_start(w2[:], cmp_w2.rearrange("l i j d -> l j i d")[l]).then_inc(s_cw, 16)
                for u in range(U_OUT, U_UP - 1):
                    load(l, u, load_cols(l, u, w_out, (u - U_OUT) * 256, 0, KD))
                load_ada(l, 20)
                load_ada(l, 21)
                load(l, U_UP - 1, load_cols(l, U_UP - 1, w_out, 3 * 256, 0, KD))
                load_ada(l, 22)
                load_ada(l, 23)
                with sp.Fori(0, LOOPED // BODY) as i:
                    for s in range(BODY):
                        u = U_UP + s
                        sp.wait_ge(s_used, l * UNITS + i * BODY + (slot_need(u) + CREDIT))
                        src = ffn_up.rearrange("l (k p) n -> l p k n", p=P)
                        dst = w_raw[:, u % RAW, :].rearrange("p (k n) -> p k n", k=KD)
                        for side in range(2):
                            sp.dma_start(dst[:, :, side * P:(side + 1) * P],
                                         src[l, :, :, bass.ds(i * (BODY * P) + (s * P + side * F), P)])\
                                .then_inc(s_w[u % RAW], 16)
                for j in range(LOOPED, KF):
                    load_up(l, U_UP + j, j)
                for d in range(UNITS - U_DOWN):
                    u = U_DOWN + d
                    load(l, u, load_cols(l, u, ffn_down, (d // 3) * 256, *DOWN_K[d % 3]))
            for c8 in range(KD):
                sp.wait_ge(s_yev, c8 + 1)
                sp.dma_start(out[0].rearrange("(t p) n -> p t n", p=P)[:, :, c8 * P:(c8 + 1) * P],
                             otok[:, :, c8 * P:(c8 + 1) * P]).then_inc(s_out, 16)
            sp.wait_ge(s_out, 16 * KD)

        @block.gpsimd
        def _(pool):
            g = nc.gpsimd
            g.memset(ident[:], 0.0)
            g.memset(identb[:], 0.0)
            g.memset(tri[:], 0.0)
            g.memset(triT[:], 0.0)
            g.memset(ones[:], 1.0)
            g.memset(cmask[:], 0.0)
            g.memset(eps[:], EPS)
            pool.drain()
            for m in (ident, identb):
                g.affine_select(out=m[:], in_=m[:], compare_op=ALU.not_equal, fill=1.0, base=0,
                                pattern=[[-1, P]], channel_multiplier=1)
            g.affine_select(out=tri[:], in_=tri[:], compare_op=ALU.is_ge, fill=NEG, base=0,
                            pattern=[[-1, P]], channel_multiplier=1)
            g.affine_select(out=triT[:], in_=triT[:], compare_op=ALU.is_ge, fill=-NEG, base=0,
                            pattern=[[1, P]], channel_multiplier=-1)
            g.affine_select(out=cmask[:], in_=cmask[:], compare_op=ALU.is_ge, fill=NEG, base=-(CB - 1),
                            pattern=[[P, TT], [-CS, NCP]], channel_multiplier=1)
            pool.drain().then_inc(s_const, 1)
            pool.drain().then_inc(s_flo, CREDIT)

            def low(l, u, i=0):
                pool.wait_ge(s_hi, l * UNITS + i * BODY + (u + 1))
                g.tensor_tensor(w_lo[:, u % RAW, :], w_raw[:, u % RAW, :],
                                w_hi[:, u % HI, :].bitcast(F32), ALU.subtract).then_inc(s_lo, 1)

            def low_part(l, u, n):
                pool.wait_ge(s_hi, l * UNITS + u + 1)
                g.tensor_tensor(w_lo[:, u % RAW, 0:n], w_raw[:, u % RAW, 0:n],
                                w_hi[:, u % HI, 0:n].bitcast(F32), ALU.subtract).then_inc(s_lo, 1)

            def square(first, norm, c8):
                pool.wait_ge(s_xu, first + c8 + 1)
                if c8 == 0:
                    pool.wait_ge(s_ss, norm)
                    g.tensor_tensor(sqacc[:], xT[:, 0, :], xT[:, 0, :], ALU.mult)
                else:
                    g.tensor_tensor(hm[:, 0, :], xT[:, c8, :], xT[:, c8, :], ALU.mult)
                    pool.drain()
                    g.tensor_tensor(sqacc[:], sqacc[:], hm[:, 0, :], ALU.add)
                if c8 == KD - 2:
                    pool.drain().then_inc(s_sqa, 1)
                else:
                    pool.drain()

            for c8 in range(KD - 1):
                square(0, 0, c8)
            with pool.Fori(0, L) as l:
                low(l, 0)
                pool.wait_ge(s_ss, 2 * l + 1)
                low(l, 1)
                g.memset(v_sw[:, :, :, :, DH:DH + 1], 1.0)
                g.memset(v_m[:, :, :, MD:MD + 1], 1.0)
                pool.drain().then_inc(s_vone, 1)
                for u in range(2, 16):
                    if u in (4, 5):
                        low_part(l, u, 4 * 288)
                    else:
                        low(l, u)
                for t in range(TT):
                    pool.wait_ge(s_coef, l * TT + t + 1)
                    for br in range(2):
                        g.tensor_tensor(t1[:], o_sw[:, t % 2, :, br, 0:DH],
                                        coef[:, :, br:br + 1].broadcast_to([P, NH, DH]), ALU.mult)
                        pool.drain()
                        o3 = mixt[:, t, 0:T].rearrange("p (h d) -> p h d", h=NH)
                        g.tensor_tensor(o3, o3, t1[:], ALU.add)
                        pool.drain()
                    g.tensor_tensor(t1[:], o3, o3, ALU.mult)
                    pool.drain().then_inc(s_comb, 1)
                    pool.wait_ge(s_asq, l * TT + t + 1)
                pool.wait_ge(s_rh, l + 1)
                for t in range(TT):
                    o3 = mixt[:, t, T:D].rearrange("p (h d) -> p h d", h=MH)
                    g.tensor_tensor(o3, o3, ssq2[:, t, NH:NH + MH].unsqueeze(2).broadcast_to([P, MH, MD]),
                                    ALU.mult)
                pool.drain().then_inc(s_mixm, 1)
                for q in range(4):
                    if q < 3:
                        low(l, 16 + q)
                    for c8 in (2 * q, 2 * q + 1):
                        if c8 < KD - 1:
                            square(KD + 2 * KD * l, 2 * l + 1, c8)
                low(l, 19)

                def hidden_low(l, f, i, idx):
                    pool.wait_ge(s_fhi, l * KF + i * BODY + (f + 1))
                    g.tensor_tensor(hid_lo[:, bass.ds(idx, 1), :], ft[:, f % 2:f % 2 + 1, :],
                                    hid_hi[:, bass.ds(idx, 1), :].bitcast(F32), ALU.subtract)\
                        .then_inc(s_flo, 1)

                with pool.Fori(0, LOOPED // BODY) as i:
                    for s in range(BODY):
                        low(l, U_UP + 2 + s, i)
                        hidden_low(l, s, i, i * BODY + s)
                for f in range(LOOPED, KF):
                    if f + 2 + U_UP < U_DOWN:
                        low(l, U_UP + 2 + f)
                    else:
                        d = f + 2 + U_UP - U_DOWN
                        k0, k1 = DOWN_K[d % 3]
                        low_part(l, U_DOWN + d, (k1 - k0) * 256)
                    hidden_low(l, f, 0, f)
                for q in range(4):
                    for d in range(3 * q + 2, min(3 * q + 5, UNITS - U_DOWN)):
                        k0, k1 = DOWN_K[d % 3]
                        low_part(l, U_DOWN + d, (k1 - k0) * 256)
                    for c8 in (2 * q, 2 * q + 1):
                        if c8 < KD - 1:
                            square(2 * KD + 2 * KD * l, 2 * l + 2, c8)

        @block.scalar
        def _(act):
            s = nc.scalar

            for row, n, src in loads:
                act.dma_start(prow[row % P:row % P + n, row // P, :], src).then_inc(s_par, 16)
            act.dma_start(pos_i[:], positions[0].rearrange("(t p) -> p t", p=P),
                          allow_slow_non_contiguous=True).then_inc(s_pos, 16)

            act.wait_ge(s_ang, 1)
            s.activation(sin[:], ang[:], ACT.Sin).then_inc(s_sin, 1)
            act.wait_ge(s_ang, 2)
            s.activation(cos[:], angn[:], ACT.Sin).then_inc(s_sin, 1)
            act.wait_ge(s_pall, 1)
            s.activation(cact[:], par_all[:, CROW:CROW + KD], ACT.Silu).then_inc(s_cact, 1)

            def last_square(first, norm):
                act.wait_ge(s_xu, first + KD)
                act.wait_ge(s_ss, norm)
                s.activation(hm[:, 1, :], xT[:, KD - 1, :], ACT.Square).then_inc(s_sql, 1)

            def high(l, u, i=0, n=SLOT):
                r = u % RAW
                before = u // RAW
                per = (UNITS + RAW - 1 - r) // RAW
                act.wait_ge(s_w[r], l * (32 * per) + i * (32 * BODY // RAW) + 32 * (before + 1))
                act.wait_ge(s_used, l * UNITS + i * BODY + (u - 1 + CREDIT))
                s.activation(w_hi[:, u % HI, 0:n], w_raw[:, r, 0:n], ACT.Copy).then_inc(s_hi, 1)

            def width(u):
                if u in (4, 5):
                    return 4 * 288
                if u >= U_DOWN:
                    k0, k1 = DOWN_K[(u - U_DOWN) % 3]
                    return (k1 - k0) * 256
                return SLOT

            def norm_root(norm):
                act.wait_ge(s_ss, norm + 1)
                s.activation(rstd[:], bank[7], ACT.Sqrt, bias=eps[:, 0:1], scale=1.0 / D).then_inc(s_rt, 1)

            def norm_high(chunks, shift):
                for c8 in range(KD):
                    act.wait_ge(s_hm, chunks + c8 + 1)
                    s.activation(h_hi[:, c8, :], hm[:, c8 % 2, :], ACT.Identity,
                                 bias=mod[:, shift + c8:shift + c8 + 1]).then_inc(s_hhi, 1)

            last_square(0, 0)
            with act.Fori(0, L) as l:
                high(l, 0)
                high(l, 1)
                norm_root(2 * l)
                norm_high(2 * KD * l, 0)
                for u in range(U_OUT):
                    high(l, u + 2, n=width(u + 2))
                    if U_MQK < u <= U_MV:
                        for c8 in (2 * (u - U_MQK) - 2, 2 * (u - U_MQK) - 1):
                            act.wait_ge(s_cv2, l * 2 * MH + c8 + 1)
                            s.activation(mqk[:, c8, :], mqk[:, c8, :], ACT.Silu).then_inc(s_cv3, 1)
                    if U_MQK <= u < U_MV:
                        for c8 in (2 * (u - U_MQK), 2 * (u - U_MQK) + 1):
                            projected(act, l, PJ_MQK + c8)
                            s.activation(mqk[:, c8, :], bank[(PJ_MQK + c8) % PB], ACT.Identity,
                                         bias=par[:, MB + c8:MB + c8 + 1],
                                         scale=par[:, MW + 3 * KD + c8:MW + 3 * KD + c8 + 1]).then_inc(s_cv1, 1)
                for t in range(TT):
                    projected(act, l, PJ_MO + t)
                    s.activation(so[:, t, :], bank[(PJ_MO + t) % PB], ACT.Sigmoid).then_inc(s_moev, 1)
                act.wait_ge(s_aused, l * AUNITS + 20 + CREDIT)
                s.activation(gat[:], gif[:, :, 0:NGATE], ACT.Sigmoid).then_inc(s_gat, 1)
                for r in range(R):
                    act.wait_ge(s_tp, l * 10 + r + 1)
                    s.activation(qT[:, r, :], bank[(PJ + r) % PB], ACT.Copy, scale=DH ** -0.5).then_inc(s_tq, 1)
                act.wait_ge(s_hid, l + 1)
                hid_ps = bank[6][0:DH, 0:4 * NCP].rearrange("p (i g n) -> p i g n", i=2, g=NG)
                s.activation(hidk[:, :, 0:NC], hid_ps[:, 0, :, 0:NC], ACT.Silu)
                for gr in range(NG):
                    last = s.activation(hidv[:, gr, :, 0:NC],
                                        hid_ps[:, 1, gr:gr + 1, 0:NC].broadcast_to([DH, 4, NC]), ACT.Silu)
                last.then_inc(s_hids, 1)
                act.wait_ge(s_ib, l + 1)
                s.activation(fe[:], fe[:], ACT.Exp, scale=-1.0)
                act.drain()
                s.activation(fe[:], fe[:], ACT.Ln, bias=ones[0:MH, 0:1]).then_inc(s_ln, 1)
                for t in range(TT):
                    act.wait_ge(s_csub, l * TT + t + 1)
                    s.activation(csc[:, t], csc[:, t], ACT.Exp).then_inc(s_cexp, 1)
                act.wait_ge(s_col, l + 1)
                cols = bank[5][:, 0:2 * TT * MH].rearrange("p (i t h) -> p i t h", i=2, t=TT)
                s.activation(acol[:, 0], cols[:, 0], ACT.Copy)
                s.activation(acol[:, 1], cols[:, 1], ACT.Exp, scale=-1.0).then_inc(s_acol, 1)
                for w in range(TT * NH + 1):
                    if w < TT * NH:
                        t, n = w // NH, (w // NH + 1) * P
                        act.wait_ge(s_nm, l * 32 + w + 1)
                        if w >= 2:
                            act.wait_ge(s_T, l * 32 + w - 1)
                        for br in range(2):
                            last = s.activation(probs[:, w % 2, br, 0:n], pair(w % 2)[br][:, 0:n], ACT.Exp,
                                                bias=nmx[:, w % 2, br:br + 1])
                        last.then_inc(s_exp, 1)
                    if w >= 1:
                        v = w - 1
                        n = (v // NH + 1) * P
                        act.wait_ge(s_T, l * 32 + v + 1)
                        if v >= 2:
                            act.wait_ge(s_PV, l * 32 + v - 1)
                        s.activation(probsT[:, v % 2, 0].rearrange("p k q -> p (k q)")[:, 0:n],
                                     bank[4][:, 0:n], ACT.Copy).then_inc(s_ta, 1)
                for h in range(MH + 1):
                    if h < MH:
                        for j in range(TT):
                            z = h * TT + j
                            n = (TT - j) * P
                            act.wait_ge(s_mS, l * 16 + z + 1)
                            if z >= 2:
                                act.wait_ge(s_mWS, l * 16 + z - 1)
                            s.activation(mw[:, z % 2, 0:n], pair(z % 2)[1][:, 0:n], ACT.Exp,
                                         bias=acol[:, 0, j, h:h + 1], scale=-1.0).then_inc(s_mW, 1)
                    if h >= 1:
                        for e in range(2):
                            act.wait_ge(s_mev, l * 8 + 2 * (h - 1) + e + 1)
                            for t in (2 * e, 2 * e + 1):
                                last = s.activation(sqj[:], mixt[:, t, T + (h - 1) * MD:T + h * MD], ACT.Square,
                                                    accum_out=ssq[:, t, NH + h - 1:NH + h])
                                act.drain()
                act.wait_ge(s_asq, l * TT + TT)
                s.activation(ssq2[:, :, 0:NH], ssq[:, :, 0:NH], ACT.Sqrt, bias=eps[:, 0:1], scale=1.0 / DH)
                s.activation(ssq2[:, :, NH:], ssq[:, :, NH:], ACT.Sqrt, bias=eps[:, 0:1], scale=1.0 / MD)\
                    .then_inc(s_rt2, 1)
                for c8 in range(KD):
                    act.wait_ge(s_mT, l * KD + c8 + 1)
                    s.activation(h_hi[:, c8, :], bank[c8 % 4], ACT.Copy,
                                 scale=par[:, MG + c8:MG + c8 + 1]).then_inc(s_mhi, 1)
                for u in (16, 17, 18):
                    high(l, u)
                last_square(KD + 2 * KD * l, 2 * l + 1)
                norm_root(2 * l + 1)
                high(l, 19)
                norm_high(2 * KD * l + KD, 24)

                def hidden_step(l, f, i, idx):
                    unit_used(act, l, i * BODY + (U_UP + f))
                    a_ps = pair(f % 3)[0]
                    s.activation(fy[:, f % 2, :], a_ps, ACT.Identity,
                                 bias=par[:, bass.ds(idx + FB, 1)],
                                 scale=par[:, bass.ds(idx + FW + 2 * KF, 1)]).then_inc(s_y1, 1)
                    act.wait_ge(s_y2, l * KF + i * BODY + (f + 1))
                    s.activation(fy[:, f % 2, :], fy[:, f % 2, :], ACT.Silu).then_inc(s_z, 1)
                    act.wait_ge(s_fv, l * KF + i * BODY + (f + 1 + CREDIT))
                    s.activation(hid_hi[:, bass.ds(idx, 1), :], ft[:, f % 2:f % 2 + 1, :], ACT.Copy)\
                        .then_inc(s_fhi, 1)

                with act.Fori(0, LOOPED // BODY) as i:
                    for f in range(BODY):
                        high(l, U_UP + 2 + f, i)
                        hidden_step(l, f, i, i * BODY + f)
                for f in range(LOOPED, KF):
                    high(l, U_UP + 2 + f, n=width(U_UP + 2 + f))
                    hidden_step(l, f, 0, f)
                for u in range(U_DOWN + 2, UNITS):
                    high(l, u, n=width(u))
                last_square(2 * KD + 2 * KD * l, 2 * l + 2)
            norm_root(2 * L)
            for c8 in range(KD):
                act.wait_ge(s_yT, c8 + 1)
                s.activation(otok[:, :, c8 * P:(c8 + 1) * P],
                             bank[c8 % 4].rearrange("p (t n) -> p t n", t=TT), ACT.Copy).then_inc(s_yev, 1)

        @block.vector
        def _(dve):
            v = nc.vector

            PI = 3.1415925
            C1, C2 = 6.28125, 0.0019350051879882812
            C3 = float(2 * np.pi - C1 - C2)
            inv = (np.float32(500000.0) ** (-np.arange(0, 2 * HALF, 2, dtype=np.float32) / np.float32(2 * HALF)))
            for i in range(HALF):
                v.memset(invf[:, i:i + 1], float(inv[i]))
            dve.wait_ge(s_pos, 32)
            v.tensor_copy(posf[:], pos_i[:])
            dve.drain().then_inc(s_fv, CREDIT)
            v.tensor_tensor(ang[:], posf[:].unsqueeze(2).broadcast_to([P, TT, HALF]),
                            invf[:].unsqueeze(1).broadcast_to([P, TT, HALF]), ALU.mult)
            dve.drain()
            MAGIC = 12582912.0
            v.tensor_scalar(angn[:], ang[:], float(1 / (2 * np.pi)), MAGIC, ALU.mult, ALU.add)
            dve.drain()
            v.tensor_scalar(angn[:], angn[:], MAGIC, None, ALU.subtract)
            for step in (C1, C2, C3):
                dve.drain()
                v.scalar_tensor_tensor(out=ang[:], in0=angn[:], scalar=-step, in1=ang[:], op0=ALU.mult, op1=ALU.add)
            dve.drain()
            v.tensor_scalar(angn[:], ang[:], float(np.pi / 2), None, ALU.add)
            v.tensor_scalar(ang[:], ang[:], PI, -PI, ALU.min, ALU.max)
            dve.drain().then_inc(s_ang, 1)
            v.tensor_scalar(cos[:], angn[:], PI, -float(2 * np.pi), ALU.is_gt, ALU.mult)
            dve.drain()
            v.tensor_tensor(angn[:], angn[:], cos[:], ALU.add)
            dve.drain()
            v.tensor_scalar(angn[:], angn[:], PI, -PI, ALU.min, ALU.max)
            dve.drain().then_inc(s_ang, 1)

            for c8 in range(KD):
                dve.wait_ge(s_xT, c8 + 1)
                v.tensor_copy(xT[:, c8, :], bank[c8 % 7]).then_inc(s_xu, 1)
            dve.wait_ge(s_prT, 1)
            v.tensor_copy(par_all[:], bank[7][:, 0:NROW])
            dve.drain().then_inc(s_pall, 1)

            def norm(l, n, chunks, which):
                dve.wait_ge(s_rt, n + 1)
                v.reciprocal(rstd[:], rstd[:])
                dve.drain()
                shift = (0, 24)[which]
                for c8 in range(KD + 1):
                    if c8 < KD:
                        v.scalar_tensor_tensor(out=hm[:, c8 % 2, :], in0=xT[:, c8, :],
                                               scalar=am[:, which, c8:c8 + 1], in1=rstd[:],
                                               op0=ALU.mult, op1=ALU.mult).then_inc(s_hm, 1)
                    if c8 >= 1:
                        b = c8 - 1
                        dve.wait_ge(s_hhi, chunks + b + 1)
                        v.scalar_tensor_tensor(out=h_lo[:, b, :], in0=hm[:, b % 2, :],
                                               scalar=mod[:, shift + b:shift + b + 1],
                                               in1=h_hi[:, b, :].bitcast(F32),
                                               op0=ALU.add, op1=ALU.subtract).then_inc(s_hlo, 1)
                        dve.wait_ge(s_hlo, chunks + b + 1)

            def x_update(l, gate):
                for q in range(4):
                    unit_used(dve, l, U_OUT + q if gate == 16 else U_DOWN + 3 * q + 2)
                    for e in range(2):
                        c8 = 2 * q + e
                        ps = (pair((q + 2) % 3) if gate == 16 else pair((q + 1) % 3))[e]
                        v.scalar_tensor_tensor(out=xT[:, c8, :], in0=ps, scalar=mod[:, gate + c8:gate + c8 + 1],
                                               in1=xT[:, c8, :], op0=ALU.mult, op1=ALU.add).then_inc(s_xu, 1)

            with dve.Fori(0, L) as l:
                v.tensor_copy(par[:], par_all[:, bass.ds(l * NPAR, NPAR)])
                dve.drain()
                dve.wait_ge(s_aused, l * AUNITS + 8 + CREDIT)
                v.tensor_tensor(mod[:, 0:16], bank[6][:, 0:16], par[:, AB:AB + 16], ALU.add)
                dve.drain()
                v.scalar_tensor_tensor(out=am[:, 0, :], in0=mod[:, 8:16], scalar=1.0, in1=par[:, N1:N1 + KD],
                                       op0=ALU.add, op1=ALU.mult)
                dve.drain().then_inc(s_mod, 1)
                norm(l, 2 * l, 2 * KD * l, 0)

                for t in range(TT):
                    projected(dve, l, t)
                    v.tensor_copy(tok[:, t, 0:T].rearrange("p (r g d) -> p g r d", r=R, g=NG),
                                  bank[t % PB].rearrange("p (g r d) -> p g r d", r=R, g=NG)).then_inc(s_pev, 1)
                for t in range(TT):
                    i = TT + t
                    projected(dve, l, i)
                    ps = bank[i % PB]
                    for at, off in ((512, 0), (1024, 128)):
                        v.tensor_copy(tok[:, t, at:at + 256].rearrange("p (g s d) -> p g s d", g=NG, s=2),
                                      ps[:, off:off + 128].rearrange("p (g s d) -> p g s d", g=NG, s=1)
                                      .broadcast_to([P, NG, 2, DH]))
                    v.tensor_copy(tok[:, t, 768:896], ps[:, 256:384])
                    v.tensor_copy(v_sw[:, t, 0, :, 0:DH], ps[:, 384:512].rearrange("p (g d) -> p g d", g=NG))\
                        .then_inc(s_pev, 1)
                for t in range(TT):
                    i = 2 * TT + t
                    projected(dve, l, i)
                    ps = bank[i % PB]
                    v.tensor_copy(tok[:, t, 896:1024], ps[:, 0:128])
                    v.tensor_copy(v_sw[:, t, 1, :, 0:DH], ps[:, 128:256].rearrange("p (g d) -> p g d", g=NG))
                    v.tensor_copy(gif[:, t, :], ps[:, 256:288]).then_inc(s_pev, 1)
                dve.wait_ge(s_sin, 2)
                dve.drain()
                heads = tok[:, :, 0:1024].rearrange("p t (h d) -> p t h d", d=DH)
                x1, x2 = heads[:, :, :, 0:HALF], heads[:, :, :, HALF:2 * HALF]
                x1s, x2s = (hm[:, i, :].rearrange("p (t h d) -> p t h d", t=TT, d=HALF) for i in range(2))
                cosb, sinb = (m[:].unsqueeze(2).broadcast_to([P, TT, 16, HALF]) for m in (cos, sin))
                v.tensor_tensor(x1s, x1, sinb, ALU.mult)
                v.tensor_tensor(x2s, x2, sinb, ALU.mult)
                dve.drain()
                v.tensor_tensor(x1, x1, cosb, ALU.mult)
                v.tensor_tensor(x2, x2, cosb, ALU.mult)
                dve.drain()
                v.tensor_tensor(x1, x1, x2s, ALU.subtract)
                v.tensor_tensor(x2, x2, x1s, ALU.add)
                dve.drain().then_inc(s_rope, 1)
                for c0 in range(0, 2 * MH, 2):
                    for k in (2, 1, 0):
                        sh = MC - 1 - k
                        for c8 in (c0, c0 + 1):
                            if k == 2:
                                dve.wait_ge(s_cv1, l * 2 * MH + c8 + 1)
                            last = v.scalar_tensor_tensor(
                                out=mqk[:, c8, sh:T], in0=bank[(PJ_MQK + c8) % PB][:, 0:T - sh],
                                scalar=par[:, MW + k * KD + c8:MW + k * KD + c8 + 1], in1=mqk[:, c8, sh:T],
                                op0=ALU.mult, op1=ALU.add)
                            if k == 0:
                                last.then_inc(s_cv2, 1)
                        if k:
                            dve.drain()
                for t in range(TT):
                    i = PJ_MV + t
                    projected(dve, l, i)
                    v.tensor_copy(v_m[:, t, :, 0:MD], bank[i % PB].rearrange("p (h d) -> p h d", h=MH))\
                        .then_inc(s_mvev, 1)
                dve.wait_ge(s_aused, l * AUNITS + 20 + CREDIT)
                v.tensor_tensor(mod[:, 16:40], bank[6][:, 16:40], par[:, AB + 16:AB + 40], ALU.add)
                v.memset(hidk[:], 0.0)
                v.memset(hidv[:], 0.0)
                v.memset(kcmp[:], 0.0)
                v.memset(vcmp[:], 0.0)
                dve.drain()
                v.scalar_tensor_tensor(out=am[:, 1, :], in0=mod[:, 32:40], scalar=1.0, in1=par[:, N2:N2 + KD],
                                       op0=ALU.add, op1=ALU.mult)
                dve.drain().then_inc(s_mod, 1)
                dve.wait_ge(s_ift, l + 1)
                v.tensor_scalar(ib[:], bank[5][0:MH, :], gate_b[:, bass.ds(l, 1), 0:1].rearrange("h a b -> h (a b)"),
                                None, ALU.add)
                v.tensor_scalar(fb[:], bank[7][0:MH, :], gate_b[:, bass.ds(l, 1), 1:2].rearrange("h a b -> h (a b)"),
                                None, ALU.add)
                dve.drain()
                v.scalar_tensor_tensor(out=fe[:], in0=fb[:], scalar=-1.0, in1=fb[:], op0=ALU.mult, op1=ALU.max)
                dve.drain().then_inc(s_ib, 1)
                for j in range(R, R + 2):
                    dve.wait_ge(s_tp, l * 10 + j + 1)
                    v.tensor_copy(kT[:, j - R, :], bank[(PJ + j) % PB]).then_inc(s_tk, 1)
                for j in range(R + 2, 10):
                    dve.wait_ge(s_tp, l * 10 + j + 1)
                    i, n = (j - R - 2) // 2, j - R - 2
                    for half in range(2):
                        p0, p1 = half * DH, (half + 1) * DH
                        src = bank[(PJ + j) % PB][p0:p1, :].rearrange("p (n c s) -> p n c s", s=2, c=CS // 2)
                        for ab in range(2):
                            pos = par[p0:p1, CP + i * CS + ab * (CS // 2):CP + i * CS + (ab + 1) * (CS // 2)]
                            last = v.tensor_tensor(
                                xab[p0:p1, n, ab, :].rearrange("p (n c) -> p n c", c=CS // 2), src[:, :, :, half],
                                pos.unsqueeze(1).broadcast_to([DH, NCP, CS // 2]), ALU.add)
                    last.then_inc(s_tk, 1)
                dve.wait_ge(s_cmp, l + 1)
                for g in range(NG):
                    v.tensor_copy(kcmp[g * DH:(g + 1) * DH, g, :], bank[7][g * DH:(g + 1) * DH, 0:NCP])
                for r in range(R):
                    last = v.tensor_copy(vcmp[r * NCP:(r + 1) * NCP, :, r, :],
                                         bank[7][r * NCP:(r + 1) * NCP, 64:64 + NG * DH]
                                         .rearrange("p (g d) -> p g d", g=NG))
                last.then_inc(s_cmpev, 1)
                for t in range(TT):
                    dve.wait_ge(s_cS, l * TT + t + 1)
                    v.tensor_tensor(csc[:, t].rearrange("p (g r) n -> p r g n", g=NG),
                                    bank[t][:, 0:NH * NCP].rearrange("p (r g n) -> p r g n", r=R, g=NG),
                                    cmask[:, t, :].unsqueeze(1).unsqueeze(1).broadcast_to([P, R, NG, NCP]), ALU.add)
                dve.drain()
                v.tensor_reduce(out=cmx[:], in_=csc[:], axis=AX.X, op=ALU.max)
                dve.drain()
                v.tensor_scalar(cmx[:], cmx[:], NEG / 10, None, ALU.max)
                dve.drain()
                for t in range(TT):
                    v.tensor_tensor(csc[:, t], csc[:, t], cmx[:, t, :].unsqueeze(2).broadcast_to([P, NH, NCP]),
                                    ALU.subtract).then_inc(s_csub, 1)
                dve.wait_ge(s_ln, l + 1)
                one = ones[0:MH, 0:1].broadcast_to([MH, T])
                v.scalar_tensor_tensor(out=fb[:], in0=fb[:], scalar=0.0, in1=fe[:], op0=ALU.min, op1=ALU.subtract)
                dve.drain()
                v.tensor_tensor_scan(brow[:], one, fb[:], 0.0, ALU.mult, ALU.add)
                dve.drain()
                v.tensor_tensor(ib[:], ib[:], brow[:], ALU.subtract)
                dve.drain()
                v.tensor_tensor_scan(arow[:], one, ib[:], -3.0e38, ALU.mult, ALU.max)
                dve.drain()
                v.tensor_tensor(mrow[:], brow[:], arow[:], ALU.add)
                dve.drain().then_inc(s_rows, 1)
                dve.wait_ge(s_cexp, l * TT + TT)
                v.tensor_reduce(out=csum[:], in_=csc[:], axis=AX.X, op=ALU.add)
                dve.drain()
                v.tensor_scalar(csum[:], csum[:], TINY, None, ALU.max)
                dve.drain()
                v.reciprocal(csum[:], csum[:])
                dve.drain()
                dve.wait_ge(s_gat, l + 1)
                gates = gat[:].rearrange("p t (h b) -> p t h b", b=3)
                v.tensor_tensor(csum[:], csum[:], gates[:, :, :, 0], ALU.mult)
                dve.drain()
                for t in range(TT):
                    dve.wait_ge(s_cT, l * TT + t // 2 * 2 + 2)
                    v.tensor_copy(pT[:, t].rearrange("p g q -> p (g q)"),
                                  bank[4 + t // 2][:, (t % 2) * 256:(t % 2) * 256 + 256]).then_inc(s_cTev, 1)
                for t in range(TT):
                    dve.wait_ge(s_cO, l * TT + t + 1)
                    v.tensor_tensor(mixt[:, t, 0:T].rearrange("p (h d) -> p h d", h=NH),
                                    bank[t].rearrange("p (h d) -> p h d", h=NH),
                                    csum[:, t, :].unsqueeze(2).broadcast_to([P, NH, DH]), ALU.mult)\
                        .then_inc(s_cev, 1)

                def outputs(k):
                    t, h = k // 4, 2 * (k % 4)
                    dve.wait_ge(s_PV, l * 32 + 2 * k + 2)
                    if h == 0 and t >= 2:
                        dve.wait_ge(s_comb, l * TT + t - 1)
                    v.tensor_copy(o_sw[:, t % 2, h:h + 2].rearrange("p h b d -> p (h b d)"),
                                  bank[6 + k % 2][:, 0:4 * (DH + 1)]).then_inc(s_oev, 1)
                    if h == NH - 2:
                        if t >= 1:
                            squares(t - 1)
                        dve.drain()
                        v.reciprocal(coef[:], o_sw[:, t % 2, :, :, DH])
                        dve.drain()
                        v.tensor_tensor(coef[:], coef[:], gates[:, t, :, 1:3], ALU.mult)
                        dve.drain().then_inc(s_coef, 1)

                def squares(t):
                    dve.wait_ge(s_comb, l * TT + t + 1)
                    v.tensor_reduce(out=ssq[:, t, 0:NH], in_=t1[:], axis=AX.X, op=ALU.add).then_inc(s_asq, 1)

                for w in range(TT * NH + 1):
                    if w < TT * NH:
                        n = (w // NH + 1) * P
                        dve.wait_ge(s_S, l * 32 + w + 1)
                        if w >= 2:
                            dve.wait_ge(s_exp, l * 32 + w - 1)
                        v.tensor_reduce(out=nmx[:, w % 2, :], in_=psum[:, 2 * (w % 2):2 * (w % 2) + 2, 0:n],
                                        axis=AX.X, op=ALU.max, negate=True).then_inc(s_nm, 1)
                    if w >= 1:
                        b = w - 1
                        n = (b // NH + 1) * P
                        dve.wait_ge(s_T, l * 32 + b + 1)
                        if b >= 2:
                            dve.wait_ge(s_PV, l * 32 + b - 1)
                        v.tensor_copy(probsT[:, b % 2, 1].rearrange("p k q -> p (k q)")[:, 0:n],
                                      bank[5][:, 0:n]).then_inc(s_td, 1)
                    if w >= 3 and w % 2:
                        outputs((w - 3) // 2)
                outputs(TT * NH // 2 - 1)
                squares(TT - 1)

                def head_out(h):
                    for e in range(2):
                        dve.wait_ge(s_mO, l * 8 + 2 * h + e + 1)
                        ps = bank[6 + e][:, 0:2 * (MD + 1)].rearrange("p (t d) -> p t d", t=2)
                        v.scalar_tensor_tensor(out=den[:, e, :], in0=ps[:, :, MD], scalar=-1.0,
                                               in1=acol[:, 1, 2 * e:2 * e + 2, h], op0=ALU.mult, op1=ALU.max)
                        dve.drain()
                        v.tensor_tensor(den[:, e, :], ps[:, :, MD], den[:, e, :], ALU.max)
                        dve.drain()
                        v.reciprocal(den[:, e, :], den[:, e, :])
                        dve.drain()
                        for i in range(2):
                            t = 2 * e + i
                            last = v.scalar_tensor_tensor(
                                out=mixt[:, t, T + h * MD:T + (h + 1) * MD], in0=ps[:, i, 0:MD],
                                scalar=den[:, e, i:i + 1], in1=so[:, t, h * MD:(h + 1) * MD],
                                op0=ALU.mult, op1=ALU.mult)
                        last.then_inc(s_mev, 1)

                for h in range(MH):
                    for j in range(TT):
                        z, n = h * TT + j, (TT - j) * P
                        dve.wait_ge(s_mW, l * 16 + z + 1)
                        if h >= 2:
                            dve.wait_ge(s_mO, l * 8 + 2 * (h - 1))
                        v.scalar_tensor_tensor(out=mws[:, h % 2, W_OFF[j]:W_OFF[j] + n],
                                               in0=pair(z % 2)[0][:, 0:n], scalar=MSCALE, in1=mw[:, z % 2, 0:n],
                                               op0=ALU.mult, op1=ALU.mult).then_inc(s_mWS, 1)
                        if j == 1 and h >= 1:
                            head_out(h - 1)
                head_out(MH - 1)
                dve.wait_ge(s_rt2, l + 1)
                v.reciprocal(ssq2[:], ssq2[:])
                dve.drain().then_inc(s_rh, 1)
                for t in range(TT):
                    o3 = mixt[:, t, 0:T].rearrange("p (h d) -> p h d", h=NH)
                    v.tensor_tensor(o3, o3, ssq2[:, t, 0:NH].unsqueeze(2).broadcast_to([P, NH, DH]), ALU.mult)
                dve.drain().then_inc(s_mixa, 1)
                for c8 in range(KD):
                    dve.wait_ge(s_mhi, l * KD + c8 + 1)
                    v.scalar_tensor_tensor(out=h_lo[:, c8, :], in0=bank[c8 % 4],
                                           scalar=par[:, MG + c8:MG + c8 + 1], in1=h_hi[:, c8, :].bitcast(F32),
                                           op0=ALU.mult, op1=ALU.subtract).then_inc(s_mlo, 1)
                x_update(l, 16)
                norm(l, 2 * l + 1, 2 * KD * l + KD, 1)
                dve.wait_ge(s_aused, l * AUNITS + 24 + CREDIT)
                v.tensor_tensor(mod[:, 40:48], bank[6][:, 40:48], par[:, AB + 40:AB + 48], ALU.add)
                dve.drain().then_inc(s_mod, 1)

                def hidden_step(l, f, i, idx):
                    a_ps, v_ps = pair(f % 3)
                    y = fy[:, f % 2, :]
                    dve.wait_ge(s_y1, l * KF + i * BODY + (f + 1))
                    v.scalar_tensor_tensor(out=y[:, 1:T], in0=a_ps[:, 0:T - 1],
                                           scalar=par[:, bass.ds(idx + FW + KF, 1)], in1=y[:, 1:T],
                                           op0=ALU.mult, op1=ALU.add)
                    dve.drain()
                    v.scalar_tensor_tensor(out=y[:, 2:T], in0=a_ps[:, 0:T - 2],
                                           scalar=par[:, bass.ds(idx + FW, 1)], in1=y[:, 2:T],
                                           op0=ALU.mult, op1=ALU.add).then_inc(s_y2, 1)
                    dve.wait_ge(s_z, l * KF + i * BODY + (f + 1))
                    dve.wait_ge(s_flo, l * KF + i * BODY + (f - 1 + CREDIT))
                    v.tensor_tensor(ft[:, f % 2, :], v_ps, y, ALU.mult).then_inc(s_fv, 1)

                with dve.Fori(0, LOOPED // BODY) as i:
                    for f in range(BODY):
                        hidden_step(l, f, i, i * BODY + f)
                for f in range(LOOPED, KF):
                    hidden_step(l, f, 0, f)
                x_update(l, 40)
            dve.wait_ge(s_rt, 2 * L + 1)
            v.reciprocal(rstd[:], rstd[:])
            dve.drain()
            for c8 in range(KD):
                if c8 >= 2:
                    dve.wait_ge(s_yT, c8 - 1)
                v.scalar_tensor_tensor(out=hm[:, c8 % 2, :], in0=xT[:, c8, :],
                                       scalar=par_all[:, FROW + c8:FROW + c8 + 1], in1=rstd[:],
                                       op0=ALU.mult, op1=ALU.mult).then_inc(s_fin, 1)

        @block.tensor
        def _(pe):
            m = nc.tensor.matmul

            pe.drain().then_inc(s_used, CREDIT)
            pe.drain().then_inc(s_aused, CREDIT)
            pe.wait_ge(s_const, 1)
            pe.wait_ge(s_x, 16 * TT)
            for c8 in range(KD):
                if c8 == 7:
                    pe.wait_ge(s_xu, 1)
                for t in range(TT):
                    last = nc.tensor.transpose(bank[c8 % 7][:, t * P:(t + 1) * P],
                                               xtok[:, t, c8 * P:(c8 + 1) * P], ident[:])
                last.then_inc(s_xT, 1)
            pe.wait_ge(s_par, 16 * len(loads))
            for i in range(4):
                n = min(P, NROW - i * P)
                last = nc.tensor.transpose(bank[7][:, i * P:i * P + n], prow[0:n, i, :], ident[0:n, 0:n])
            last.then_inc(s_prT, 1)
            pe.wait_ge(s_cact, 1)

            def ada(l, j):
                pe.wait_ge(s_a[j % 2], l * (16 * AUNITS // 2) + 16 * (j // 2 + 1))
                for half in range(2):
                    for k in range(KD):
                        last = m(bank[6][:, 2 * j + half:2 * j + half + 1],
                                 a_raw[:, j % 2, k * 256 + half * P:k * 256 + (half + 1) * P],
                                 cact[:, k:k + 1], start=(k == 0), stop=(k == KD - 1))
                last.then_inc(s_aused, 1)

            def sum_squares(n):
                pe.wait_ge(s_sqa, n + 1)
                m(bank[7], ones[:], sqacc[:], start=True, stop=False)
                pe.wait_ge(s_sql, n + 1)
                m(bank[7], ones[:], hm[:, 1, :], start=False, stop=True).then_inc(s_ss, 1)

            def three(ps, l_hi, l_lo, r_hi, r_lo, first, last):
                m(ps, l_hi, r_hi, start=first, stop=False)
                m(ps, l_hi, r_lo, start=False, stop=False)
                return m(ps, l_lo, r_hi, start=False, stop=last)

            def psum_free(l, i):
                b = i - PB
                if b >= PJ_MV:
                    pe.wait_ge(s_mvev, l * TT + b - PJ_MV + 1)
                elif b >= PJ_MQK:
                    pe.wait_ge(s_cv2, l * 2 * MH + b - PJ_MQK + 1)
                elif b >= 0:
                    pe.wait_ge(s_pev, l * PJ_MQK + b + 1)

            def token_unit(l, u, i0, n):
                pe.wait_ge(s_lo, l * UNITS + u + 1)
                for kk in range(4):
                    k = (u % 2) * 4 + kk
                    if u < 2:
                        pe.wait_ge(s_hlo, l * 2 * KD + k + 1)
                    for t in range(TT):
                        if k == 0:
                            psum_free(l, i0 + t)
                        tile = slice(t * P, (t + 1) * P)
                        last = three(bank[(i0 + t) % PB][:, 0:n], h_hi[:, k, tile], h_lo[:, k, tile],
                                     w_hi[:, u % HI, kk * n:(kk + 1) * n], w_lo[:, u % RAW, kk * n:(kk + 1) * n],
                                     k == 0, k == KD - 1)
                        if k == KD - 1 and t < TT - 1:
                            last.then_inc(s_proj, 1)
                last.then_inc(s_used, 1)

            def column_unit(u, banks, nk, rhs, first, last, ready=None):
                for kk in range(nk):
                    if ready is not None:
                        ready(kk)
                    for e in range(2):
                        at = kk * 256 + e * P
                        hi, lo = rhs(kk)
                        ins = three(banks[e], w_hi[:, u % HI, at:at + P], w_lo[:, u % RAW, at:at + P], hi, lo,
                                    first and kk == 0, last and kk == nk - 1)
                return ins

            def h_of(k):
                return h_hi[:, k, :], h_lo[:, k, :]

            with pe.Fori(0, L) as l:
                ada(l, 0)
                ada(l, 1)
                sum_squares(2 * l)
                for j in range(2, 8):
                    ada(l, j)
                for u in range(U_OUT):
                    if u < U_MQK:
                        token_unit(l, u, (u // 2) * TT, 512 if u < 4 else 288)
                    elif u < U_MV:
                        i0 = PJ_MQK + 2 * (u - U_MQK)
                        pe.wait_ge(s_lo, l * UNITS + u + 1)
                        psum_free(l, i0)
                        psum_free(l, i0 + 1)
                        column_unit(u, (bank[i0 % PB], bank[(i0 + 1) % PB]), KD, h_of, True, True)\
                            .then_inc(s_used, 1)
                    else:
                        token_unit(l, u, PJ_MV if u < U_MO else PJ_MO, 512)
                    if u < 12:
                        ada(l, 8 + u)
                    if u == 11:
                        pe.wait_ge(s_pev, l * PJ_MQK + 12)
                        for i, b in enumerate((5, 7)):
                            for t in range(TT):
                                last = nc.tensor.transpose(bank[b][0:MH, t * P:(t + 1) * P],
                                                           gif[:, t, NGATE + i * MH:NGATE + (i + 1) * MH], ident[:])
                        last.then_inc(s_ift, 1)
                pe.wait_ge(s_rope, l + 1)
                for j in range(10):
                    if j == 0:
                        pe.wait_ge(s_mvev, l * TT + TT)
                    elif j < PB:
                        pe.wait_ge(s_moev, l * TT + j)
                    elif j - PB < R:
                        pe.wait_ge(s_tq, l * R + j - PB + 1)
                    else:
                        pe.wait_ge(s_tk, l * 6 + j - PB - R + 1)
                    off = (j * P if j < R else 768 + (j - R) * P if j < R + 2
                           else (512, 1024)[(j - R - 2) // 2] + (j % 2) * P)
                    for t in range(TT):
                        last = nc.tensor.transpose(bank[(PJ + j) % PB][:, t * P:(t + 1) * P],
                                                   tok[:, t, off:off + P], ident[:])
                    last.then_inc(s_tp, 1)
                pe.wait_ge(s_cw, l * 48 + 48)
                pe.wait_ge(s_tk, l * 6 + 6)
                pe.wait_ge(s_mod, l * 3 + 2)
                for n in range(4):
                    for c16 in range(CB // 2):
                        ab, cc = c16 // (CS // 2), c16 % (CS // 2)
                        x3 = xab[:, n, ab, :].rearrange("p (n c) -> p n c", c=CS // 2)
                        last = m(bank[6][0:DH, n * NCP:n * NCP + NC], w1[:, n // 2, c16, :],
                                 x3[:, ab:ab + NC, cc], start=(c16 == 0), stop=(c16 == CB // 2 - 1))
                last.then_inc(s_hid, 1)
                pe.wait_ge(s_hids, l + 1)
                pe.wait_ge(s_ib, l + 1)
                for g in range(NG):
                    m(bank[7][:, 64 + g * DH:64 + (g + 1) * DH], hidv[:, g].rearrange("p r n -> p (r n)"),
                      w2[:, 1, :], start=True, stop=True)
                for g in range(NG):
                    last = m(bank[7][g * DH:(g + 1) * DH, 0:NCP], w2[:, 0, :], hidk[:, g, :], start=True, stop=True)
                last.then_inc(s_cmp, 1)
                pe.wait_ge(s_cmpev, l + 1)
                pe.wait_ge(s_tq, l * R + R)
                for t in range(TT):
                    for r in range(R):
                        last = m(bank[t][:, r * 2 * NCP:(r + 1) * 2 * NCP], qT[:, r, t * P:(t + 1) * P],
                                 kcmp[:].rearrange("p g n -> p (g n)"), start=True, stop=True)
                    last.then_inc(s_cS, 1)
                for t in range(TT):
                    pe.wait_ge(s_cexp, l * TT + t + 1)
                    for g in range(NG):
                        at = (t % 2) * 256 + g * P
                        last = nc.tensor.transpose(bank[4 + t // 2][:, at:at + P],
                                                   csc[:, t, g * R:(g + 1) * R, :].rearrange("p r n -> p (r n)"),
                                                   ident[:])
                    last.then_inc(s_cT, 1)
                for t in range(TT):
                    pe.wait_ge(s_cTev, l * TT + t + 1)
                    for g in range(NG):
                        last = m(bank[t][:, g * R * DH:(g + 1) * R * DH], pT[:, t, g, :],
                                 vcmp[:, g].rearrange("p r d -> p (r d)"), start=True, stop=True)
                    last.then_inc(s_cO, 1)
                pe.wait_ge(s_rows, l + 1)
                for i, rows in enumerate((ib, mrow)):
                    for t in range(TT):
                        last = m(bank[5][:, i * 16 + t * MH:i * 16 + (t + 1) * MH],
                                 rows[:, t * P:(t + 1) * P], ident[0:MH, 0:MH], start=True, stop=True)
                last.then_inc(s_col, 1)

                def scores(w):
                    t, h = w // NH, w % NH
                    g, r, n = h // R, h % R, (w // NH + 1) * P
                    if w >= 2:
                        pe.wait_ge(s_exp, l * 32 + w - 1)
                    for br in range(2):
                        ps = bank[2 * (w % 2) + br]
                        m(ps[:, 0:n], qT[g * DH:(g + 1) * DH, r, t * P:(t + 1) * P],
                          kT[g * DH:(g + 1) * DH, br, 0:n], start=True, stop=False)
                        last = m(ps[:, t * P:n], identb[:], tri[:], start=False, stop=True)
                    last.then_inc(s_S, 1)

                def transposes(w):
                    pe.wait_ge(s_exp, l * 32 + w + 1)
                    if w >= 1:
                        pe.wait_ge(s_ta, l * 32 + w)
                        pe.wait_ge(s_td, l * 32 + w)
                    for br in range(2):
                        for kb in range(w // NH + 1):
                            last = nc.tensor.transpose(bank[4 + br][:, kb * P:(kb + 1) * P],
                                                       probs[:, w % 2, br, kb * P:(kb + 1) * P], ident[:])
                    last.then_inc(s_T, 1)

                def values(w):
                    k, h, t = w // 2, w % NH, w // NH
                    pe.wait_ge(s_ta, l * 32 + w + 1)
                    pe.wait_ge(s_td, l * 32 + w + 1)
                    if w % 2 == 0 and k >= 2:
                        pe.wait_ge(s_oev, l * 16 + k - 1)
                    for br in range(2):
                        at = (w % 2) * 2 * (DH + 1) + br * (DH + 1)
                        for kb in range(t + 1):
                            last = m(bank[6 + k % 2][:, at:at + DH + 1], probsT[:, w % 2, br, kb, :],
                                     v_sw[:, kb, br, h // R, :], start=(kb == 0), stop=(kb == t))
                    last.then_inc(s_PV, 1)

                pe.wait_ge(s_cev, l * TT + TT)
                pe.wait_ge(s_acol, l + 1)
                pe.wait_ge(s_vone, l + 1)
                scores(0)
                for w in range(TT * NH):
                    if w + 1 < TT * NH:
                        scores(w + 1)
                    transposes(w)
                    if w >= 1:
                        values(w - 1)
                values(TT * NH - 1)

                def sources(z):
                    h, j = z // TT, z % TT
                    n = (TT - j) * P
                    if z >= 2:
                        pe.wait_ge(s_mWS, l * 16 + z - 1)
                    ps, bc = pair(z % 2)
                    m(ps[:, 0:n], mqk[:, MH + h, j * P:(j + 1) * P], mqk[:, h, j * P:T], start=True, stop=True)
                    m(bc[:, 0:n], ident[0:MH, h:h + 1].broadcast_to([MH, P]), arow[:, j * P:T],
                      start=True, stop=False)
                    m(bc[:, 0:P], identb[:], triT[:], start=False, stop=True).then_inc(s_mS, 1)

                def head_values(h):
                    pe.wait_ge(s_mWS, l * 16 + 4 * h + 4)
                    for t in range(TT):
                        e = t // 2
                        if t % 2 == 0:
                            if h >= 1:
                                pe.wait_ge(s_mev, l * 8 + 2 * (h - 1) + e + 1)
                            else:
                                pe.wait_ge(s_oev, l * 16 + 15 + e)
                        for j in range(t + 1):
                            at = W_OFF[j] + (t - j) * P
                            last = m(bank[6 + e][:, (t % 2) * (MD + 1):(t % 2 + 1) * (MD + 1)],
                                     mws[:, h % 2, at:at + P], v_m[:, j, h, :], start=(j == 0), stop=(j == t))
                        if t % 2:
                            last.then_inc(s_mO, 1)

                pe.wait_ge(s_cv3, l * 2 * MH + 2 * MH)
                pe.wait_ge(s_exp, l * 32 + 32)
                for z in range(MH * TT):
                    sources(z)
                    if z % TT == 1 and z > TT:
                        head_values(z // TT - 1)
                head_values(MH - 1)

                pe.wait_ge(s_mixa, l + 1)
                pe.wait_ge(s_mixm, l + 1)
                for c8 in range(KD):
                    if c8 >= 4:
                        pe.wait_ge(s_mlo, l * KD + c8 - 3)
                    for t in range(TT):
                        last = nc.tensor.transpose(bank[c8 % 4][:, t * P:(t + 1) * P],
                                                   mixt[:, t, c8 * P:(c8 + 1) * P], ident[:])
                    last.then_inc(s_mT, 1)
                for q in range(4):
                    u = U_OUT + q
                    pe.wait_ge(s_lo, l * UNITS + u + 1)
                    if q == 3:
                        pe.wait_ge(s_xu, KD + 2 * KD * l + 2)

                    def mixed(kk):
                        pe.wait_ge(s_mlo, l * KD + kk + 1)

                    column_unit(u, pair((q + 2) % 3), KD, h_of, True, True, mixed if q == 0 else None)\
                        .then_inc(s_used, 1)
                ada(l, 20)
                ada(l, 21)
                sum_squares(2 * l + 1)
                for j in range(22, 24):
                    ada(l, j)

                def up(l, f, i):
                    pe.wait_ge(s_lo, l * UNITS + i * BODY + (U_UP + f + 1))
                    pe.wait_ge(s_fv, l * KF + i * BODY + (f - 2 + CREDIT))
                    for kk in range(KD):
                        if f == 0:
                            pe.wait_ge(s_hlo, l * 2 * KD + KD + kk + 1)
                        for e in range(2):
                            at = kk * 256 + e * P
                            last = three(pair(f % 3)[e], w_hi[:, f % HI, at:at + P], w_lo[:, f % RAW, at:at + P],
                                         h_hi[:, kk, :], h_lo[:, kk, :], kk == 0, kk == KD - 1)
                    last.then_inc(s_used, 1)

                with pe.Fori(0, LOOPED // BODY) as i:
                    for f in range(BODY):
                        up(l, f, i)
                for f in range(LOOPED, KF):
                    up(l, f, 0)
                for d in range(UNITS - U_DOWN):
                    u, q = U_DOWN + d, d // 3
                    k0, k1 = DOWN_K[d % 3]
                    pe.wait_ge(s_lo, l * UNITS + u + 1)
                    if d % 3 == 0:
                        if q < 3:
                            pe.wait_ge(s_fv, l * KF + 20 + q + CREDIT)
                        else:
                            pe.wait_ge(s_xu, 2 * KD + 2 * KD * l + 2)

                    def made(kk):
                        pe.wait_ge(s_flo, l * KF + k0 + kk + 1 + CREDIT)

                    last = column_unit(u, pair((q + 1) % 3), k1 - k0,
                                       lambda kk: (hid_hi[:, k0 + kk, :], hid_lo[:, k0 + kk, :]),
                                       d % 3 == 0, d % 3 == 2, made if q == 0 else None)
                    last.then_inc(s_used, 1)
            sum_squares(2 * L)
            for c8 in range(KD):
                pe.wait_ge(s_fin, c8 + 1)
                if c8 >= 4:
                    pe.wait_ge(s_yev, c8 - 3)
                for t in range(TT):
                    last = nc.tensor.transpose(bank[c8 % 4][:, t * P:(t + 1) * P],
                                               hm[:, c8 % 2, t * P:(t + 1) * P], ident[:])
                last.then_inc(s_yT, 1)


NAMES = ["x", "c", "positions", "norm1_g", "norm2_g", "ada_w", "ada_b", "w_in", "cmp_pos", "cmp_w1", "cmp_w2",
         "att_norm_g", "m_conv_w", "m_conv_b", "m_gate_b", "m_norm_g", "w_out", "ffn_up", "ffn_conv_w",
         "ffn_conv_b", "ffn_down", "final_g"]


def kernel(**inputs):
    import concourse.bacc as bacc
    from concourse.bass_utils import run_bass_kernel_spmd

    nc = bacc.Bacc("TRN2", target_bir_lowering=False, num_devices=1)
    arrays, args = {}, []
    for name in NAMES:
        a = np.ascontiguousarray(inputs[name])
        arrays[f"in_{name}"] = a
        args.append(nc.dram_tensor(f"in_{name}", a.shape, dt.from_np(a.dtype), kind="ExternalInput").ap())
    out = nc.dram_tensor("out", (1, T, D), F32, kind="ExternalOutput").ap()
    build(nc, *args, out)
    r = run_bass_kernel_spmd(nc, [arrays], core_ids=[0])
    return r.results[0]["out"]
```

```python
from contextlib import ExitStack

import numpy as np
import concourse.bass as bass
from concourse import mybir

dt = mybir.dt
F32, F32R, BF16 = dt.float32, dt.float32r, dt.bfloat16
ALU = mybir.AluOpType
ACT = mybir.ActivationFunctionType
AX = mybir.AxisListType

P = 128
D = 1024
T = 512
L = 2
KD = D // P
TT = T // P
F = 2816
KF = F // P
NH, DH, NG = 8, 64, 2
R = NH // NG
MH, MD = 4, 128
MC, FC = 4, 3
HALF = 8
CB, CS = 32, 16
NC = (T - CB) // CS + 1
NCP = NC + 1
IN_COLS = 3360
EPS = 1e-6
NEG = -1e30
TINY = 1e-30
MSCALE = float(np.float32(MD ** -0.5))

C_Q, C_KC, C_VC, C_KS, C_VS, C_KW, C_VW, C_G = 0, 512, 640, 768, 896, 1024, 1152, 1280
C_MQK, C_MV, C_IF, C_MO = 1304, 2328, 2840, 2848
NGATE = 24

PARS = [("ada_b", 48), ("norm1_g", KD), ("norm2_g", KD), ("m_conv_w", 4 * KD), ("cmp_pos", CB),
        ("ffn_conv_b", KF), ("m_conv_b", KD), ("ffn_conv_w", 3 * KF), ("att_norm_g", KD // 2),
        ("m_norm_g", KD // 2)]
AB, N1, N2, MW, CP, FB, MB, FW, MG = (sum(n for _, n in PARS[:i]) for i in range(9))
NPAR = sum(n for _, n in PARS)

U_QKV, U_MV, U_MO, U_MQK, U_OUT, U_UP, U_DOWN, UNITS = 0, 6, 8, 10, 14, 18, 40, 52
SLOT = 2048
RAW, HI = 3, 2
AUNITS = 24
ARING = 4
EARLY = 8
DOWN_K = [(0, 8), (8, 15), (15, 22)]
BODY = 6
LOOPED = KF // BODY * BODY
CREDIT = 2

PB = 5
NJ = 16
J_K, J_X = 8, 12
T_BANK = (4, 5, 7, 6)
NW = NH * TT
W_OFF = [0, 512, 896, 1152]
W_ALL = 1280


NEXT_AT = {18: 0, 20: 1, 21: 2, 22: 3, 23: 4, 25: 5, 27: 6, 29: 7}


def slot_need(u):
    return u - 2 if u >= RAW else (0, -2, -1)[u]


def build(nc, x, c, positions, norm1_g, norm2_g, ada_w, ada_b, w_in, cmp_pos, cmp_w1, cmp_w2,
          att_norm_g, m_conv_w, m_conv_b, m_gate_b, m_norm_g, w_out, ffn_up, ffn_conv_w,
          ffn_conv_b, ffn_down, final_g, out):
    ctx = ExitStack()
    with ctx:
        cursor = [16512]

        def place(name, shape, dtype=F32, at=None):
            size = int(np.prod(shape[1:])) * (2 if dtype == BF16 else 4)
            if at is None:
                at = cursor[0]
                cursor[0] += (size + 31) // 32 * 32
            return nc.alloc_sbuf_tensor_at(name, shape, dtype, offset=at)

        xT = place("xT", [P, KD, T])
        h_hi = place("h_hi", [P, KD, T], F32R)
        ot = place("ot", [DH + 1, 2, T], at=cursor[0])
        h_lo = place("h_lo", [P, KD, T], F32R)
        raw_at = cursor[0]
        w_raw = place("w_raw", [P, RAW, SLOT])
        w_lo = place("w_lo", [P, RAW, SLOT], F32R, at=raw_at)
        w_hi = place("w_hi", [P, HI, SLOT], F32R)
        rstd = place("rstd", [P, T])
        hm_at = cursor[0]
        hm = place("hm", [P, 3, T])
        asum = place("asum", [P, 2, T], at=hm_at)
        ident = place("ident", [P, P])
        identr = place("identr", [8, P], F32R)
        identb = place("identb", [P, P], BF16)
        tri = place("tri", [P, P], BF16)
        triT = place("triT", [P, P], BF16)
        ones = place("ones", [P, P])
        eps = place("eps", [P, 1])
        par_all = place("par_all", [P, 4, P])
        par = place("par", [P, NPAR])
        cact = place("cact", [P, KD])
        mod = place("mod", [P, 48])
        am = place("am", [P, 2, KD])
        cos = place("cos", [P, TT, 2, HALF])
        sin = place("sin", [P, TT, 2, HALF])
        cmask = place("cmask", [P, TT, NCP])
        gate_b = place("gate_b", [MH, L, 2])
        ada_at = cursor[0]
        a_raw = place("a_raw", [P, 2, SLOT])
        union = cursor[0]
        hid_hi = place("hid_hi", [P, KF, T], F32R)
        hid_lo = place("hid_lo", [P, KF, T], F32R)
        end = cursor[0]

        class Region:
            def __init__(self, at, stop):
                self.at, self.stop = at, stop

            def place(self, name, shape, dtype=F32):
                size = (int(np.prod(shape[1:])) * 4 + 31) // 32 * 32
                t = place(name, shape, dtype, at=self.at)
                self.at += size
                assert self.at <= self.stop, (name, self.at - self.stop)
                return t

        mix = Region(union, end)
        tok_at = mix.at
        tok = mix.place("tok", [P, NJ, TT, P])
        qk = place("qk", [P, NJ, T], F32R, at=tok_at)
        mw = place("mw", [P, 3, T], at=tok_at)
        mws = place("mws", [P, 2, W_ALL], at=tok_at + 3 * T * 4)
        v_sw = mix.place("v_sw", [P, TT, 2, NG, DH + 1])
        v_m = mix.place("v_m", [P, TT, MH, MD + 1])
        mixt_at = mix.at
        mixt = mix.place("mixt", [P, TT, D])
        a_mix = place("a_mix", [P, 2, SLOT], at=mixt_at)
        a_slot = [a_raw[:, 0, :], a_raw[:, 1, :], a_mix[:, 0, :], a_mix[:, 1, :]]
        mqk_at = mix.at
        mqk = mix.place("mqk", [P, 2 * MH, T])
        xab = place("xab", [P, 4, 2, CS // 2 * NCP], at=mqk_at)
        w1 = place("w1", [P, 2, CB // 2, DH], at=mqk_at + 8192)
        arow = mix.place("arow", [MH, T])
        late = mix.at
        pt = mix.place("pt", [P, 2, 2, T])
        rt = place("rt", [P, 2, 14, 2 * TT, HALF], at=late)
        pT = place("pT", [P, TT, 2, P], at=late)
        gif = mix.place("gif", [P, TT, NGATE + 2 * MH])
        asum0 = place("asum0", [P, 2, T], at=mixt_at - 8256)
        a_mqk = place("a_mqk", [P, 2, SLOT], at=mqk_at)
        a_tok = place("a_tok", [P, 2, SLOT], at=tok_at + 16384)
        a_early = a_slot + [a[:, i, :] for a in (a_mqk, a_tok) for i in range(2)]
        xtok = place("xtok", [P, TT, D], at=tok_at)
        otok = place("otok", [P, TT, D], at=mixt_at)
        prow = place("prow", [P, 4, P], at=late)
        pos_i = place("pos_i", [P, TT], dt.int32, at=late + 4096)
        ang = place("ang", [P, TT, HALF], at=late + 4096 + 64)
        angn = place("angn", [P, TT, HALF], at=late + 4096 + 64 + 128)
        posf = place("posf", [P, TT], at=late + 4096 + 64 + 256)
        invf = place("invf", [P, HALF], at=late + 4096 + 64 + 288)
        over = place("over", [P, TT, HALF], at=late + 4096 + 64 + 320)

        att = Region(ada_at, union)
        ib, fb, fe, brow = (att.place(n, [MH, T]) for n in ("ib", "fb", "fe", "brow"))
        mrow = fe
        t12 = place("t12", [P, 2, 2, TT, DH], at=ada_at)
        sqb = place("sqb", [P, TT, DH], at=ada_at + 4096)
        gat = att.place("gat", [P, TT, NGATE])
        csc = place("csc", [P, TT, NH, NCP], at=hm_at)
        nrow = place("nrow", [8, 2, T], F32R, at=hm_at)
        hidk = att.place("hidk", [DH, NG, NCP])
        hidv = att.place("hidv", [DH, NG, 4, NCP])
        kcmp = att.place("kcmp", [P, NG, NCP])
        vcmp = att.place("vcmp", [P, NG, R, DH])
        w2 = att.place("w2", [DH, 2, DH])
        cmx = att.place("cmx", [P, TT, NH])
        csum = att.place("csum", [P, TT, NH])
        nmx = att.place("nmx", [P, 2, TT, R, 2])
        coef = att.place("coef", [P, 2, TT])
        acol = att.place("acol", [P, 2, TT, MH])
        den = att.place("den", [P, 2, 2])
        ssq = att.place("ssq", [P, TT, NH + MH])
        ssq2 = att.place("ssq2", [P, TT, NH + MH])
        sqj = att.place("sqj", [P, MD])

        ffn = Region(ada_at, union)
        fy = ffn.place("fy", [P, 2, T])
        ft = ffn.place("ft", [P, 2, T])

        psum = ctx.enter_context(nc.psum_tensor("psum", [P, 8, T], F32))
        bank = [psum[:, i, :] for i in range(8)]

        def sem(name):
            return ctx.enter_context(nc.semaphore(name))

        s_w = [sem(f"s_w{i}") for i in range(RAW)]
        s_a = [sem(f"s_a{i}") for i in range(ARING)]
        s_e = [sem(f"s_e{i}") for i in range(EARLY)]
        s_asum, s_ag = sem("s_asum"), sem("s_ag")
        s_cw = sem("s_cw")
        s_x, s_par, s_pos, s_out = sem("s_x"), sem("s_par"), sem("s_pos"), sem("s_out")
        s_const, s_ang, s_sin = sem("s_const"), sem("s_ang"), sem("s_sin")
        s_prT, s_pall, s_cact, s_xT = sem("s_prT"), sem("s_pall"), sem("s_cact"), sem("s_xT")
        s_hi, s_lo, s_used = sem("s_hi"), sem("s_lo"), sem("s_used")
        s_aused, s_mod = sem("s_aused"), sem("s_mod")
        s_sqa, s_sql, s_ss, s_rt = sem("s_sqa"), sem("s_sql"), sem("s_ss"), sem("s_rt")
        s_hm, s_hhi, s_hlo = sem("s_hm"), sem("s_hhi"), sem("s_hlo")
        s_proj = sem("s_proj")
        s_qev, s_pev, s_mvev, s_moev = (sem(n) for n in ("s_qev", "s_pev", "s_mvev", "s_moev"))
        s_vone = sem("s_vone")
        s_cv1, s_cv2, s_cv3 = sem("s_cv1"), sem("s_cv2"), sem("s_cv3")
        s_rope = sem("s_rope")
        s_ift, s_ib, s_ln, s_rows, s_col, s_acol = (sem(n) for n in
                                                    ("s_ift", "s_ib", "s_ln", "s_rows", "s_col", "s_acol"))
        s_tp, s_thi, s_tev = sem("s_tp"), sem("s_thi"), sem("s_tev")
        s_hid, s_hids, s_cmp, s_cmpev = sem("s_hid"), sem("s_hids"), sem("s_cmp"), sem("s_cmpev")
        s_cS, s_csub, s_cexp, s_cT, s_cTev, s_cO, s_cev = (sem(n) for n in (
            "s_cS", "s_csub", "s_cexp", "s_cT", "s_cTev", "s_cO", "s_cev"))
        s_gat = sem("s_gat")
        s_S, s_nm, s_ST, s_exp, s_PV = (sem(n) for n in ("s_S", "s_nm", "s_ST", "s_exp", "s_PV"))
        s_nr, s_nrow = sem("s_nr"), sem("s_nrow")
        s_oev, s_oT = sem("s_oev"), sem("s_oT")
        s_gated, s_comb, s_asq = sem("s_gated"), sem("s_comb"), sem("s_asq")
        s_mS, s_mW, s_mWS = sem("s_mS"), sem("s_mW"), sem("s_mWS")
        s_mO, s_mev = sem("s_mO"), sem("s_mev")
        s_rt2, s_rh, s_mixa, s_mixm = sem("s_rt2"), sem("s_rh"), sem("s_mixa"), sem("s_mixm")
        s_mT, s_mhi, s_mlo = sem("s_mT"), sem("s_mhi"), sem("s_mlo")
        s_xu = sem("s_xu")
        s_y1, s_y2, s_z, s_fv, s_fhi, s_flo = (sem(n) for n in (
            "s_y1", "s_y2", "s_z", "s_fv", "s_fhi", "s_flo"))
        s_fin, s_yT, s_yev = sem("s_fin"), sem("s_yT"), sem("s_yev")

        block = ctx.enter_context(nc.Block())

        def pair(i):
            return bank[2 * i], bank[2 * i + 1]

        C_BANK = (6, 7, 4, 5)

        def score_bank(w):
            return 4 if w < NW // 2 and w % 2 else 6

        def beside(z):
            a = NW // 2 + z + (z + 2) // 3
            return [] if z >= 12 else [a, a + 1] if z % 3 == 0 else [a]

        def done_beside(z):
            return sum(len(beside(i)) for i in range(z + 1))

        def unit_used(eng, l, u):
            eng.wait_ge(s_used, l * UNITS + (u + 1 + CREDIT))

        def projected(eng, l, group, t):
            if t < TT - 1:
                eng.wait_ge(s_proj, l * 5 * (TT - 1) + group * (TT - 1) + t + 1)
            else:
                unit_used(eng, l, 2 * group + 1)

        ffw = ffn_conv_w.rearrange("l w (r q) -> l (w r) q", q=P)
        tiles = [[("ada_b", ada_b.rearrange("l (r q) -> (l r) q", q=P)),
                  ("norm1_g", norm1_g.rearrange("l (r q) -> (l r) q", q=P)),
                  ("norm2_g", norm2_g.rearrange("l (r q) -> (l r) q", q=P))],
                 [("m_conv_w", m_conv_w.rearrange("l w (r q) -> (l w r) q", q=P)),
                  ("cmp_pos", cmp_pos.rearrange("l i (c s) d -> (l i c) (s d)", s=2))],
                 [("ffn_conv_w", ffw[0]), ("ffn_conv_b", ffn_conv_b.rearrange("l (r q) -> (l r) q", q=P)),
                  ("m_conv_b", m_conv_b.rearrange("l (r q) -> (l r) q", q=P))],
                 [("c", c.rearrange("o (r q) -> (o r) q", q=P)),
                  ("att_norm_g", att_norm_g.rearrange("l (r q) -> (l r) q", q=P)),
                  ("m_norm_g", m_norm_g.rearrange("l (r q) -> (l r) q", q=P)),
                  ("final_g", final_g.rearrange("(r q) -> r q", q=P)), ("ffn_conv_w1", ffw[1])]]
        loads, where, tile_rows = [], {}, []
        for i, tile in enumerate(tiles):
            row = 0
            for name, src in tile:
                loads.append((i, row, src))
                where[name] = i * P + row
                row += src.shape[0]
            assert row <= P
            tile_rows.append(row)
        CROW, FROW = where["c"], where["final_g"]
        step_of = {name: n for name, n in PARS}
        step_of["ffn_conv_w"] = where["ffn_conv_w1"] - where["ffn_conv_w"]

        @block.sync
        def _(sp):
            for t in range(TT):
                sp.dma_start(xtok[:, t, :], x[0, t * P:(t + 1) * P, :]).then_inc(s_x, 16)
            sp.dma_start(gate_b[:], m_gate_b.rearrange("l (t h) -> h l t", t=2),
                         allow_slow_non_contiguous=True).then_inc(s_pos, 16)

            sp.wait_ge(s_par, 16 * len(loads))
            for i in range(EARLY):
                sp.dma_start(a_early[i].rearrange("p (k n) -> p k n", k=KD // 2),
                             ada_w.rearrange("l (k p) n -> l p k n", p=P)
                             [0, :, i % 2 * 4:i % 2 * 4 + 4, i // 2 * T:(i // 2 + 1) * T]).then_inc(s_e[i], 16)

            def load(l, u, parts):
                parts = list(parts)
                sp.wait_ge(s_used, l * UNITS + slot_need(u) + CREDIT)
                for dst, src in parts:
                    sp.dma_start(dst, src).then_inc(s_w[u % RAW], 16)

            def slot(u, k, n):
                return w_raw[:, u % RAW, 0:k * n].rearrange("p (k n) -> p k n", k=k)

            def load_rows(l, u, w, col, n):
                half = (u % 2) * 4
                src = w.rearrange("l (k p) n -> l p k n", p=P)
                for i in range(2):
                    yield (slot(u, 4, n)[:, 2 * i:2 * i + 2, :],
                           src[l, :, half + 2 * i:half + 2 * i + 2, col:col + n])

            def load_cols(l, u, w, col, k0, k1):
                src = w.rearrange("l (k p) n -> l p k n", p=P)
                mid = (k1 - k0) // 2
                for a, b in ((0, mid), (mid, k1 - k0)):
                    yield slot(u, k1 - k0, 256)[:, a:b, :], src[l, :, k0 + a:k0 + b, col:col + 256]

            def ada_rows(l, j):
                return ada_w.rearrange("l (k p) n -> l p k n", p=P)[
                    l, :, j % 2 * 4:j % 2 * 4 + 4, j // 2 * T:(j // 2 + 1) * T]

            def load_ada(l, j):
                sp.wait_ge(s_aused, l * AUNITS + max(j - ARING + 1, EARLY))
                sp.dma_start(a_slot[j % ARING].rearrange("p (k n) -> p k n", k=KD // 2), ada_rows(l, j))\
                    .then_inc(s_a[j % ARING], 16)

            def load_next(l, after, i):
                sp.wait_ge(s_aused, l * AUNITS + (AUNITS + i))
                sp.dma_start(a_slot[1].rearrange("p (k n) -> p k n", k=KD // 2), ada_rows(after, i))\
                    .then_inc(s_e[i], 16)

            def load_w_in(l, u):
                if u < 4:
                    load(l, u, load_rows(l, u, w_in, (u // 2) * 512, 512))
                elif u < 6:
                    half = (u % 2) * 4
                    src = w_in.rearrange("l (k p) n -> l p k n", p=P)
                    dst = slot(u, 4, 288)
                    load(l, u, [(dst[:, :, 0:280], src[l, :, half:half + 4, 1024:1304]),
                                (dst[:, :, 280:288], src[l, :, half:half + 4, C_IF:C_IF + 8])])
                elif u < U_MQK:
                    load(l, u, load_rows(l, u, w_in, C_MV if u < U_MO else C_MO, 512))
                else:
                    load(l, u, load_cols(l, u, w_in, C_MQK + (u - U_MQK) * 256, 0, KD))

            def load_up(l, u, j):
                src = ffn_up.rearrange("l (k p) n -> l p k n", p=P)
                dst = w_raw[:, u % RAW, :].rearrange("p (k n) -> p k n", k=KD)
                load(l, u, [(dst[:, :, 0:P], src[l, :, :, bass.ds(j * P, P)]),
                            (dst[:, :, P:2 * P], src[l, :, :, bass.ds(j * P + F, P)])])

            with sp.Fori(0, L) as l:
                after = sp.snap(l * -1 + (L - 1))
                for u in range(RAW):
                    load_w_in(l, u)
                for j in range(EARLY, EARLY + 2):
                    load_ada(l, j)
                for i in range(2):
                    sp.dma_start(w1[:, i, :, :], cmp_w1.rearrange("l i (c p) j -> l p i c j", p=P)[l, :, i])\
                        .then_inc(s_cw, 16)
                for u in range(RAW, U_OUT):
                    load_w_in(l, u)
                    for j in {3: range(10, 14), 4: range(14, 18), 5: (18, 19), 6: (20, 21), 8: (22, 23)}.get(u, ()):
                        load_ada(l, j)
                    if u == 11:
                        sp.wait_ge(s_aused, l * AUNITS + AUNITS)
                        sp.dma_start(w2[:], cmp_w2.rearrange("l i j d -> l j i d")[l]).then_inc(s_cw, 16)
                for u in range(U_OUT, U_UP):
                    load(l, u, load_cols(l, u, w_out, (u - U_OUT) * 256, 0, KD))
                with sp.Fori(0, LOOPED // BODY) as i:
                    for s in range(BODY):
                        u = U_UP + s
                        sp.wait_ge(s_used, l * UNITS + i * BODY + (slot_need(u) + CREDIT))
                        src = ffn_up.rearrange("l (k p) n -> l p k n", p=P)
                        dst = w_raw[:, u % RAW, :].rearrange("p (k n) -> p k n", k=KD)
                        for side in range(2):
                            sp.dma_start(dst[:, :, side * P:(side + 1) * P],
                                         src[l, :, :, bass.ds(i * (BODY * P) + (s * P + side * F), P)])\
                                .then_inc(s_w[u % RAW], 16)
                for j in range(LOOPED, KF):
                    load_up(l, U_UP + j, j)
                    if j in NEXT_AT:
                        load_next(l, after, NEXT_AT[j])
                for d in range(UNITS - U_DOWN):
                    u = U_DOWN + d
                    load(l, u, load_cols(l, u, ffn_down, (d // 3) * 256, *DOWN_K[d % 3]))
                    if KF + d in NEXT_AT:
                        load_next(l, after, NEXT_AT[KF + d])
            for c8 in range(KD):
                sp.wait_ge(s_yev, c8 + 1)
                sp.dma_start(out[0].rearrange("(t p) n -> p t n", p=P)[:, :, c8 * P:(c8 + 1) * P],
                             otok[:, :, c8 * P:(c8 + 1) * P]).then_inc(s_out, 16)
            sp.wait_ge(s_out, 16 * KD)

        @block.gpsimd
        def _(pool):
            g = nc.gpsimd
            g.memset(ident[:], 0.0)
            g.memset(identb[:], 0.0)
            g.memset(tri[:], 0.0)
            g.memset(triT[:], 0.0)
            g.memset(ones[:], 1.0)
            g.memset(cmask[:], 0.0)
            g.memset(eps[:], EPS)
            pool.drain()
            for m in (ident, identb):
                g.affine_select(out=m[:], in_=m[:], compare_op=ALU.not_equal, fill=1.0, base=0,
                                pattern=[[-1, P]], channel_multiplier=1)
            g.affine_select(out=tri[:], in_=tri[:], compare_op=ALU.is_ge, fill=NEG, base=0,
                            pattern=[[-1, P]], channel_multiplier=1)
            g.affine_select(out=triT[:], in_=triT[:], compare_op=ALU.is_ge, fill=NEG, base=0,
                            pattern=[[1, P]], channel_multiplier=-1)
            g.affine_select(out=cmask[:], in_=cmask[:], compare_op=ALU.is_ge, fill=NEG, base=-(CB - 1),
                            pattern=[[P, TT], [-CS, NCP]], channel_multiplier=1)
            pool.drain().then_inc(s_const, 1)
            pool.drain().then_inc(s_flo, CREDIT)

            def low(l, u, i=0):
                pool.wait_ge(s_hi, l * UNITS + i * BODY + (u + 1))
                g.tensor_tensor(w_lo[:, u % RAW, :], w_raw[:, u % RAW, :],
                                w_hi[:, u % HI, :].bitcast(F32), ALU.subtract).then_inc(s_lo, 1)

            def low_part(l, u, n):
                pool.wait_ge(s_hi, l * UNITS + u + 1)
                g.tensor_tensor(w_lo[:, u % RAW, 0:n], w_raw[:, u % RAW, 0:n],
                                w_hi[:, u % HI, 0:n].bitcast(F32), ALU.subtract).then_inc(s_lo, 1)

            def square(first, norm, c8):
                pool.wait_ge(s_xu, first + c8 + 1)
                if c8 == 0:
                    pool.wait_ge(s_ss, norm)
                    g.tensor_tensor(hm[:, 2, :], xT[:, 0, :], xT[:, 0, :], ALU.mult)
                else:
                    g.tensor_tensor(rstd[:], xT[:, c8, :], xT[:, c8, :], ALU.mult)
                    pool.drain()
                    g.tensor_tensor(hm[:, 2, :], hm[:, 2, :], rstd[:], ALU.add)
                if c8 == KD - 3:
                    pool.drain().then_inc(s_sqa, 1)
                else:
                    pool.drain()

            for c8 in range(KD - 2):
                square(0, 0, c8)
            with pool.Fori(0, L) as l:
                low(l, 0)
                pool.wait_ge(s_ss, 2 * l + 1)
                low(l, 1)
                g.memset(v_sw[:, :, :, :, DH:DH + 1], 1.0)
                g.memset(v_m[:, :, :, MD:MD + 1], 1.0)
                pool.drain().then_inc(s_vone, 1)
                for u in range(2, 16):
                    if u in (4, 5):
                        low_part(l, u, 4 * 288)
                    else:
                        low(l, u)
                for h in range(NH):
                    pool.wait_ge(s_gated, l * NH + h + 1)
                    o3 = mixt[:, :, h * DH:(h + 1) * DH]
                    for br in range(2):
                        g.tensor_tensor(o3, o3, t12[:, h % 2, br], ALU.add)
                        if br == 0:
                            pool.drain()
                    pool.drain()
                    if h >= 1:
                        pool.wait_ge(s_asq, l * NH + h)
                    g.tensor_tensor(sqb[:], o3, o3, ALU.mult).then_inc(s_comb, 1)
                pool.wait_ge(s_rh, l + 1)
                for t in range(TT):
                    o3 = mixt[:, t, T:D].rearrange("p (h d) -> p h d", h=MH)
                    g.tensor_tensor(o3, o3, ssq2[:, t, NH:NH + MH].unsqueeze(2).broadcast_to([P, MH, MD]),
                                    ALU.mult)
                pool.drain().then_inc(s_mixm, 1)
                for q in range(4):
                    if q < 3:
                        low(l, 16 + q)
                    for c8 in (2 * q, 2 * q + 1):
                        if c8 < KD - 2:
                            square(KD + 2 * KD * l, 2 * l + 1, c8)
                low(l, 19)

                def hidden_low(l, f, i, idx):
                    pool.wait_ge(s_fhi, l * KF + i * BODY + (f + 1))
                    g.tensor_tensor(hid_lo[:, bass.ds(idx, 1), :], ft[:, f % 2:f % 2 + 1, :],
                                    hid_hi[:, bass.ds(idx, 1), :].bitcast(F32), ALU.subtract)\
                        .then_inc(s_flo, 1)

                with pool.Fori(0, LOOPED // BODY) as i:
                    for s in range(BODY):
                        low(l, U_UP + 2 + s, i)
                        hidden_low(l, s, i, i * BODY + s)
                for f in range(LOOPED, KF):
                    if f + 2 + U_UP < U_DOWN:
                        low(l, U_UP + 2 + f)
                    else:
                        d = f + 2 + U_UP - U_DOWN
                        k0, k1 = DOWN_K[d % 3]
                        low_part(l, U_DOWN + d, (k1 - k0) * 256)
                    hidden_low(l, f, 0, f)
                for q in range(4):
                    for d in range(3 * q + 2, min(3 * q + 5, UNITS - U_DOWN)):
                        k0, k1 = DOWN_K[d % 3]
                        low_part(l, U_DOWN + d, (k1 - k0) * 256)
                    for c8 in (2 * q, 2 * q + 1):
                        if c8 < KD - 2:
                            square(2 * KD + 2 * KD * l, 2 * l + 2, c8)

        @block.scalar
        def _(act):
            s = nc.scalar

            act.dma_start(pos_i[:], positions[0].rearrange("(t p) -> p t", p=P),
                          allow_slow_non_contiguous=True).then_inc(s_pos, 16)
            for i, row, src in sorted(loads, key=lambda x: -x[0]):
                act.dma_start(prow[row:row + src.shape[0], i, :], src).then_inc(s_par, 16)

            def rope_tables():
                act.wait_ge(s_ang, 1)
                for i in range(2):
                    s.activation(sin[:, :, i, :], ang[:], ACT.Sin)
                act.wait_ge(s_ang, 2)
                for i in range(2):
                    last = s.activation(cos[:, :, i, :], angn[:], ACT.Sin)
                last.then_inc(s_sin, 1)
                act.wait_ge(s_const, 1)
                s.activation(identr[:], ident[0:8, :], ACT.Copy)

            def last_squares(first, norm, late=None):
                for i in range(2):
                    act.wait_ge(s_xu, first + KD - 1 + i)
                    if late is not None and i == 0:
                        act.wait_ge(s_ag, late)
                    if i == 0:
                        act.wait_ge(s_ss, norm)
                    s.activation(hm[:, i, :], xT[:, KD - 2 + i, :], ACT.Square).then_inc(s_sql, 1)

            def high(l, u, i=0, n=SLOT):
                r = u % RAW
                before = u // RAW
                per = (UNITS + RAW - 1 - r) // RAW
                act.wait_ge(s_w[r], l * (32 * per) + i * (32 * BODY // RAW) + 32 * (before + 1))
                act.wait_ge(s_used, l * UNITS + i * BODY + (u - 1 + CREDIT))
                s.activation(w_hi[:, u % HI, 0:n], w_raw[:, r, 0:n], ACT.Copy).then_inc(s_hi, 1)

            def width(u):
                if u in (4, 5):
                    return 4 * 288
                if u >= U_DOWN:
                    k0, k1 = DOWN_K[(u - U_DOWN) % 3]
                    return (k1 - k0) * 256
                return SLOT

            def norm_root(norm):
                act.wait_ge(s_ss, norm + 1)
                s.activation(rstd[:], bank[7], ACT.Sqrt, bias=eps[:, 0:1], scale=1.0 / D).then_inc(s_rt, 1)

            def norm_high(chunks, shift):
                for c8 in range(KD):
                    act.wait_ge(s_hm, chunks + c8 + 1)
                    s.activation(h_hi[:, c8, :], hm[:, c8 % 3, :], ACT.Identity,
                                 bias=mod[:, shift + c8:shift + c8 + 1]).then_inc(s_hhi, 1)

            rope_tables()
            act.wait_ge(s_pall, 1)
            s.activation(cact[:], par_all[:].rearrange("p a b -> p (a b)")[:, CROW:CROW + KD], ACT.Silu)\
                .then_inc(s_cact, 1)
            for c8 in range(KD):
                act.wait_ge(s_xT, c8 + 1)
                s.activation(xT[:, c8, :], bank[c8 % 6], ACT.Copy).then_inc(s_xu, 1)
            last_squares(0, 0)
            with act.Fori(0, L) as l:
                norm_root(2 * l)
                high(l, 0)
                norm_high(2 * KD * l, 0)
                high(l, 1)
                def conv_first(c8):
                    s.activation(mqk[:, c8, :], bank[c8 % 4], ACT.Identity, bias=par[:, MB + c8:MB + c8 + 1],
                                 scale=par[:, MW + 3 * KD + c8:MW + 3 * KD + c8 + 1]).then_inc(s_cv1, 1)

                def conv_silu(c8):
                    act.wait_ge(s_cv2, l * 2 * MH + c8 + 1)
                    s.activation(mqk[:, c8, :], mqk[:, c8, :], ACT.Silu).then_inc(s_cv3, 1)

                def high_of(j, scale):
                    act.wait_ge(s_tp, l * NJ + (j - J_K + 4 if j >= J_K else j + 8) + 1)
                    b = T_BANK[(j - J_K + 4 if j >= J_K else j + 8) % 4]
                    s.activation(qk[:, j, :], bank[b], ACT.Copy, scale=scale).then_inc(s_thi, 1)

                for u in range(U_OUT):
                    if u == U_MO + 1:
                        for j in range(J_K, J_K + 4):
                            high_of(j, 1.0)
                        for j in range(NH):
                            high_of(j, DH ** -0.5)
                    if u == U_MQK + 3:
                        act.wait_ge(s_col, l + 1)
                        cols = bank[6][:, 0:2 * TT * MH].rearrange("p (i t h) -> p i t h", i=2, t=TT)
                        s.activation(acol[:, 0], cols[:, 0], ACT.Copy)
                        s.activation(acol[:, 1], cols[:, 1], ACT.Exp, scale=-1.0).then_inc(s_acol, 1)
                    high(l, u + 2, n=width(u + 2))
                    if u == 1:
                        for t in range(TT):
                            projected(act, l, 0, t)
                            s.activation(tok[:, 0:NH, t, :].rearrange("p h (s d) -> p h s d", s=2),
                                         bank[t].rearrange("p (h s d) -> p h s d", h=NH, s=1)
                                         .broadcast_to([P, NH, 2, DH]), ACT.Copy).then_inc(s_qev, 1)
                    if u == U_MQK - 1:
                        for t in range(TT):
                            projected(act, l, 4, t)
                            s.activation(mixt[:, t, T:D], bank[t], ACT.Sigmoid).then_inc(s_moev, 1)
                        s.activation(gat[:], gif[:, :, 0:NGATE], ACT.Sigmoid).then_inc(s_gat, 1)
                    if u >= U_MQK:
                        for c8 in (2 * (u - U_MQK), 2 * (u - U_MQK) + 1):
                            conv_first(c8)
                    if u == U_MQK:
                        act.wait_ge(s_hid, l + 1)
                        hid_ps = bank[4][0:DH, 0:4 * NCP].rearrange("p (i g n) -> p i g n", i=2, g=NG)
                        s.activation(hidk[:, :, 0:NC], hid_ps[:, 0, :, 0:NC], ACT.Silu)
                        for gr in range(NG):
                            last = s.activation(hidv[:, gr, :, 0:NC],
                                                hid_ps[:, 1, gr:gr + 1, 0:NC].broadcast_to([DH, 4, NC]), ACT.Silu)
                        last.then_inc(s_hids, 1)
                    if u == U_MQK + 1:
                        for c8 in (0, 1):
                            conv_silu(c8)
                        act.wait_ge(s_ib, l + 1)
                        s.activation(fe[:], fe[:], ACT.Exp, scale=-1.0)
                        act.drain()
                        s.activation(fe[:], fe[:], ACT.Ln, bias=ones[0:MH, 0:1]).then_inc(s_ln, 1)
                        for t in range(TT):
                            act.wait_ge(s_csub, l * TT + t + 1)
                            s.activation(csc[:, t], csc[:, t], ACT.Exp).then_inc(s_cexp, 1)
                for c8 in range(2, 2 * MH):
                    conv_silu(c8)

                def max_rows(g):
                    act.wait_ge(s_nr, l * 2 + g + 1)
                    s.activation(nrow[:, g, :], bank[6][0:8, :], ACT.Copy).then_inc(s_nrow, 1)

                max_rows(0)
                def evacuate(h):
                    act.wait_ge(s_PV, l * NW + TT * h + TT)
                    if h:
                        act.wait_ge(s_oT, l * NH + h)
                    s.activation(ot[:], psum[0:DH + 1, 4:6, :], ACT.Copy).then_inc(s_oev, 1)

                for z in range(NW):
                    if z % TT == 1 and z > TT:
                        evacuate(z // TT - 1)
                    if z == 15:
                        max_rows(1)
                    n = (TT - z % TT) * P
                    act.wait_ge(s_ST, l * NW + z + 1)
                    if z >= 2:
                        act.wait_ge(s_PV, l * NW + z - 1)
                    s.activation(pt[:, z % 2, :, 0:n], psum[:, 2 * (z % 2):2 * (z % 2) + 2, 0:n], ACT.Exp)\
                        .then_inc(s_exp, 1)
                evacuate(NH - 1)
                for h in range(MH + 1):
                    if h < MH:
                        for j in range(TT):
                            z = h * TT + j
                            n = (TT - j) * P
                            act.wait_ge(s_mS, l * 16 + z + 1)
                            if z >= 3:
                                act.wait_ge(s_mWS, l * 16 + z - 2)
                            s.activation(mw[:, z % 3, 0:n], pair(z % 3)[1][:, 0:n], ACT.Exp,
                                         bias=acol[:, 0, j, h:h + 1]).then_inc(s_mW, 1)
                    if h >= 1:
                        for e in range(2):
                            act.wait_ge(s_mev, l * 8 + 2 * (h - 1) + e + 1)
                            for t in (2 * e, 2 * e + 1):
                                last = s.activation(sqj[:], mixt[:, t, T + (h - 1) * MD:T + h * MD], ACT.Square,
                                                    accum_out=ssq[:, t, NH + h - 1:NH + h])
                                act.drain()
                act.wait_ge(s_asq, l * NH + NH)
                s.activation(ssq2[:, :, 0:NH], ssq[:, :, 0:NH], ACT.Sqrt, bias=eps[:, 0:1], scale=1.0 / DH)
                s.activation(ssq2[:, :, NH:], ssq[:, :, NH:], ACT.Sqrt, bias=eps[:, 0:1], scale=1.0 / MD)\
                    .then_inc(s_rt2, 1)
                for c8 in range(KD):
                    act.wait_ge(s_mT, l * KD + c8 + 1)
                    s.activation(h_hi[:, c8, :], bank[c8 % 4], ACT.Copy,
                                 scale=par[:, MG + c8:MG + c8 + 1]).then_inc(s_mhi, 1)
                for u in (16, 17, 18):
                    high(l, u)
                last_squares(KD + 2 * KD * l, 2 * l + 1)
                norm_root(2 * l + 1)
                high(l, 19)
                norm_high(2 * KD * l + KD, 24)

                def hidden_step(l, f, i, idx):
                    unit_used(act, l, i * BODY + (U_UP + f))
                    a_ps = pair(f % 3)[0]
                    s.activation(fy[:, f % 2, :], a_ps, ACT.Identity,
                                 bias=par[:, bass.ds(idx + FB, 1)],
                                 scale=par[:, bass.ds(idx + FW + 2 * KF, 1)]).then_inc(s_y1, 1)
                    act.wait_ge(s_y2, l * KF + i * BODY + (f + 1))
                    s.activation(fy[:, f % 2, :], fy[:, f % 2, :], ACT.Silu).then_inc(s_z, 1)
                    act.wait_ge(s_fv, l * KF + i * BODY + (f + 1 + CREDIT))
                    s.activation(hid_hi[:, bass.ds(idx, 1), :], ft[:, f % 2:f % 2 + 1, :], ACT.Copy)\
                        .then_inc(s_fhi, 1)

                with act.Fori(0, LOOPED // BODY) as i:
                    for f in range(BODY):
                        high(l, U_UP + 2 + f, i)
                        hidden_step(l, f, i, i * BODY + f)
                for f in range(LOOPED, KF):
                    high(l, U_UP + 2 + f, n=width(U_UP + 2 + f))
                    hidden_step(l, f, 0, f)
                for u in range(U_DOWN + 2, UNITS):
                    high(l, u, n=width(u))
                last_squares(2 * KD + 2 * KD * l, 2 * l + 2, l * (AUNITS // 2) + (AUNITS + EARLY) // 2)
            norm_root(2 * L)
            for c8 in range(KD):
                act.wait_ge(s_yT, c8 + 1)
                s.activation(otok[:, :, c8 * P:(c8 + 1) * P],
                             bank[c8 % 4].rearrange("p (t n) -> p t n", t=TT), ACT.Copy).then_inc(s_yev, 1)

        @block.vector
        def _(dve):
            v = nc.vector

            PI = 3.1415925
            C1, C2 = 6.28125, 0.0019350051879882812
            C3 = float(2 * np.pi - C1 - C2)
            inv = (np.float32(500000.0) ** (-np.arange(0, 2 * HALF, 2, dtype=np.float32) / np.float32(2 * HALF)))
            for i in range(HALF):
                v.memset(invf[:, i:i + 1], float(inv[i]))
            dve.wait_ge(s_pos, 32)
            v.tensor_copy(posf[:], pos_i[:])
            dve.drain().then_inc(s_fv, CREDIT)
            v.tensor_tensor(ang[:], posf[:].unsqueeze(2).broadcast_to([P, TT, HALF]),
                            invf[:].unsqueeze(1).broadcast_to([P, TT, HALF]), ALU.mult)
            dve.drain()
            MAGIC = 12582912.0
            v.tensor_scalar(angn[:], ang[:], float(1 / (2 * np.pi)), MAGIC, ALU.mult, ALU.add)
            dve.drain()
            v.tensor_scalar(angn[:], angn[:], MAGIC, None, ALU.subtract)
            for step in (C1, C2, C3):
                dve.drain()
                v.scalar_tensor_tensor(out=ang[:], in0=angn[:], scalar=-step, in1=ang[:], op0=ALU.mult, op1=ALU.add)
            dve.drain()
            v.tensor_scalar(angn[:], ang[:], float(np.pi / 2), None, ALU.add)
            v.tensor_scalar(ang[:], ang[:], PI, -PI, ALU.min, ALU.max)
            dve.drain().then_inc(s_ang, 1)
            v.tensor_scalar(over[:], angn[:], PI, -float(2 * np.pi), ALU.is_gt, ALU.mult)
            dve.drain()
            v.tensor_tensor(angn[:], angn[:], over[:], ALU.add)
            dve.drain()
            v.tensor_scalar(angn[:], angn[:], PI, -PI, ALU.min, ALU.max)
            dve.drain().then_inc(s_ang, 1)

            dve.wait_ge(s_prT, 1)
            for i in range(4):
                last = v.tensor_copy(par_all[:, i, 0:tile_rows[i]], bank[7][:, i * P:i * P + tile_rows[i]])
            last.then_inc(s_pall, 1)

            def norm(l, n, chunks, which):
                dve.wait_ge(s_rt, n + 1)
                v.reciprocal(rstd[:], rstd[:])
                dve.drain()
                shift = (0, 24)[which]
                for c8 in range(KD + 1):
                    if c8 < KD:
                        if c8 >= 3:
                            dve.wait_ge(s_hlo, chunks + c8 - 2)
                        v.scalar_tensor_tensor(out=hm[:, c8 % 3, :], in0=xT[:, c8, :],
                                               scalar=am[:, which, c8:c8 + 1], in1=rstd[:],
                                               op0=ALU.mult, op1=ALU.mult).then_inc(s_hm, 1)
                    if c8 >= 1:
                        b = c8 - 1
                        dve.wait_ge(s_hhi, chunks + b + 1)
                        v.scalar_tensor_tensor(out=h_lo[:, b, :], in0=hm[:, b % 3, :],
                                               scalar=mod[:, shift + b:shift + b + 1],
                                               in1=h_hi[:, b, :].bitcast(F32),
                                               op0=ALU.add, op1=ALU.subtract).then_inc(s_hlo, 1)

            def x_update(l, gate, ada=None):
                for q in range(4):
                    for i in (4, 5) if q == 0 else (5 + q,) if q < 3 else ():
                        if ada is not None:
                            ada(l, AUNITS + i)
                    unit_used(dve, l, U_OUT + q if gate == 16 else U_DOWN + 3 * q + 2)
                    for e in range(2):
                        c8 = 2 * q + e
                        ps = (pair((q + 2) % 3) if gate == 16 else pair((q + 1) % 3))[e]
                        v.scalar_tensor_tensor(out=xT[:, c8, :], in0=ps, scalar=mod[:, gate + c8:gate + c8 + 1],
                                               in1=xT[:, c8, :], op0=ALU.mult, op1=ALU.add).then_inc(s_xu, 1)

            def multiply(j, src, sums):
                cols, dst = src.rearrange("p (k n) -> p k n", k=KD // 2), sums[:, j // 2 % 2, :]
                for kk in range(KD // 2):
                    k = j % 2 * (KD // 2) + kk
                    if k == 0:
                        last = v.tensor_scalar(dst, cols[:, kk, :], cact[:, k:k + 1], None, ALU.mult)
                    else:
                        last = v.scalar_tensor_tensor(out=dst, in0=cols[:, kk, :], scalar=cact[:, k:k + 1], in1=dst,
                                                      op0=ALU.mult, op1=ALU.add)
                    if kk == KD // 2 - 1:
                        last.then_inc(s_aused, 1)
                    if k < KD - 1:
                        dve.drain()
                    else:
                        dve.drain().then_inc(s_asum, 1)

            def ada(l, j):
                if j % 2 == 0:
                    dve.drain()
                    dve.wait_ge(s_ag, l * (AUNITS // 2) + j // 2 - 1)
                if j < AUNITS:
                    dve.wait_ge(s_a[j % ARING], l * (16 * (AUNITS - EARLY) // ARING) + 16 * ((j - EARLY) // ARING + 1))
                    multiply(j, a_slot[j % ARING], asum)
                else:
                    dve.wait_ge(s_e[j - AUNITS], 16 * l + 32)
                    multiply(j, a_slot[1], asum)

            dve.wait_ge(s_cact, 1)
            for j in range(EARLY):
                if j % 2 == 0 and j >= 4:
                    dve.wait_ge(s_ag, j // 2 - 1)
                dve.wait_ge(s_e[j], 16)
                multiply(j, a_early[j], asum0)
            with dve.Fori(0, L) as l:
                flat = par_all[:].rearrange("p a b -> p (a b)")
                at = 0
                for name, n in PARS:
                    v.tensor_copy(par[:, at:at + n], flat[:, bass.ds(l * step_of[name] + where[name], n)])
                    at += n
                dve.drain()
                dve.wait_ge(s_ag, l * (AUNITS // 2) + EARLY // 2)
                v.tensor_tensor(mod[:, 0:16], bank[6][:, 0:16], par[:, AB:AB + 16], ALU.add)
                dve.drain()
                v.scalar_tensor_tensor(out=am[:, 0, :], in0=mod[:, 8:16], scalar=1.0, in1=par[:, N1:N1 + KD],
                                       op0=ALU.add, op1=ALU.mult)
                dve.drain().then_inc(s_mod, 1)
                norm(l, 2 * l, 2 * KD * l, 0)

                def doubled(j, t, src):
                    return v.tensor_copy(tok[:, j:j + NG, t, :].rearrange("p g (s d) -> p g s d", s=2),
                                         src.rearrange("p (g s d) -> p g s d", g=NG, s=1)
                                         .broadcast_to([P, NG, 2, DH]))

                for j in range(EARLY, 16):
                    ada(l, j)
                for i in range(TT, 3 * TT):
                    group, t = i // TT, i % TT
                    if i == 2 * TT:
                        for j in range(16, 20):
                            ada(l, j)
                    projected(dve, l, group, t)
                    ps = bank[i % PB]
                    if group == 1:
                        doubled(J_X, t, ps[:, 0:128])
                        doubled(J_X + 2, t, ps[:, 128:256])
                        doubled(J_K, t, ps[:, 256:384])
                        last = v.tensor_copy(v_sw[:, t, 0, :, 0:DH],
                                             ps[:, 384:512].rearrange("p (g d) -> p g d", g=NG))
                    else:
                        doubled(J_K + 2, t, ps[:, 0:128])
                        v.tensor_copy(v_sw[:, t, 1, :, 0:DH], ps[:, 128:256].rearrange("p (g d) -> p g d", g=NG))
                        last = v.tensor_copy(gif[:, t, :], ps[:, 256:288])
                    last.then_inc(s_pev, 1)
                dve.drain()
                dve.wait_ge(s_sin, 1)
                dve.wait_ge(s_qev, l * TT + TT)
                heads = tok[:, 0:14].rearrange("p j t (s d) -> p j (t s) d", d=DH)
                x1, x2 = heads[:, :, :, 0:HALF], heads[:, :, :, HALF:2 * HALF]
                cosb, sinb = (m[:].rearrange("p t s d -> p (t s) d").unsqueeze(1)
                              .broadcast_to([P, 14, 2 * TT, HALF]) for m in (cos, sin))
                v.tensor_tensor(rt[:, 0], x1, sinb, ALU.mult)
                v.tensor_tensor(rt[:, 1], x2, sinb, ALU.mult)
                dve.drain()
                v.tensor_tensor(x1, x1, cosb, ALU.mult)
                v.tensor_tensor(x2, x2, cosb, ALU.mult)
                dve.drain()
                v.tensor_tensor(x1, x1, rt[:, 1], ALU.subtract)
                v.tensor_tensor(x2, x2, rt[:, 0], ALU.add)
                dve.drain().then_inc(s_rope, 1)
                for j in range(20, AUNITS):
                    ada(l, j)
                for t in range(TT):
                    projected(dve, l, 3, t)
                    v.tensor_copy(v_m[:, t, :, 0:MD], bank[t].rearrange("p (h d) -> p h d", h=MH))\
                        .then_inc(s_mvev, 1)
                dve.wait_ge(s_ag, l * (AUNITS // 2) + AUNITS // 2)
                v.tensor_tensor(mod[:, 16:48], bank[6][:, 16:48], par[:, AB + 16:AB + 48], ALU.add)
                v.memset(hidk[:], 0.0)
                v.memset(hidv[:], 0.0)
                v.memset(vcmp[:], 0.0)
                dve.drain()
                v.scalar_tensor_tensor(out=am[:, 1, :], in0=mod[:, 32:40], scalar=1.0, in1=par[:, N2:N2 + KD],
                                       op0=ALU.add, op1=ALU.mult)
                dve.drain().then_inc(s_mod, 1)
                dve.wait_ge(s_ift, l + 1)
                v.tensor_scalar(ib[:], bank[5][0:MH, :], gate_b[:, bass.ds(l, 1), 0:1].rearrange("h a b -> h (a b)"),
                                None, ALU.add)
                v.tensor_scalar(fb[:], bank[7][0:MH, :], gate_b[:, bass.ds(l, 1), 1:2].rearrange("h a b -> h (a b)"),
                                None, ALU.add)
                dve.drain()
                v.scalar_tensor_tensor(out=fe[:], in0=fb[:], scalar=-1.0, in1=fb[:], op0=ALU.mult, op1=ALU.max)
                dve.drain().then_inc(s_ib, 1)
                for n in range(4):
                    dve.wait_ge(s_tp, l * NJ + n + 1)
                    for half in range(2):
                        p0, p1 = half * DH, (half + 1) * DH
                        src = bank[T_BANK[n]][p0:p1, :].rearrange("p (n c s) -> p n c s", s=2, c=CS // 2)
                        for ab in range(2):
                            col = CP + n // 2 * CS + ab * (CS // 2)
                            last = v.tensor_tensor(
                                xab[p0:p1, n, ab, :].rearrange("p (n c) -> p n c", c=CS // 2), src[:, :, :, half],
                                par[p0:p1, col:col + CS // 2].unsqueeze(1).broadcast_to([DH, NCP, CS // 2]),
                                ALU.add)
                    last.then_inc(s_tev, 1)
                for n in range(4):
                    dve.wait_ge(s_thi, l * (NJ - 4) + n + 1)
                    v.tensor_tensor(qk[:, J_X + n, :], bank[T_BANK[n]], qk[:, J_K + n, :].bitcast(F32),
                                    ALU.subtract).then_inc(s_tev, 1)
                for h in range(NH):
                    dve.wait_ge(s_thi, l * (NJ - 4) + 4 + h + 1)
                    low = qk[DH:P, h, :]
                    v.scalar_tensor_tensor(out=low, in0=bank[T_BANK[h % 4]][DH:P, :], scalar=DH ** -0.5,
                                           in1=low.bitcast(F32), op0=ALU.mult, op1=ALU.subtract).then_inc(s_tev, 1)

                def conv_rest(c0):
                    for k in (2, 1, 0):
                        sh = MC - 1 - k
                        for c8 in (c0, c0 + 1):
                            if k == 2:
                                dve.wait_ge(s_cv1, l * 2 * MH + c8 + 1)
                            last = v.scalar_tensor_tensor(
                                out=mqk[:, c8, sh:T], in0=bank[c8 % 4][:, 0:T - sh],
                                scalar=par[:, MW + k * KD + c8:MW + k * KD + c8 + 1], in1=mqk[:, c8, sh:T],
                                op0=ALU.mult, op1=ALU.add)
                            if k == 0:
                                last.then_inc(s_cv2, 1)
                        if k:
                            dve.drain()

                conv_rest(0)
                dve.wait_ge(s_cmp, l + 1)
                v.tensor_copy(kcmp[:].rearrange("p g n -> p (g n)"), bank[5][:, 0:NG * NCP])
                for r in range(R):
                    last = v.tensor_copy(vcmp[r * NCP:(r + 1) * NCP, :, r, :],
                                         bank[5][r * NCP:(r + 1) * NCP, 64:64 + NG * DH]
                                         .rearrange("p (g d) -> p g d", g=NG))
                last.then_inc(s_cmpev, 1)
                for t in range(TT):
                    dve.wait_ge(s_cS, l * TT + t + 1)
                    v.tensor_tensor(csc[:, t], bank[4 + t][:, 0:NH * NCP].rearrange("p (h n) -> p h n", h=NH),
                                    cmask[:, t, :].unsqueeze(1).broadcast_to([P, NH, NCP]), ALU.add)
                dve.drain()
                v.tensor_reduce(out=cmx[:], in_=csc[:], axis=AX.X, op=ALU.max)
                dve.drain()
                v.tensor_scalar(cmx[:], cmx[:], NEG / 10, None, ALU.max)
                dve.drain()
                for t in range(TT):
                    v.tensor_tensor(csc[:, t], csc[:, t], cmx[:, t, :].unsqueeze(2).broadcast_to([P, NH, NCP]),
                                    ALU.subtract).then_inc(s_csub, 1)
                conv_rest(2)
                dve.wait_ge(s_ln, l + 1)
                one = ones[0:MH, 0:1].broadcast_to([MH, T])
                v.scalar_tensor_tensor(out=fb[:], in0=fb[:], scalar=0.0, in1=fe[:], op0=ALU.min, op1=ALU.subtract)
                dve.drain()
                v.tensor_tensor_scan(brow[:], one, fb[:], 0.0, ALU.mult, ALU.add)
                dve.drain()
                v.tensor_tensor(ib[:], ib[:], brow[:], ALU.subtract)
                dve.drain()
                v.tensor_tensor_scan(arow[:], one, ib[:], -3.0e38, ALU.mult, ALU.max)
                dve.drain()
                v.tensor_tensor(mrow[:], brow[:], arow[:], ALU.add)
                dve.drain()
                v.tensor_scalar(arow[:], arow[:], -1.0, None, ALU.mult)
                dve.drain().then_inc(s_rows, 1)
                dve.wait_ge(s_cexp, l * TT + TT)
                v.tensor_reduce(out=csum[:], in_=csc[:], axis=AX.X, op=ALU.add)
                dve.drain()
                v.tensor_scalar(csum[:], csum[:], TINY, None, ALU.max)
                dve.drain()
                v.reciprocal(csum[:], csum[:])
                dve.drain()
                dve.wait_ge(s_gat, l + 1)
                gates = gat[:].rearrange("p t (h b) -> p t h b", b=3)
                v.tensor_tensor(csum[:], csum[:], gates[:, :, :, 0], ALU.mult)
                dve.drain()
                for i in range(2):
                    dve.wait_ge(s_cT, l * TT + 2 * i + 2)
                    v.tensor_copy(pT[:, 2 * i:2 * i + 2].rearrange("p t g q -> p (t g q)"), bank[4 + i])\
                        .then_inc(s_cTev, 1)
                for t in range(TT):
                    dve.wait_ge(s_cO, l * TT + t + 1)
                    v.tensor_tensor(mixt[:, t, 0:T].rearrange("p (h d) -> p h d", h=NH),
                                    bank[C_BANK[t]].rearrange("p (h d) -> p h d", h=NH),
                                    csum[:, t, :].unsqueeze(2).broadcast_to([P, NH, DH]), ALU.mult)\
                        .then_inc(s_cev, 1)
                conv_rest(4)

                def maxima(w):
                    h, t = w // TT, w % TT
                    b, n = score_bank(w), (t + 1) * P
                    dve.wait_ge(s_S, l * NW + w + 1)
                    v.tensor_reduce(out=nmx[:, h // R, t, h % R, :], in_=psum[:, b:b + 2, 0:n],
                                    axis=AX.X, op=ALU.max, negate=True).then_inc(s_nm, 1)

                for w in range(3):
                    maxima(w)
                conv_rest(6)
                for w in range(3, NW // 2):
                    maxima(w)

                def gated(h):
                    dve.wait_ge(s_oT, l * NH + h + 1)
                    ps = psum[:, 6:8, 0:TT * (DH + 1)].rearrange("p b (t d) -> p b t d", t=TT)
                    v.reciprocal(coef[:], ps[:, :, :, DH])
                    dve.drain()
                    v.tensor_tensor(coef[:], coef[:], gates[:, :, h, 1:3].rearrange("p t b -> p b t"), ALU.mult)
                    dve.drain()
                    if h >= 2:
                        dve.wait_ge(s_comb, l * NH + h - 1)
                    v.tensor_tensor(t12[:, h % 2], ps[:, :, :, 0:DH],
                                    coef[:].unsqueeze(3).broadcast_to([P, 2, TT, DH]), ALU.mult)\
                        .then_inc(s_gated, 1)

                def squares(h):
                    dve.wait_ge(s_comb, l * NH + h + 1)
                    v.tensor_reduce(out=ssq[:, :, h], in_=sqb[:], axis=AX.X, op=ALU.add).then_inc(s_asq, 1)

                for z in range(NW):
                    for w in beside(z):
                        maxima(w)
                    if z % TT == 0 and z:
                        gated(z // TT - 1)
                        if z > TT:
                            squares(z // TT - 2)
                gated(NH - 1)
                squares(NH - 2)
                squares(NH - 1)

                def head_out(h):
                    for e in range(2):
                        dve.wait_ge(s_mO, l * 8 + 2 * h + e + 1)
                        ps = bank[6 + e][:, 0:2 * (MD + 1)].rearrange("p (t d) -> p t d", t=2)
                        v.scalar_tensor_tensor(out=den[:, e, :], in0=ps[:, :, MD], scalar=-1.0,
                                               in1=acol[:, 1, 2 * e:2 * e + 2, h], op0=ALU.mult, op1=ALU.max)
                        dve.drain()
                        v.tensor_tensor(den[:, e, :], ps[:, :, MD], den[:, e, :], ALU.max)
                        dve.drain()
                        v.reciprocal(den[:, e, :], den[:, e, :])
                        dve.drain()
                        for i in range(2):
                            t = 2 * e + i
                            last = v.scalar_tensor_tensor(
                                out=mixt[:, t, T + h * MD:T + (h + 1) * MD], in0=ps[:, i, 0:MD],
                                scalar=den[:, e, i:i + 1], in1=mixt[:, t, T + h * MD:T + (h + 1) * MD],
                                op0=ALU.mult, op1=ALU.mult)
                        last.then_inc(s_mev, 1)

                for h in range(MH):
                    for j in range(TT):
                        z, n = h * TT + j, (TT - j) * P
                        dve.wait_ge(s_mW, l * 16 + z + 1)
                        if h >= 2:
                            dve.wait_ge(s_mO, l * 8 + 2 * (h - 1))
                        v.scalar_tensor_tensor(out=mws[:, h % 2, W_OFF[j]:W_OFF[j] + n],
                                               in0=pair(z % 3)[0][:, 0:n], scalar=MSCALE, in1=mw[:, z % 3, 0:n],
                                               op0=ALU.mult, op1=ALU.mult).then_inc(s_mWS, 1)
                        if j == 1 and h >= 1:
                            head_out(h - 1)
                head_out(MH - 1)
                dve.wait_ge(s_rt2, l + 1)
                v.reciprocal(ssq2[:], ssq2[:])
                dve.drain().then_inc(s_rh, 1)
                for t in range(TT):
                    o3 = mixt[:, t, 0:T].rearrange("p (h d) -> p h d", h=NH)
                    v.tensor_tensor(o3, o3, ssq2[:, t, 0:NH].unsqueeze(2).broadcast_to([P, NH, DH]), ALU.mult)
                dve.drain().then_inc(s_mixa, 1)
                for c8 in range(KD):
                    dve.wait_ge(s_mhi, l * KD + c8 + 1)
                    v.scalar_tensor_tensor(out=h_lo[:, c8, :], in0=bank[c8 % 4],
                                           scalar=par[:, MG + c8:MG + c8 + 1], in1=h_hi[:, c8, :].bitcast(F32),
                                           op0=ALU.mult, op1=ALU.subtract).then_inc(s_mlo, 1)
                x_update(l, 16)
                norm(l, 2 * l + 1, 2 * KD * l + KD, 1)

                def hidden_step(l, f, i, idx):
                    a_ps, v_ps = pair(f % 3)
                    y = fy[:, f % 2, :]
                    dve.wait_ge(s_y1, l * KF + i * BODY + (f + 1))
                    v.scalar_tensor_tensor(out=y[:, 1:T], in0=a_ps[:, 0:T - 1],
                                           scalar=par[:, bass.ds(idx + FW + KF, 1)], in1=y[:, 1:T],
                                           op0=ALU.mult, op1=ALU.add)
                    dve.drain()
                    v.scalar_tensor_tensor(out=y[:, 2:T], in0=a_ps[:, 0:T - 2],
                                           scalar=par[:, bass.ds(idx + FW, 1)], in1=y[:, 2:T],
                                           op0=ALU.mult, op1=ALU.add).then_inc(s_y2, 1)
                    dve.wait_ge(s_z, l * KF + i * BODY + (f + 1))
                    dve.wait_ge(s_flo, l * KF + i * BODY + (f - 1 + CREDIT))
                    v.tensor_tensor(ft[:, f % 2, :], v_ps, y, ALU.mult).then_inc(s_fv, 1)

                with dve.Fori(0, LOOPED // BODY) as i:
                    for f in range(BODY):
                        hidden_step(l, f, i, i * BODY + f)
                for f in range(LOOPED, KF):
                    hidden_step(l, f, 0, f)
                    ada(l, AUNITS + f - LOOPED)
                x_update(l, 40, ada)
            dve.wait_ge(s_rt, 2 * L + 1)
            v.reciprocal(rstd[:], rstd[:])
            dve.drain()
            for c8 in range(KD):
                if c8 >= 3:
                    dve.wait_ge(s_yT, c8 - 2)
                v.scalar_tensor_tensor(out=hm[:, c8 % 3, :], in0=xT[:, c8, :],
                                       scalar=par_all[:, FROW // P, FROW % P + c8:FROW % P + c8 + 1], in1=rstd[:],
                                       op0=ALU.mult, op1=ALU.mult).then_inc(s_fin, 1)

        @block.tensor
        def _(pe):
            m = nc.tensor.matmul

            pe.drain().then_inc(s_used, CREDIT)
            pe.wait_ge(s_const, 1)
            pe.wait_ge(s_par, 16 * len(loads))
            for i in range(4):
                n = tile_rows[i]
                last = nc.tensor.transpose(bank[7][:, i * P:i * P + n], prow[0:n, i, :], ident[0:n, 0:n])
            last.then_inc(s_prT, 1)
            pe.wait_ge(s_x, 16 * TT)
            for c8 in range(KD):
                if c8 >= 6:
                    pe.wait_ge(s_xu, c8 - 5)
                for t in range(TT):
                    last = nc.tensor.transpose(bank[c8 % 6][:, t * P:(t + 1) * P],
                                               xtok[:, t, c8 * P:(c8 + 1) * P], ident[:])
                last.then_inc(s_xT, 1)

            def ada_sums(l, g, src=asum):
                pe.wait_ge(s_asum, l * (AUNITS // 2) + g + 1)
                for i in range(4):
                    at = 4 * (g % (AUNITS // 2)) + i
                    last = m(bank[6][:, at:at + 1], src[:, g % 2, i * P:(i + 1) * P], ones[:, 0:1],
                             start=True, stop=True)
                last.then_inc(s_ag, 1)

            def sum_squares(n):
                pe.wait_ge(s_sqa, n + 1)
                m(bank[7], ones[:], hm[:, 2, :], start=True, stop=False)
                for i in range(2):
                    pe.wait_ge(s_sql, 2 * n + 1 + i)
                    last = m(bank[7], ones[:], hm[:, i, :], start=False, stop=(i == 1))
                last.then_inc(s_ss, 1)

            def three(ps, l_hi, l_lo, r_hi, r_lo, first, last):
                m(ps, l_hi, r_hi, start=first, stop=False)
                m(ps, l_hi, r_lo, start=False, stop=False)
                return m(ps, l_lo, r_hi, start=False, stop=last)

            def tile_free(l, group, t):
                if group < 3:
                    b = group * TT + t - PB
                    if b >= TT:
                        pe.wait_ge(s_pev, l * 2 * TT + b - TT + 1)
                    elif b >= 0:
                        pe.wait_ge(s_qev, l * TT + b + 1)
                elif group == 3:
                    last = max(i for i in range(3 * TT) if i % PB == t)
                    pe.wait_ge(s_pev, l * 2 * TT + last - TT + 1)
                else:
                    pe.wait_ge(s_mvev, l * TT + t + 1)

            def token_unit(l, u, n, between=None):
                group = u // 2
                pe.wait_ge(s_lo, l * UNITS + u + 1)
                for kk in range(4):
                    k = (u % 2) * 4 + kk
                    if u < 2:
                        pe.wait_ge(s_hlo, l * 2 * KD + k + 1)
                    for t in range(TT):
                        if k == 0:
                            tile_free(l, group, t)
                        tile = slice(t * P, (t + 1) * P)
                        b = (group * TT + t) % PB if group < 3 else t
                        last = three(bank[b][:, 0:n], h_hi[:, k, tile], h_lo[:, k, tile],
                                     w_hi[:, u % HI, kk * n:(kk + 1) * n], w_lo[:, u % RAW, kk * n:(kk + 1) * n],
                                     k == 0, k == KD - 1)
                        if k == KD - 1 and t < TT - 1:
                            last.then_inc(s_proj, 1)
                    if kk == 3:
                        last.then_inc(s_used, 1)
                    if between is not None:
                        between(kk)

            def column_unit(u, banks, nk, rhs, first, last, ready=None, between=None):
                for kk in range(nk):
                    if ready is not None:
                        ready(kk)
                    for e in range(2):
                        at = kk * 256 + e * P
                        hi, lo = rhs(kk)
                        ins = three(banks[e], w_hi[:, u % HI, at:at + P], w_lo[:, u % RAW, at:at + P], hi, lo,
                                    first and kk == 0, last and kk == nk - 1)
                    if kk == nk - 1:
                        ins.then_inc(s_used, 1)
                    if between is not None:
                        between(kk)

            def h_of(k):
                return h_hi[:, k, :], h_lo[:, k, :]

            sum_squares(0)
            for g in range(EARLY // 2):
                ada_sums(0, g, asum0)
            with pe.Fori(0, L) as l:
                ada_at_step = {(1, 3): 4, (2, 1): 5, (2, 3): 6, (3, 1): 7, (5, 1): 8, (5, 3): 9, (7, 1): 10,
                               (7, 3): 11}

                def beside_ada(u):
                    def between(kk):
                        if (u, kk) in ada_at_step:
                            ada_sums(l, ada_at_step[u, kk])
                    return between

                for u in range(U_MV):
                    token_unit(l, u, 512 if u < 4 else 288, beside_ada(u))

                def transpose_chunk(n):
                    j = (J_X + n, J_K + n - 4, n - 8, n - 8)[n // 4]
                    if n == 0:
                        pe.wait_ge(s_rope, l + 1)
                    elif n in (1, 2):
                        pe.wait_ge(s_ib, l + 1)
                    elif n == 3:
                        pe.wait_ge(s_mod, l * 2 + 2)
                    else:
                        pe.wait_ge(s_tev, l * NJ + n - 3)
                    for t in range(TT):
                        last = nc.tensor.transpose(bank[T_BANK[n % 4]][:, t * P:(t + 1) * P], tok[:, j, t, :],
                                                   ident[:])
                    last.then_inc(s_tp, 1)

                def gate_rows():
                    pe.wait_ge(s_pev, l * 2 * TT + 2 * TT)
                    for i, b in enumerate((5, 7)):
                        for t in range(TT):
                            last = nc.tensor.transpose(bank[b][0:MH, t * P:(t + 1) * P],
                                                       gif[:, t, NGATE + i * MH:NGATE + (i + 1) * MH], ident[:])
                    last.then_inc(s_ift, 1)

                def compress(n):
                    for c16 in range(CB // 2):
                        ab, cc = c16 // (CS // 2), c16 % (CS // 2)
                        x3 = xab[:, n, ab, :].rearrange("p (n c) -> p n c", c=CS // 2)
                        last = m(bank[4][0:DH, n * NCP:n * NCP + NC], w1[:, n // 2, c16, :],
                                 x3[:, ab:ab + NC, cc], start=(c16 == 0), stop=(c16 == CB // 2 - 1))
                    if n == 3:
                        last.then_inc(s_hid, 1)

                def compressed():
                    pe.wait_ge(s_hids, l + 1)
                    for g in range(NG):
                        m(bank[5][:, 64 + g * DH:64 + (g + 1) * DH], hidv[:, g].rearrange("p r n -> p (r n)"),
                          w2[:, 1, :], start=True, stop=True)
                    for g in range(NG):
                        for half in range(2):
                            last = m(bank[5][half * DH:(half + 1) * DH, g * NCP:(g + 1) * NCP], w2[:, 0, :],
                                     hidk[:, g, :], start=True, stop=True)
                    last.then_inc(s_cmp, 1)

                def compressed_scores(t):
                    if t == 0:
                        pe.wait_ge(s_cmpev, l + 1)
                    for h in range(NH):
                        last = m(bank[4 + t][:, h * NCP:(h + 1) * NCP], qk[:, h, t * P:(t + 1) * P].bitcast(F32),
                                 kcmp[:, h // R, :], start=True, stop=True)
                    last.then_inc(s_cS, 1)

                def compressed_transposes(t):
                    pe.wait_ge(s_cexp, l * TT + TT)
                    for g in range(NG):
                        at = (t % 2) * 256 + g * P
                        last = nc.tensor.transpose(bank[4 + t // 2][:, at:at + P],
                                                   csc[:, t, g * R:(g + 1) * R, :].rearrange("p r n -> p (r n)"),
                                                   ident[:])
                    last.then_inc(s_cT, 1)

                def compressed_outputs(t):
                    pe.wait_ge(s_cTev, l * 2 + (2 if t >= 2 else t // 2 + 1))
                    for g in range(NG):
                        last = m(bank[C_BANK[t]][:, g * R * DH:(g + 1) * R * DH], pT[:, t, g, :],
                                 vcmp[:, g].rearrange("p r d -> p (r d)"), start=True, stop=True)
                    last.then_inc(s_cO, 1)

                def gate_columns():
                    pe.wait_ge(s_rows, l + 1)
                    pe.wait_ge(s_cev, l * TT + 1)
                    for i, rows in enumerate((ib, mrow)):
                        for t in range(TT):
                            last = m(bank[6][:, i * 16 + t * MH:i * 16 + (t + 1) * MH],
                                     rows[:, t * P:(t + 1) * P], ident[0:MH, 0:MH], start=True, stop=True)
                    last.then_inc(s_col, 1)

                def scores(w, after_head=None):
                    h, t = w // TT, w % TT
                    b, n = score_bank(w), (t + 1) * P
                    if w == 0:
                        pe.wait_ge(s_cev, l * TT + TT)
                        pe.wait_ge(s_acol, l + 1)
                    elif w == NW // 2:
                        pe.wait_ge(s_nrow, l * 2 + 1)
                    elif after_head is not None:
                        pe.wait_ge(s_gated, l * NH + after_head + 1)
                    elif w > NW // 2:
                        pe.wait_ge(s_nm, l * NW + w)
                    elif w >= 2:
                        pe.wait_ge(s_nm, l * NW + w - 1)
                    for br in range(2):
                        ps = bank[b + br]
                        m(ps[:, 0:n], qk[:, h, t * P:(t + 1) * P], qk[:, J_K + 2 * br + h // R, 0:n],
                          start=True, stop=False)
                        last = m(ps[:, t * P:n], identb[:], tri[:], start=False, stop=True)
                    last.then_inc(s_S, 1)

                def max_rows(g):
                    pe.wait_ge(s_nm, l * NW + (g + 1) * NW // 2)
                    for t in range(TT):
                        last = nc.tensor.transpose(bank[6][0:8, t * P:(t + 1) * P],
                                                   nmx[:, g, t].rearrange("p h b -> p (h b)"), ident[:])
                    last.then_inc(s_nr, 1)

                def beside_mo1(kk):
                    if kk == 0:
                        gate_rows()
                    for n in (2 * kk, 2 * kk + 1):
                        transpose_chunk(n)

                def beside_mo2(kk):
                    for n in (8 + 2 * kk, 9 + 2 * kk):
                        transpose_chunk(n)

                def beside_mqk(i, kk):
                    if i == 0:
                        if kk == 0:
                            pe.wait_ge(s_cw, l * 48 + 48)
                            pe.wait_ge(s_tev, l * NJ + NJ)
                        if kk % 2 == 0:
                            compress(kk // 2)
                    elif i == 1:
                        if kk == 2:
                            compressed()
                        if kk in (5, 6):
                            compressed_scores(2 * (kk - 5))
                            compressed_scores(2 * (kk - 5) + 1)
                    elif i == 2:
                        if kk in (5, 6):
                            compressed_transposes(2 * (kk - 5))
                            compressed_transposes(2 * (kk - 5) + 1)
                    else:
                        if kk in (0, 1):
                            compressed_outputs(2 * kk)
                            compressed_outputs(2 * kk + 1)
                        if kk == 3:
                            gate_columns()
                        if kk >= 5:
                            scores(kk - 5)

                token_unit(l, U_MV, 512)
                token_unit(l, U_MV + 1, 512, beside_ada(U_MV + 1))
                token_unit(l, U_MO, 512, beside_mo1)
                token_unit(l, U_MO + 1, 512, beside_mo2)
                for i in range(4):
                    u = U_MQK + i
                    pe.wait_ge(s_lo, l * UNITS + u + 1)
                    if i < 2:
                        pe.wait_ge(s_moev, l * TT + 2 * i + 2)
                    else:
                        pe.wait_ge(s_cv2, l * 2 * MH + 2 * i - 2)
                    column_unit(u, (bank[2 * i % 4], bank[(2 * i + 1) % 4]), KD, h_of, True, True,
                                between=lambda kk: beside_mqk(i, kk))
                for w in range(3, NW // 2):
                    scores(w)
                max_rows(0)

                def key_scores(z):
                    h, kb = z // TT, z % TT
                    n, g = (TT - kb) * P, h // R
                    keys = slice(kb * P, (kb + 1) * P)
                    if z == 0:
                        pe.wait_ge(s_cv2, l * 2 * MH + 2 * MH)
                    if z % (NW // 2) == 0:
                        pe.wait_ge(s_nrow, l * 2 + g + 1)
                    if z >= 2:
                        pe.wait_ge(s_exp, l * NW + z - 1)
                    for br in range(2):
                        ps = bank[2 * (z % 2) + br]
                        q = qk[:, h, kb * P:T]
                        m(ps[:, 0:n], qk[:, J_K + 2 * br + g, keys], q, start=True, stop=False)
                        m(ps[:, 0:n], qk[:, J_X + 2 * br + g, keys], q, start=False, stop=False)
                        row = 2 * (h % R) + br
                        m(ps[:, 0:n], identr[:, row:row + 1].broadcast_to([8, P]), nrow[:, g, kb * P:T],
                          start=False, stop=False)
                        last = m(ps[:, 0:P], identb[:], triT[:], start=False, stop=True)
                    last.then_inc(s_ST, 1)

                def values(z):
                    h, kb = z // TT, z % TT
                    pe.wait_ge(s_exp, l * NW + z + 1)
                    if kb == 0:
                        if h == 0:
                            pe.wait_ge(s_nm, l * NW + NW // 2)
                        else:
                            pe.wait_ge(s_oev, l * NH + h)
                    for br in range(2):
                        last = m(bank[4 + br][0:DH + 1, kb * P:T], v_sw[:, kb, br, h // R, :],
                                 pt[:, z % 2, br, 0:(TT - kb) * P], start=(kb == 0), stop=(kb == TT - 1),
                                 skip_group_check=True)
                    last.then_inc(s_PV, 1)

                def outputs(h):
                    pe.wait_ge(s_oev, l * NH + h + 1)
                    if h <= 2:
                        pe.wait_ge(s_nm, l * NW + NW // 2 + done_beside(TT * (h + 1)))
                    else:
                        if h == 3:
                            pe.wait_ge(s_nrow, l * 2 + 2)
                        pe.wait_ge(s_gated, l * NH + h)
                    for br in range(2):
                        for t in range(TT):
                            last = nc.tensor.transpose(bank[6 + br][:, t * (DH + 1):(t + 1) * (DH + 1)],
                                                       ot[:, br, t * P:(t + 1) * P], ident[0:DH + 1, 0:DH + 1])
                    last.then_inc(s_oT, 1)

                pe.wait_ge(s_vone, l + 1)
                key_scores(0)
                key_scores(1)
                for z in range(NW):
                    if z + 2 < NW:
                        key_scores(z + 2)
                    for i, w in enumerate(beside(z)):
                        scores(w, z // TT - 1 if i == 0 and z > TT and z % TT == 1 else None)
                    if z == 13:
                        pe.wait_ge(s_gated, l * NH + 3)
                        max_rows(1)
                    values(z)
                    if z % TT == 0 and z:
                        outputs(z // TT - 1)

                def sources(z):
                    h, j = z // TT, z % TT
                    n = (TT - j) * P
                    if z >= 3:
                        pe.wait_ge(s_mWS, l * 16 + z - 2)
                    ps, bc = pair(z % 3)
                    m(ps[:, 0:n], mqk[:, MH + h, j * P:(j + 1) * P], mqk[:, h, j * P:T], start=True, stop=True)
                    m(bc[:, 0:n], ident[0:MH, h:h + 1].broadcast_to([MH, P]), arow[:, j * P:T],
                      start=True, stop=False)
                    m(bc[:, 0:P], identb[:], triT[:], start=False, stop=True).then_inc(s_mS, 1)

                def head_values(h):
                    pe.wait_ge(s_mWS, l * 16 + 4 * h + 4)
                    for t in range(TT):
                        e = t // 2
                        if t % 2 == 0:
                            if h >= 1:
                                pe.wait_ge(s_mev, l * 8 + 2 * (h - 1) + e + 1)
                        for j in range(t + 1):
                            at = W_OFF[j] + (t - j) * P
                            last = m(bank[6 + e][:, (t % 2) * (MD + 1):(t % 2 + 1) * (MD + 1)],
                                     mws[:, h % 2, at:at + P], v_m[:, j, h, :], start=(j == 0), stop=(j == t))
                        if t % 2:
                            last.then_inc(s_mO, 1)

                pe.wait_ge(s_cv3, l * 2 * MH + 2 * MH)
                for z in range(MH * TT):
                    if z == 2:
                        outputs(NH - 1)
                    if z == TT + 1:
                        pe.wait_ge(s_gated, l * NH + NH)
                    sources(z)
                    if z % TT == 1 and z > TT:
                        head_values(z // TT - 1)
                head_values(MH - 1)

                pe.wait_ge(s_mixa, l + 1)
                pe.wait_ge(s_mixm, l + 1)
                for c8 in range(KD):
                    if c8 >= 4:
                        pe.wait_ge(s_mlo, l * KD + c8 - 3)
                    for t in range(TT):
                        last = nc.tensor.transpose(bank[c8 % 4][:, t * P:(t + 1) * P],
                                                   mixt[:, t, c8 * P:(c8 + 1) * P], ident[:])
                    last.then_inc(s_mT, 1)
                for q in range(4):
                    u = U_OUT + q
                    pe.wait_ge(s_lo, l * UNITS + u + 1)
                    if q == 3:
                        pe.wait_ge(s_xu, KD + 2 * KD * l + 2)

                    def mixed(kk):
                        pe.wait_ge(s_mlo, l * KD + kk + 1)

                    column_unit(u, pair((q + 2) % 3), KD, h_of, True, True, mixed if q == 0 else None)
                sum_squares(2 * l + 1)

                def up(l, f, i):
                    pe.wait_ge(s_lo, l * UNITS + i * BODY + (U_UP + f + 1))
                    pe.wait_ge(s_fv, l * KF + i * BODY + (f - 2 + CREDIT))
                    for kk in range(KD):
                        if f == 0:
                            pe.wait_ge(s_hlo, l * 2 * KD + KD + kk + 1)
                        for e in range(2):
                            at = kk * 256 + e * P
                            last = three(pair(f % 3)[e], w_hi[:, f % HI, at:at + P], w_lo[:, f % RAW, at:at + P],
                                         h_hi[:, kk, :], h_lo[:, kk, :], kk == 0, kk == KD - 1)
                    last.then_inc(s_used, 1)

                with pe.Fori(0, LOOPED // BODY) as i:
                    for f in range(BODY):
                        up(l, f, i)
                for f in range(LOOPED, KF):
                    up(l, f, 0)
                    if f == LOOPED + 2:
                        ada_sums(l, AUNITS // 2)
                for d in range(UNITS - U_DOWN):
                    if d in (1, 5, 8):
                        ada_sums(l, AUNITS // 2 + {1: 1, 5: 2, 8: 3}[d])
                    u, q = U_DOWN + d, d // 3
                    k0, k1 = DOWN_K[d % 3]
                    pe.wait_ge(s_lo, l * UNITS + u + 1)
                    if d % 3 == 0:
                        if q < 3:
                            pe.wait_ge(s_fv, l * KF + 20 + q + CREDIT)
                        else:
                            pe.wait_ge(s_xu, 2 * KD + 2 * KD * l + 2)

                    def made(kk):
                        pe.wait_ge(s_flo, l * KF + k0 + kk + 1 + CREDIT)

                    column_unit(u, pair((q + 1) % 3), k1 - k0,
                                lambda kk: (hid_hi[:, k0 + kk, :], hid_lo[:, k0 + kk, :]),
                                d % 3 == 0, d % 3 == 2, made if q == 0 else None)
                sum_squares(2 * l + 2)
            for c8 in range(KD):
                pe.wait_ge(s_fin, c8 + 1)
                if c8 >= 4:
                    pe.wait_ge(s_yev, c8 - 3)
                for t in range(TT):
                    last = nc.tensor.transpose(bank[c8 % 4][:, t * P:(t + 1) * P],
                                               hm[:, c8 % 3, t * P:(t + 1) * P], ident[:])
                last.then_inc(s_yT, 1)


NAMES = ["x", "c", "positions", "norm1_g", "norm2_g", "ada_w", "ada_b", "w_in", "cmp_pos", "cmp_w1", "cmp_w2",
         "att_norm_g", "m_conv_w", "m_conv_b", "m_gate_b", "m_norm_g", "w_out", "ffn_up", "ffn_conv_w",
         "ffn_conv_b", "ffn_down", "final_g"]


def kernel(**inputs):
    import concourse.bacc as bacc
    from concourse.bass_utils import run_bass_kernel_spmd

    nc = bacc.Bacc("TRN2", target_bir_lowering=False, num_devices=1)
    arrays, args = {}, []
    for name in NAMES:
        a = np.ascontiguousarray(inputs[name])
        arrays[f"in_{name}"] = a
        args.append(nc.dram_tensor(f"in_{name}", a.shape, dt.from_np(a.dtype), kind="ExternalInput").ap())
    out = nc.dram_tensor("out", (1, T, D), F32, kind="ExternalOutput").ap()
    build(nc, *args, out)
    r = run_bass_kernel_spmd(nc, [arrays], core_ids=[0])
    return r.results[0]["out"]
```

```python
from contextlib import ExitStack

import numpy as np
import concourse.bass as bass
from concourse import mybir

dt = mybir.dt
F32, F32R, BF16 = dt.float32, dt.float32r, dt.bfloat16
ALU = mybir.AluOpType
ACT = mybir.ActivationFunctionType
AX = mybir.AxisListType

P = 128
D = 1024
T = 512
L = 2
KD = D // P
TT = T // P
F = 2816
KF = F // P
NH, DH, NG = 8, 64, 2
R = NH // NG
MH, MD = 4, 128
MC, FC = 4, 3
HALF = 8
CB, CS = 32, 16
NC = (T - CB) // CS + 1
NCP = NC + 1
EPS = 1e-6
NEG = -1e30
TINY = 1e-30
MSCALE = float(np.float32(MD ** -0.5))

C_MQK, C_MV, C_IF, C_MO = 1304, 2328, 2840, 2848
NGATE = 24

PARS = [("ada_b", 48), ("norm1_g", KD), ("norm2_g", KD), ("m_conv_w", 4 * KD), ("cmp_pos", CB),
        ("ffn_conv_b", KF), ("m_conv_b", KD), ("ffn_conv_w", 3 * KF), ("att_norm_g", KD // 2),
        ("m_norm_g", KD // 2)]
AB, N1, N2, MW, CP, FB, MB, FW, MG = (sum(n for _, n in PARS[:i]) for i in range(9))
NPAR = sum(n for _, n in PARS)

U_QKV, U_MV, U_MO, U_MQK, U_OUT, U_UP, U_DOWN, UNITS = 0, 6, 8, 10, 14, 18, 40, 52
SLOT = 2048
RAW, HI = 3, 2
AUNITS = 24
ARING = 4
EARLY = 8
DOWN_K = [(0, 8), (8, 15), (15, 22)]
BODY = 6
LOOPED = KF // BODY * BODY
CREDIT = 2

PB = 6
NJ = 16
J_K, J_X = 8, 12
T_BANK = (4, 5, 7, 6)
NW = NH * TT
BH = 2
NB = NH // BH
BW = BH * TT
W_OFF = [0, 512, 896, 1152]
W_ALL = 1280


NEXT_AT = {20: 0, 21: 1, 22: 2, 23: 3, 24: 4, 26: 5, 28: 6, 30: 7}


def slot_of(u):
    return (u + (u >= U_DOWN)) % RAW


def slot_need(u):
    before = [v for v in range(u) if slot_of(v) == slot_of(u)]
    return before[-1] + 1 if before else max(v for v in range(UNITS) if slot_of(v) == slot_of(u)) - UNITS + 1


def build(nc, x, c, positions, norm1_g, norm2_g, ada_w, ada_b, w_in, cmp_pos, cmp_w1, cmp_w2,
          att_norm_g, m_conv_w, m_conv_b, m_gate_b, m_norm_g, w_out, ffn_up, ffn_conv_w,
          ffn_conv_b, ffn_down, final_g, out):
    ctx = ExitStack()
    with ctx:
        cursor = [16512]

        def place(name, shape, dtype=F32, at=None):
            size = int(np.prod(shape[1:])) * (2 if dtype == BF16 else 4)
            if at is None:
                at = cursor[0]
                cursor[0] += (size + 31) // 32 * 32
            return nc.alloc_sbuf_tensor_at(name, shape, dtype, offset=at)

        xT = place("xT", [P, KD, T])
        qm = place("qm", [DH + 2, NH, T], F32R, at=cursor[0])
        h_hi = place("h_hi", [P, KD, T], F32R)
        ot = place("ot", [DH + 1, 2, T], at=cursor[0])
        late_craw = place("late_craw", [P, 2, T], at=cursor[0] + 2 * 4 * T)
        h_lo = place("h_lo", [P, KD, T], F32R)
        raw_at = cursor[0]
        w_raw = place("w_raw", [P, RAW, SLOT])
        w_lo = place("w_lo", [P, RAW, SLOT], F32R, at=raw_at)
        w_hi = place("w_hi", [P, HI, SLOT], F32R)
        sq = place("sq", [P, T])
        diag = place("diag", [P, TT, P], at=cursor[0] - 4 * T)
        hm_at = cursor[0]
        hm = place("hm", [P, 3, T])
        asum = place("asum", [P, 2, T], at=hm_at)
        craw = [sq[:], hm[:, 2, :], late_craw[:, 0, :], late_craw[:, 1, :]]
        ident = place("ident", [P, P])
        identr = place("identr", [MH, P], F32R)
        identb = place("identb", [P, P], BF16)
        tri = place("tri", [P, P], BF16)
        triT = place("triT", [P, P], BF16)
        ones = place("ones", [P, P])
        eps = place("eps", [P, 1])
        ms = place("ms", [P, TT])
        root = place("root", [P, TT])
        tiny = place("tiny", [P, 1])
        par_all = place("par_all", [P, 4, P])
        par = place("par", [P, NPAR])
        cact = place("cact", [P, KD])
        mod = place("mod", [P, 48])
        am = place("am", [P, 2, KD])
        cos = place("cos", [P, TT, 2, HALF])
        sin = place("sin", [P, TT, 2, HALF])
        cmask = place("cmask", [P, TT, NCP])
        gate_b = place("gate_b", [MH, L, 2])
        ada_at = cursor[0]
        a_raw = place("a_raw", [P, 2, SLOT])
        union = cursor[0]
        hid_hi = place("hid_hi", [P, KF, T], F32R)
        hid_lo = place("hid_lo", [P, KF, T], F32R)
        end = cursor[0]

        class Region:
            def __init__(self, at, stop):
                self.at, self.stop = at, stop

            def place(self, name, shape, dtype=F32):
                size = (int(np.prod(shape[1:])) * 4 + 31) // 32 * 32
                t = place(name, shape, dtype, at=self.at)
                self.at += size
                assert self.at <= self.stop, (name, self.at - self.stop)
                return t

        mix = Region(union, end)
        tok_at = mix.at
        tok = mix.place("tok", [P, NJ, TT, P])
        qk = place("qk", [P, NJ, T], F32R, at=tok_at)
        mw = place("mw", [P, 3, T], at=tok_at)
        mws = place("mws", [P, 2, W_ALL], at=tok_at + 3 * T * 4)
        v_sw = mix.place("v_sw", [P, TT, 2, NG, DH + 1])
        v_m = mix.place("v_m", [P, TT, MH, MD + 1])
        mixt_at = mix.at
        mixt = mix.place("mixt", [P, TT, D])
        a_mix = place("a_mix", [P, 2, SLOT], at=mixt_at)
        a_slot = [a_raw[:, 0, :], a_raw[:, 1, :], a_mix[:, 0, :], a_mix[:, 1, :]]
        mqk_at = mix.at
        mqk = mix.place("mqk", [P, 2 * MH, T])
        xab = place("xab", [P, 4, 2, CS // 2 * NCP], at=mqk_at)
        w1 = place("w1", [P, 2, CB // 2, DH], at=mqk_at + 8192)
        a_hi = mix.place("a_hi", [MH, T], F32R)
        late = mix.at
        pt = mix.place("pt", [P, 2, 2, T])
        rt = place("rt", [P, 2, 14, 2 * TT, HALF], at=late)
        pT = place("pT", [P, TT, 2, P], at=late)
        gif = mix.place("gif", [P, TT, NGATE + 2 * MH])
        asum0 = place("asum0", [P, 2, T], at=mixt_at - 8256)
        a_mqk = place("a_mqk", [P, 2, SLOT], at=mqk_at)
        a_tok = place("a_tok", [P, 2, SLOT], at=tok_at + 16384)
        a_early = a_slot + [a[:, i, :] for a in (a_mqk, a_tok) for i in range(2)]
        xtok = place("xtok", [P, TT, D], at=tok_at)
        otok = place("otok", [P, TT, D], at=mixt_at)
        prow = place("prow", [P, 4, P], at=late)
        pos_i = place("pos_i", [P, TT], dt.int32, at=late + 4096)
        ang = place("ang", [P, TT, HALF], at=late + 4096 + 64)
        angn = place("angn", [P, TT, HALF], at=late + 4096 + 64 + 128)
        posf = place("posf", [P, TT], at=late + 4096 + 64 + 256)
        invf = place("invf", [P, HALF], at=late + 4096 + 64 + 288)
        over = place("over", [P, TT, HALF], at=late + 4096 + 64 + 320)

        att = Region(ada_at, union)
        ib, fb, fe, brow = (att.place(n, [MH, T]) for n in ("ib", "fb", "fe", "brow"))
        mrow = fe
        a_lo = place("a_lo", [MH, T], F32R, at=ada_at + 3 * 4 * T)
        t12 = place("t12", [P, 2, 2, TT, DH], at=ada_at)
        sqb = place("sqb", [P, TT, DH], at=ada_at + 4096)
        gat = att.place("gat", [P, TT, NGATE])
        csc = place("csc", [P, TT, NH, NCP], at=hm_at)
        hidk = att.place("hidk", [DH, NG, NCP])
        hidv = att.place("hidv", [DH, NG, 4, NCP])
        kcmp = att.place("kcmp", [P, NG, NCP])
        vcmp = att.place("vcmp", [P, NG, R, DH])
        w2 = att.place("w2", [DH, 2, DH])
        cmx = att.place("cmx", [P, TT, NH])
        csum = att.place("csum", [P, TT, NH])
        nmx = att.place("nmx", [P, NB, TT, BH, 2])
        coef = att.place("coef", [P, 2, TT])
        acol = att.place("acol", [P, 2, TT, MH])
        den = att.place("den", [P, 2, 2])
        ssq = att.place("ssq", [P, TT, NH + MH])
        ssq2 = att.place("ssq2", [P, TT, NH + MH])
        sqj = att.place("sqj", [P, MD])

        ffn = Region(ada_at, union)
        fy = ffn.place("fy", [P, 2, T])
        ft = ffn.place("ft", [P, 2, T])

        psum = ctx.enter_context(nc.psum_tensor("psum", [P, 8, T], F32))
        bank = [psum[:, i, :] for i in range(8)]

        def sem(name):
            return ctx.enter_context(nc.semaphore(name))

        s_w = [sem(f"s_w{i}") for i in range(RAW)]
        s_a = [sem(f"s_a{i}") for i in range(ARING)]
        s_e = [sem(f"s_e{i}") for i in range(EARLY)]
        s_asum, s_ag = sem("s_asum"), sem("s_ag")
        s_cw = sem("s_cw")
        s_x, s_par, s_pos, s_out = sem("s_x"), sem("s_par"), sem("s_pos"), sem("s_out")
        s_const, s_ang, s_sin = sem("s_const"), sem("s_ang"), sem("s_sin")
        s_prT, s_pall, s_cact, s_xT = sem("s_prT"), sem("s_pall"), sem("s_cact"), sem("s_xT")
        s_hi, s_lo, s_used = sem("s_hi"), sem("s_lo"), sem("s_used")
        s_aused, s_mod = sem("s_aused"), sem("s_mod")
        s_sqa, s_ss, s_ms, s_rt, s_dg, s_rb = (sem(n) for n in (
            "s_sqa", "s_ss", "s_ms", "s_rt", "s_dg", "s_rb"))
        s_sql = sem("s_sql")
        s_hm, s_hhi, s_hlo = sem("s_hm"), sem("s_hhi"), sem("s_hlo")
        s_proj = sem("s_proj")
        s_qev, s_pev, s_mvev, s_moev = (sem(n) for n in ("s_qev", "s_pev", "s_mvev", "s_moev"))
        s_vone = sem("s_vone")
        s_cv1, s_cv2, s_cv3 = sem("s_cv1"), sem("s_cv2"), sem("s_cv3")
        s_craw = sem("s_craw")
        s_rope = sem("s_rope")
        s_ift, s_ib, s_ln, s_rows, s_col, s_acol = (sem(n) for n in
                                                    ("s_ift", "s_ib", "s_ln", "s_rows", "s_col", "s_acol"))
        s_tp, s_thi, s_tev = sem("s_tp"), sem("s_thi"), sem("s_tev")
        s_hid, s_hids, s_cmp, s_cmpev = sem("s_hid"), sem("s_hids"), sem("s_cmp"), sem("s_cmpev")
        s_cS, s_csub, s_cexp, s_cT, s_cTev, s_cO, s_cev = (sem(n) for n in (
            "s_cS", "s_csub", "s_cexp", "s_cT", "s_cTev", "s_cO", "s_cev"))
        s_gat = sem("s_gat")
        s_S, s_nm, s_ST, s_exp, s_PV = (sem(n) for n in ("s_S", "s_nm", "s_ST", "s_exp", "s_PV"))
        s_nr, s_nrow = sem("s_nr"), sem("s_nrow")
        s_qm0, s_qm = sem("s_qm0"), sem("s_qm")
        s_oev, s_oT = sem("s_oev"), sem("s_oT")
        s_gated, s_comb, s_asq = sem("s_gated"), sem("s_comb"), sem("s_asq")
        s_mS, s_mW, s_mWS = sem("s_mS"), sem("s_mW"), sem("s_mWS")
        s_mO, s_mev = sem("s_mO"), sem("s_mev")
        s_rt2, s_mixa, s_mixm = sem("s_rt2"), sem("s_mixa"), sem("s_mixm")
        s_mT, s_mhi, s_mlo = sem("s_mT"), sem("s_mhi"), sem("s_mlo")
        s_xu = sem("s_xu")
        s_y1, s_y2, s_z, s_fv, s_fhi, s_flo = (sem(n) for n in (
            "s_y1", "s_y2", "s_z", "s_fv", "s_fhi", "s_flo"))
        s_fin, s_yT, s_yev = sem("s_fin"), sem("s_yT"), sem("s_yev")

        block = ctx.enter_context(nc.Block())

        def pair(i):
            return bank[2 * i], bank[2 * i + 1]

        CONV_AT = {3: MH, 5: MH + 2}
        C_BANK = (6, 7, 4, 5)

        def score_bank(w):
            return 4 if w < BW and w % 2 else 6

        BESIDE, AHEAD = (0, 2, 3, 5, 7, 8, 8, 8, 8), (1, 0, 1, 1, 1, 0, 0, 0)

        def beside(z):
            b, i = z // BW + 1, z % BW
            return range(b * BW + BESIDE[i], b * BW + BESIDE[i + 1]) if b < NB else range(0)

        def done_beside(z):
            return BW + sum(len(beside(i)) for i in range(z + 1))

        def unit_used(eng, l, u):
            eng.wait_ge(s_used, l * UNITS + (u + 1 + CREDIT))

        def projected(eng, l, group, t):
            if t < TT - 1:
                eng.wait_ge(s_proj, l * 5 * (TT - 1) + group * (TT - 1) + t + 1)
            else:
                unit_used(eng, l, 2 * group + 1)

        ffw = ffn_conv_w.rearrange("l w (r q) -> l (w r) q", q=P)
        tiles = [[("ada_b", ada_b.rearrange("l (r q) -> (l r) q", q=P)),
                  ("norm1_g", norm1_g.rearrange("l (r q) -> (l r) q", q=P)),
                  ("norm2_g", norm2_g.rearrange("l (r q) -> (l r) q", q=P))],
                 [("m_conv_w", m_conv_w.rearrange("l w (r q) -> (l w r) q", q=P)),
                  ("cmp_pos", cmp_pos.rearrange("l i (c s) d -> (l i c) (s d)", s=2))],
                 [("ffn_conv_w", ffw[0]), ("ffn_conv_b", ffn_conv_b.rearrange("l (r q) -> (l r) q", q=P)),
                  ("m_conv_b", m_conv_b.rearrange("l (r q) -> (l r) q", q=P))],
                 [("c", c.rearrange("o (r q) -> (o r) q", q=P)),
                  ("att_norm_g", att_norm_g.rearrange("l (r q) -> (l r) q", q=P)),
                  ("m_norm_g", m_norm_g.rearrange("l (r q) -> (l r) q", q=P)),
                  ("final_g", final_g.rearrange("(r q) -> r q", q=P)), ("ffn_conv_w1", ffw[1])]]
        loads, where, tile_rows = [], {}, []
        for i, tile in enumerate(tiles):
            row = 0
            for name, src in tile:
                loads.append((i, row, src))
                where[name] = i * P + row
                row += src.shape[0]
            assert row <= P
            tile_rows.append(row)
        CROW, FROW = where["c"], where["final_g"]
        step_of = {name: n for name, n in PARS}
        step_of["ffn_conv_w"] = where["ffn_conv_w1"] - where["ffn_conv_w"]

        @block.sync
        def _(sp):
            for t in range(TT):
                sp.dma_start(xtok[:, t, :], x[0, t * P:(t + 1) * P, :]).then_inc(s_x, 16)
            sp.dma_start(gate_b[:], m_gate_b.rearrange("l (t h) -> h l t", t=2),
                         allow_slow_non_contiguous=True).then_inc(s_pos, 16)

            sp.wait_ge(s_par, 16 * len(loads))
            for i in range(EARLY):
                sp.dma_start(a_early[i].rearrange("p (k n) -> p k n", k=KD // 2),
                             ada_w.rearrange("l (k p) n -> l p k n", p=P)
                             [0, :, i % 2 * 4:i % 2 * 4 + 4, i // 2 * T:(i // 2 + 1) * T]).then_inc(s_e[i], 16)

            def load(l, u, parts):
                parts = list(parts)
                sp.wait_ge(s_used, l * UNITS + slot_need(u) + CREDIT)
                for dst, src in parts:
                    sp.dma_start(dst, src).then_inc(s_w[slot_of(u)], 16)

            def slot(u, k, n):
                return w_raw[:, slot_of(u), 0:k * n].rearrange("p (k n) -> p k n", k=k)

            def load_rows(l, u, w, col, n):
                half = (u % 2) * 4
                src = w.rearrange("l (k p) n -> l p k n", p=P)
                for i in range(2):
                    yield (slot(u, 4, n)[:, 2 * i:2 * i + 2, :],
                           src[l, :, half + 2 * i:half + 2 * i + 2, col:col + n])

            def load_cols(l, u, w, col, k0, k1):
                src = w.rearrange("l (k p) n -> l p k n", p=P)
                mid = (k1 - k0) // 2
                for a, b in ((0, mid), (mid, k1 - k0)):
                    yield slot(u, k1 - k0, 256)[:, a:b, :], src[l, :, k0 + a:k0 + b, col:col + 256]

            def ada_rows(l, j):
                return ada_w.rearrange("l (k p) n -> l p k n", p=P)[
                    l, :, j % 2 * 4:j % 2 * 4 + 4, j // 2 * T:(j // 2 + 1) * T]

            def load_ada(l, j):
                sp.wait_ge(s_aused, l * AUNITS + max(j - ARING + 1, EARLY))
                sp.dma_start(a_slot[j % ARING].rearrange("p (k n) -> p k n", k=KD // 2), ada_rows(l, j))\
                    .then_inc(s_a[j % ARING], 16)

            def load_next(l, after, i):
                sp.wait_ge(s_aused, l * AUNITS + (AUNITS + i))
                sp.dma_start(a_slot[1].rearrange("p (k n) -> p k n", k=KD // 2), ada_rows(after, i))\
                    .then_inc(s_e[i], 16)

            def load_w_in(l, u):
                if u < 4:
                    load(l, u, load_rows(l, u, w_in, (u // 2) * 512, 512))
                elif u < 6:
                    half = (u % 2) * 4
                    src = w_in.rearrange("l (k p) n -> l p k n", p=P)
                    dst = slot(u, 4, 288)
                    load(l, u, [(dst[:, :, 0:280], src[l, :, half:half + 4, 1024:1304]),
                                (dst[:, :, 280:288], src[l, :, half:half + 4, C_IF:C_IF + 8])])
                elif u < U_MQK:
                    load(l, u, load_rows(l, u, w_in, C_MV if u < U_MO else C_MO, 512))
                else:
                    load(l, u, load_cols(l, u, w_in, C_MQK + (u - U_MQK) * 256, 0, KD))

            def load_up(l, u, j):
                src = ffn_up.rearrange("l (k p) n -> l p k n", p=P)
                dst = w_raw[:, slot_of(u), :].rearrange("p (k n) -> p k n", k=KD)
                load(l, u, [(dst[:, :, 0:P], src[l, :, :, bass.ds(j * P, P)]),
                            (dst[:, :, P:2 * P], src[l, :, :, bass.ds(j * P + F, P)])])

            with sp.Fori(0, L) as l:
                after = sp.snap(l * -1 + (L - 1))
                for u in range(RAW):
                    load_w_in(l, u)
                for j in range(EARLY, EARLY + 2):
                    load_ada(l, j)
                for i in range(2):
                    sp.dma_start(w1[:, i, :, :], cmp_w1.rearrange("l i (c p) j -> l p i c j", p=P)[l, :, i])\
                        .then_inc(s_cw, 16)
                for u in range(RAW, U_OUT):
                    load_w_in(l, u)
                    for j in {3: range(10, 14), 4: range(14, 18), 5: (18, 19), 6: (20, 21), 8: (22, 23)}.get(u, ()):
                        load_ada(l, j)
                    if u == 11:
                        sp.wait_ge(s_aused, l * AUNITS + AUNITS)
                        sp.dma_start(w2[:], cmp_w2.rearrange("l i j d -> l j i d")[l]).then_inc(s_cw, 16)
                for u in range(U_OUT, U_UP):
                    load(l, u, load_cols(l, u, w_out, (u - U_OUT) * 256, 0, KD))
                with sp.Fori(0, LOOPED // BODY) as i:
                    for s in range(BODY):
                        u = U_UP + s
                        sp.wait_ge(s_used, l * UNITS + i * BODY + (slot_need(u) + CREDIT))
                        src = ffn_up.rearrange("l (k p) n -> l p k n", p=P)
                        dst = w_raw[:, slot_of(u), :].rearrange("p (k n) -> p k n", k=KD)
                        for side in range(2):
                            sp.dma_start(dst[:, :, side * P:(side + 1) * P],
                                         src[l, :, :, bass.ds(i * (BODY * P) + (s * P + side * F), P)])\
                                .then_inc(s_w[slot_of(u)], 16)
                for j in range(LOOPED, KF):
                    load_up(l, U_UP + j, j)
                    if j in NEXT_AT:
                        load_next(l, after, NEXT_AT[j])
                for d in range(UNITS - U_DOWN):
                    u = U_DOWN + d
                    load(l, u, load_cols(l, u, ffn_down, (d // 3) * 256, *DOWN_K[d % 3]))
                    if KF + d in NEXT_AT:
                        load_next(l, after, NEXT_AT[KF + d])
            for c8 in range(KD):
                sp.wait_ge(s_yev, c8 + 1)
                sp.dma_start(out[0].rearrange("(t p) n -> p t n", p=P)[:, :, c8 * P:(c8 + 1) * P],
                             otok[:, :, c8 * P:(c8 + 1) * P]).then_inc(s_out, 16)
            sp.wait_ge(s_out, 16 * KD)

        @block.gpsimd
        def _(pool):
            g = nc.gpsimd
            g.memset(ident[:], 0.0)
            g.memset(identb[:], 0.0)
            g.memset(tri[:], 0.0)
            g.memset(triT[:], 0.0)
            g.memset(ones[:], 1.0)
            g.memset(cmask[:], 0.0)
            g.memset(eps[:], EPS)
            pool.drain()
            for m in (ident, identb):
                g.affine_select(out=m[:], in_=m[:], compare_op=ALU.not_equal, fill=1.0, base=0,
                                pattern=[[-1, P]], channel_multiplier=1)
            g.affine_select(out=tri[:], in_=tri[:], compare_op=ALU.is_ge, fill=NEG, base=0,
                            pattern=[[-1, P]], channel_multiplier=1)
            g.affine_select(out=triT[:], in_=triT[:], compare_op=ALU.is_ge, fill=NEG, base=0,
                            pattern=[[1, P]], channel_multiplier=-1)
            g.affine_select(out=cmask[:], in_=cmask[:], compare_op=ALU.is_ge, fill=NEG, base=-(CB - 1),
                            pattern=[[P, TT], [-CS, NCP]], channel_multiplier=1)
            pool.drain().then_inc(s_const, 1)
            pool.drain().then_inc(s_flo, CREDIT)

            def low(l, u, i=0):
                pool.wait_ge(s_hi, l * UNITS + i * BODY + (u + 1))
                g.tensor_tensor(w_lo[:, slot_of(u), :], w_raw[:, slot_of(u), :],
                                w_hi[:, u % HI, :].bitcast(F32), ALU.subtract).then_inc(s_lo, 1)

            def low_part(l, u, n):
                pool.wait_ge(s_hi, l * UNITS + u + 1)
                g.tensor_tensor(w_lo[:, slot_of(u), 0:n], w_raw[:, slot_of(u), 0:n],
                                w_hi[:, u % HI, 0:n].bitcast(F32), ALU.subtract).then_inc(s_lo, 1)

            def square(first, norm, c8):
                pool.wait_ge(s_xu, first + c8 + 1)
                if c8 == 0:
                    pool.wait_ge(s_ss, norm)
                    g.tensor_tensor(hm[:, 2, :], xT[:, 0, :], xT[:, 0, :], ALU.mult)
                else:
                    g.tensor_tensor(sq[:], xT[:, c8, :], xT[:, c8, :], ALU.mult)
                    pool.drain()
                    g.tensor_tensor(hm[:, 2, :], hm[:, 2, :], sq[:], ALU.add)
                if c8 == KD - 3:
                    pool.drain().then_inc(s_sqa, 1)
                else:
                    pool.drain()

            for c8 in range(KD - 2):
                square(0, 0, c8)
            with pool.Fori(0, L) as l:
                low(l, 0)
                pool.wait_ge(s_ss, 2 * l + 1)
                low(l, 1)
                g.memset(v_sw[:, :, :, :, DH:DH + 1], 1.0)
                g.memset(v_m[:, :, :, MD:MD + 1], 1.0)
                pool.drain().then_inc(s_vone, 1)
                for u in range(2, 16):
                    if u == U_OUT + 1:
                        unit_used(pool, l, U_OUT - 1)
                        for h in range(BH, NH):
                            q = qk[0:DH, h, :].bitcast(F32)
                            g.tensor_tensor(qm[0:DH, h, :], q, ones[0:DH, 0:1].broadcast_to([DH, T]), ALU.mult)\
                                .then_inc(s_qm, 1)
                    if u in (4, 5):
                        low_part(l, u, 4 * 288)
                    else:
                        low(l, u)
                for h in range(NH):
                    pool.wait_ge(s_gated, l * NH + h + 1)
                    o3 = mixt[:, :, h * DH:(h + 1) * DH]
                    for br in range(2):
                        g.tensor_tensor(o3, o3, t12[:, h % 2, br], ALU.add)
                        if br == 0:
                            pool.drain()
                    pool.drain()
                    if h >= 1:
                        pool.wait_ge(s_asq, l * NH + h)
                    g.tensor_tensor(sqb[:], o3, o3, ALU.mult).then_inc(s_comb, 1)
                for q in range(4):
                    for c8 in (2 * q, 2 * q + 1):
                        if c8 < KD - 2:
                            square(KD + 2 * KD * l, 2 * l + 1, c8)
                    if q < 3:
                        low(l, 16 + q)
                low(l, 19)

                def hidden_low(l, f, i, idx):
                    pool.wait_ge(s_fhi, l * KF + i * BODY + (f + 1))
                    g.tensor_tensor(hid_lo[:, bass.ds(idx, 1), :], ft[:, f % 2:f % 2 + 1, :],
                                    hid_hi[:, bass.ds(idx, 1), :].bitcast(F32), ALU.subtract)\
                        .then_inc(s_flo, 1)

                with pool.Fori(0, LOOPED // BODY) as i:
                    for s in range(BODY):
                        low(l, U_UP + 2 + s, i)
                        hidden_low(l, s, i, i * BODY + s)
                for f in range(LOOPED, KF):
                    if f + 2 + U_UP < U_DOWN:
                        low(l, U_UP + 2 + f)
                    else:
                        d = f + 2 + U_UP - U_DOWN
                        k0, k1 = DOWN_K[d % 3]
                        low_part(l, U_DOWN + d, (k1 - k0) * 256)
                    hidden_low(l, f, 0, f)
                for q in range(4):
                    for d in range(3 * q + 2, min(3 * q + 5, UNITS - U_DOWN)):
                        k0, k1 = DOWN_K[d % 3]
                        low_part(l, U_DOWN + d, (k1 - k0) * 256)
                    for c8 in (2 * q, 2 * q + 1):
                        if c8 < KD - 2:
                            square(2 * KD + 2 * KD * l, 2 * l + 2, c8)

        @block.scalar
        def _(act):
            s = nc.scalar

            act.dma_start(pos_i[:], positions[0].rearrange("(t p) -> p t", p=P),
                          allow_slow_non_contiguous=True).then_inc(s_pos, 16)
            for i, row, src in sorted(loads, key=lambda x: -x[0]):
                act.dma_start(prow[row:row + src.shape[0], i, :], src).then_inc(s_par, 16)

            def rope_tables():
                act.wait_ge(s_ang, 1)
                for i in range(2):
                    s.activation(sin[:, :, i, :], ang[:], ACT.Sin)
                act.wait_ge(s_ang, 2)
                for i in range(2):
                    last = s.activation(cos[:, :, i, :], angn[:], ACT.Sin)
                last.then_inc(s_sin, 1)
                act.wait_ge(s_const, 1)
                s.activation(identr[:], ident[0:MH, :], ACT.Copy)

            def last_squares(first, norm, late=None):
                for i in range(2):
                    act.wait_ge(s_xu, first + KD - 1 + i)
                    if late is not None and i == 0:
                        act.wait_ge(s_ag, late)
                    if i == 0:
                        act.wait_ge(s_ss, norm)
                    s.activation(hm[:, i, :], xT[:, KD - 2 + i, :], ACT.Square).then_inc(s_sql, 1)
                s.activation(tiny[:], eps[:], ACT.Sqrt)

            def high(l, u, i=0, n=SLOT):
                r = slot_of(u)
                before = sum(slot_of(v) == r for v in range(u))
                per = sum(slot_of(v) == r for v in range(UNITS))
                act.wait_ge(s_w[r], l * (32 * per) + i * (32 * BODY // RAW) + 32 * (before + 1))
                act.wait_ge(s_used, l * UNITS + i * BODY + (u - 1 + CREDIT))
                s.activation(w_hi[:, u % HI, 0:n], w_raw[:, r, 0:n], ACT.Copy).then_inc(s_hi, 1)

            def width(u):
                if u in (4, 5):
                    return 4 * 288
                if u >= U_DOWN:
                    k0, k1 = DOWN_K[(u - U_DOWN) % 3]
                    return (k1 - k0) * 256
                return SLOT

            def norm_root(norm):
                act.wait_ge(s_ms, norm + 1)
                s.activation(root[:], ms[:], ACT.Sqrt, bias=eps[:, 0:1], scale=1.0 / D).then_inc(s_rt, 1)

            def norm_high(chunks, shift):
                for c8 in range(KD):
                    act.wait_ge(s_hm, chunks + c8 + 1)
                    s.activation(h_hi[:, c8, :], hm[:, c8 % 3, :], ACT.Identity,
                                 bias=mod[:, shift + c8:shift + c8 + 1]).then_inc(s_hhi, 1)

            rope_tables()
            act.wait_ge(s_pall, 1)
            s.activation(cact[:], par_all[:].rearrange("p a b -> p (a b)")[:, CROW:CROW + KD], ACT.Silu)\
                .then_inc(s_cact, 1)
            for c8 in range(KD):
                act.wait_ge(s_xT, c8 + 1)
                s.activation(xT[:, c8, :], bank[c8 % 6], ACT.Copy).then_inc(s_xu, 1)
            last_squares(0, 0)
            with act.Fori(0, L) as l:
                high(l, 0)
                norm_root(2 * l)
                norm_high(2 * KD * l, 0)
                high(l, 1)
                def conv_first(c8):
                    s.activation(mqk[:, c8, :], bank[c8 % 4], ACT.Identity, bias=par[:, MB + c8:MB + c8 + 1],
                                 scale=par[:, MW + 3 * KD + c8:MW + 3 * KD + c8 + 1]).then_inc(s_cv1, 1)

                def conv_silu(c8):
                    act.wait_ge(s_cv2, l * 2 * MH + c8 + 1)
                    s.activation(mqk[:, c8, :], mqk[:, c8, :], ACT.Silu).then_inc(s_cv3, 1)

                def high_of(j, scale):
                    act.wait_ge(s_tp, l * NJ + (j - J_K + 4 if j >= J_K else j + 8) + 1)
                    b = T_BANK[(j - J_K + 4 if j >= J_K else j + 8) % 4]
                    s.activation(qk[:, j, :], bank[b], ACT.Copy, scale=scale).then_inc(s_thi, 1)

                def sigmoids():
                    for t in range(TT):
                        projected(act, l, 4, t)
                        s.activation(mixt[:, t, T:D], bank[t], ACT.Sigmoid).then_inc(s_moev, 1)
                    s.activation(gat[:], gif[:, :, 0:NGATE], ACT.Sigmoid).then_inc(s_gat, 1)

                for u in range(U_OUT):
                    if u == U_MO + 1:
                        for j in range(J_K, J_K + 4):
                            high_of(j, 1.0)
                        for j in range(NH):
                            if j == 5:
                                sigmoids()
                            high_of(j, DH ** -0.5)
                    if u == U_MV + 1:
                        for t in range(TT):
                            projected(act, l, 3, t)
                            s.activation(v_m[:, t, :, 0:MD], bank[t].rearrange("p (h d) -> p h d", h=MH), ACT.Copy)\
                                .then_inc(s_mvev, 1)
                    if u == U_MQK + 3:
                        act.wait_ge(s_col, l + 1)
                        cols = bank[6][:, 0:2 * TT * MH].rearrange("p (i t h) -> p i t h", i=2, t=TT)
                        s.activation(acol[:, 0], cols[:, 0], ACT.Copy)
                        s.activation(acol[:, 1], cols[:, 1], ACT.Exp, scale=-1.0).then_inc(s_acol, 1)
                    if u < U_OUT - 1:
                        high(l, u + 2, n=width(u + 2))
                    if u == 1:
                        for t in range(TT):
                            projected(act, l, 0, t)
                            s.activation(tok[:, 0:NH, t, :].rearrange("p h (s d) -> p h s d", s=2),
                                         bank[t].rearrange("p (h s d) -> p h s d", h=NH, s=1)
                                         .broadcast_to([P, NH, 2, DH]), ACT.Copy).then_inc(s_qev, 1)
                    if u >= U_MQK:
                        unit_used(act, l, u)
                        if u == U_OUT - 1:
                            s.activation(qm[0:DH, 0:BH, :], qk[0:DH, 0:BH, :].bitcast(F32), ACT.Copy)\
                                .then_inc(s_qm0, 1)
                        for c8 in (2 * (u - U_MQK), 2 * (u - U_MQK) + 1):
                            conv_first(c8)
                            if c8 >= MH:
                                s.activation(craw[c8 - MH], bank[c8 % 4], ACT.Copy).then_inc(s_craw, 1)
                    if u == U_MQK:
                        act.wait_ge(s_hid, l + 1)
                        hid_ps = bank[4][0:DH, 0:4 * NCP].rearrange("p (i g n) -> p i g n", i=2, g=NG)
                        s.activation(hidk[:, :, 0:NC], hid_ps[:, 0, :, 0:NC], ACT.Silu)
                        for gr in range(NG):
                            last = s.activation(hidv[:, gr, :, 0:NC],
                                                hid_ps[:, 1, gr:gr + 1, 0:NC].broadcast_to([DH, 4, NC]), ACT.Silu)
                        last.then_inc(s_hids, 1)
                    if u == U_MQK + 1:
                        for c8 in (0, 1):
                            conv_silu(c8)
                        act.wait_ge(s_ib, l + 1)
                        s.activation(fe[:], fe[:], ACT.Exp, scale=-1.0)
                        act.drain()
                        s.activation(fe[:], fe[:], ACT.Ln, bias=ones[0:MH, 0:1]).then_inc(s_ln, 1)
                        for t in range(TT):
                            act.wait_ge(s_csub, l * TT + t + 1)
                            s.activation(csc[:, t], csc[:, t], ACT.Exp).then_inc(s_cexp, 1)

                def max_rows(b):
                    act.wait_ge(s_nr, l * NB + b + 1)
                    s.activation(qm[DH:DH + 2, BH * b:BH * (b + 1), :], psum[DH:DH + 2, 6:6 + BH, :], ACT.Copy)\
                        .then_inc(s_nrow, 1)

                max_rows(0)
                def evacuate(h):
                    act.wait_ge(s_PV, l * NW + TT * h + TT)
                    if h:
                        act.wait_ge(s_oT, l * NH + h)
                    s.activation(ot[:], psum[0:DH + 1, 4:6, :], ACT.Copy).then_inc(s_oev, 1)

                for z in range(NW):
                    if z % TT == 1 and z > TT:
                        evacuate(z // TT - 1)
                    if z % BW == BW - 1 and z < NW - 1:
                        max_rows(z // BW + 1)
                    if z == 2:
                        high(l, U_OUT + 1)
                    if z == 20:
                        for c8 in range(2, 2 * MH):
                            conv_silu(c8)
                    n = (TT - z % TT) * P
                    act.wait_ge(s_ST, l * NW + z + 1)
                    if z >= 2:
                        act.wait_ge(s_PV, l * NW + z - 1)
                    s.activation(pt[:, z % 2, :, 0:n], psum[:, 2 * (z % 2):2 * (z % 2) + 2, 0:n], ACT.Exp)\
                        .then_inc(s_exp, 1)
                evacuate(NH - 1)
                def mixer_high(c8):
                    act.wait_ge(s_mT, l * KD + c8 + 1)
                    s.activation(h_hi[:, c8, :], bank[c8 % 4], ACT.Copy,
                                 scale=par[:, MG + c8:MG + c8 + 1]).then_inc(s_mhi, 1)

                for h in range(MH + 1):
                    if h < MH:
                        for j in range(TT):
                            z = h * TT + j
                            n = (TT - j) * P
                            act.wait_ge(s_mS, l * 16 + z + 1)
                            if z >= 3:
                                act.wait_ge(s_mWS, l * 16 + z - 2)
                            s.activation(mw[:, z % 3, 0:n], pair(z % 3)[1][:, 0:n], ACT.Exp,
                                         bias=acol[:, 0, j, h:h + 1]).then_inc(s_mW, 1)
                    if h == 1:
                        act.wait_ge(s_asq, l * NH + NH)
                        s.activation(ssq2[:, :, 0:NH], ssq[:, :, 0:NH], ACT.Sqrt, bias=eps[:, 0:1],
                                     scale=1.0 / DH).then_inc(s_rt2, 1)
                    if h == MH:
                        for c8 in range(KD // 2):
                            mixer_high(c8)
                    if h >= 1:
                        for e in range(2):
                            act.wait_ge(s_mev, l * 8 + 2 * (h - 1) + e + 1)
                            for t in (2 * e, 2 * e + 1):
                                last = s.activation(sqj[:], mixt[:, t, T + (h - 1) * MD:T + h * MD], ACT.Square,
                                                    accum_out=ssq[:, t, NH + h - 1:NH + h])
                                act.drain()
                s.activation(ssq2[:, :, NH:], ssq[:, :, NH:], ACT.Sqrt, bias=eps[:, 0:1], scale=1.0 / MD)\
                    .then_inc(s_rt2, 1)
                for c8 in range(KD // 2, KD):
                    mixer_high(c8)
                for u in (16, 17, 18):
                    high(l, u)
                last_squares(KD + 2 * KD * l, 2 * l + 1)
                high(l, 19)
                norm_root(2 * l + 1)
                norm_high(2 * KD * l + KD, 24)

                def hidden_step(l, f, i, idx):
                    unit_used(act, l, i * BODY + (U_UP + f))
                    a_ps = pair(f % 3)[0]
                    s.activation(fy[:, f % 2, :], a_ps, ACT.Identity,
                                 bias=par[:, bass.ds(idx + FB, 1)],
                                 scale=par[:, bass.ds(idx + FW + 2 * KF, 1)]).then_inc(s_y1, 1)
                    act.wait_ge(s_y2, l * KF + i * BODY + (f + 1))
                    s.activation(fy[:, f % 2, :], fy[:, f % 2, :], ACT.Silu).then_inc(s_z, 1)
                    act.wait_ge(s_fv, l * KF + i * BODY + (f + 1 + CREDIT))
                    s.activation(hid_hi[:, bass.ds(idx, 1), :], ft[:, f % 2:f % 2 + 1, :], ACT.Copy)\
                        .then_inc(s_fhi, 1)

                with act.Fori(0, LOOPED // BODY) as i:
                    for f in range(BODY):
                        high(l, U_UP + 2 + f, i)
                        hidden_step(l, f, i, i * BODY + f)
                for f in range(LOOPED, KF):
                    high(l, U_UP + 2 + f, n=width(U_UP + 2 + f))
                    hidden_step(l, f, 0, f)
                for u in range(U_DOWN + 2, UNITS):
                    high(l, u, n=width(u))
                last_squares(2 * KD + 2 * KD * l, 2 * l + 2, l * (AUNITS // 2) + (AUNITS + EARLY) // 2)
            norm_root(2 * L)
            for c8 in range(KD):
                act.wait_ge(s_yT, c8 + 1)
                s.activation(otok[:, :, c8 * P:(c8 + 1) * P],
                             bank[c8 % 4].rearrange("p (t n) -> p t n", t=TT), ACT.Copy).then_inc(s_yev, 1)

        @block.vector
        def _(dve):
            v = nc.vector

            PI = 3.1415925
            C1, C2 = 6.28125, 0.0019350051879882812
            C3 = float(2 * np.pi - C1 - C2)
            inv = (np.float32(500000.0) ** (-np.arange(0, 2 * HALF, 2, dtype=np.float32) / np.float32(2 * HALF)))
            for i in range(HALF):
                v.memset(invf[:, i:i + 1], float(inv[i]))
            dve.wait_ge(s_pos, 32)
            v.tensor_copy(posf[:], pos_i[:])
            dve.drain().then_inc(s_fv, CREDIT)
            v.tensor_tensor(ang[:], posf[:].unsqueeze(2).broadcast_to([P, TT, HALF]),
                            invf[:].unsqueeze(1).broadcast_to([P, TT, HALF]), ALU.mult)
            dve.drain()
            MAGIC = 12582912.0
            v.tensor_scalar(angn[:], ang[:], float(1 / (2 * np.pi)), MAGIC, ALU.mult, ALU.add)
            dve.drain()
            v.tensor_scalar(angn[:], angn[:], MAGIC, None, ALU.subtract)
            for step in (C1, C2, C3):
                dve.drain()
                v.scalar_tensor_tensor(out=ang[:], in0=angn[:], scalar=-step, in1=ang[:], op0=ALU.mult, op1=ALU.add)
            dve.drain()
            v.tensor_scalar(angn[:], ang[:], float(np.pi / 2), None, ALU.add)
            v.tensor_scalar(ang[:], ang[:], PI, -PI, ALU.min, ALU.max)
            dve.drain().then_inc(s_ang, 1)
            v.tensor_scalar(over[:], angn[:], PI, -float(2 * np.pi), ALU.is_gt, ALU.mult)
            dve.drain()
            v.tensor_tensor(angn[:], angn[:], over[:], ALU.add)
            dve.drain()
            v.tensor_scalar(angn[:], angn[:], PI, -PI, ALU.min, ALU.max)
            dve.drain().then_inc(s_ang, 1)

            dve.wait_ge(s_prT, 1)
            for i in range(4):
                last = v.tensor_copy(par_all[:, i, 0:tile_rows[i]], bank[7][:, i * P:i * P + tile_rows[i]])
            last.then_inc(s_pall, 1)

            def rstd(n):
                dve.wait_ge(s_ss, n + 1)
                v.tensor_reduce(out=ms[:], in_=bank[7][:, 0:3 * TT].rearrange("p (s t) -> p t s", t=TT),
                                axis=AX.X, op=ALU.add).then_inc(s_ms, 1)
                dve.wait_ge(s_rt, n + 1)
                v.reciprocal(ms[:], root[:])
                dve.drain()
                v.tensor_tensor(diag[:], ident[:].unsqueeze(1).broadcast_to([P, TT, P]),
                                ms[:].unsqueeze(2).broadcast_to([P, TT, P]), ALU.mult).then_inc(s_dg, 1)
                dve.wait_ge(s_rb, n + 1)

            def norm(l, n, chunks, which):
                rstd(n)
                shift = (0, 24)[which]
                for c8 in range(KD + 1):
                    if c8 < KD:
                        if c8 >= 3:
                            dve.wait_ge(s_hlo, chunks + c8 - 2)
                        v.scalar_tensor_tensor(out=hm[:, c8 % 3, :], in0=xT[:, c8, :],
                                               scalar=am[:, which, c8:c8 + 1], in1=bank[7],
                                               op0=ALU.mult, op1=ALU.mult).then_inc(s_hm, 1)
                    if c8 >= 1:
                        b = c8 - 1
                        dve.wait_ge(s_hhi, chunks + b + 1)
                        v.scalar_tensor_tensor(out=h_lo[:, b, :], in0=hm[:, b % 3, :],
                                               scalar=mod[:, shift + b:shift + b + 1],
                                               in1=h_hi[:, b, :].bitcast(F32),
                                               op0=ALU.add, op1=ALU.subtract).then_inc(s_hlo, 1)

            def x_update(l, gate, ada=None):
                for q in range(4):
                    for i in (4, 5) if q == 0 else (5 + q,) if q < 3 else ():
                        if ada is not None:
                            ada(l, AUNITS + i)
                    unit_used(dve, l, U_OUT + q if gate == 16 else U_DOWN + 3 * q + 2)
                    for e in range(2):
                        c8 = 2 * q + e
                        ps = (pair((q + 2) % 3) if gate == 16 else pair((q + 1) % 3))[e]
                        v.scalar_tensor_tensor(out=xT[:, c8, :], in0=ps, scalar=mod[:, gate + c8:gate + c8 + 1],
                                               in1=xT[:, c8, :], op0=ALU.mult, op1=ALU.add).then_inc(s_xu, 1)

            def multiply(j, src, sums):
                cols, dst = src.rearrange("p (k n) -> p k n", k=KD // 2), sums[:, j // 2 % 2, :]
                for kk in range(KD // 2):
                    k = j % 2 * (KD // 2) + kk
                    if k == 0:
                        last = v.tensor_scalar(dst, cols[:, kk, :], cact[:, k:k + 1], None, ALU.mult)
                    else:
                        last = v.scalar_tensor_tensor(out=dst, in0=cols[:, kk, :], scalar=cact[:, k:k + 1], in1=dst,
                                                      op0=ALU.mult, op1=ALU.add)
                    if kk == KD // 2 - 1:
                        last.then_inc(s_aused, 1)
                    if k < KD - 1:
                        dve.drain()
                    else:
                        dve.drain().then_inc(s_asum, 1)

            def ada(l, j):
                if j % 2 == 0:
                    dve.drain()
                    dve.wait_ge(s_ag, l * (AUNITS // 2) + j // 2 - 1)
                if j < AUNITS:
                    dve.wait_ge(s_a[j % ARING],
                                l * (16 * (AUNITS - EARLY) // ARING) + 16 * ((j - EARLY) // ARING + 1))
                    multiply(j, a_slot[j % ARING], asum)
                else:
                    dve.wait_ge(s_e[j - AUNITS], 16 * l + 32)
                    multiply(j, a_slot[1], asum)

            dve.wait_ge(s_cact, 1)
            for j in range(2, EARLY):
                if j % 2 == 0 and j >= 6:
                    dve.wait_ge(s_ag, j // 2 - 1)
                dve.wait_ge(s_e[j], 16)
                multiply(j, a_early[j], asum0)
            with dve.Fori(0, L) as l:
                flat = par_all[:].rearrange("p a b -> p (a b)")
                at = 0
                for name, n in PARS:
                    v.tensor_copy(par[:, at:at + n], flat[:, bass.ds(l * step_of[name] + where[name], n)])
                    at += n
                dve.drain()
                dve.wait_ge(s_ag, l * (AUNITS // 2) + EARLY // 2)
                v.tensor_tensor(mod[:, 0:16], bank[6][:, 0:16], par[:, AB:AB + 16], ALU.add)
                dve.drain()
                v.scalar_tensor_tensor(out=am[:, 0, :], in0=mod[:, 8:16], scalar=1.0, in1=par[:, N1:N1 + KD],
                                       op0=ALU.add, op1=ALU.mult)
                dve.drain().then_inc(s_mod, 1)
                norm(l, 2 * l, 2 * KD * l, 0)

                def doubled(j, t, src):
                    return v.tensor_copy(tok[:, j:j + NG, t, :].rearrange("p g (s d) -> p g s d", s=2),
                                         src.rearrange("p (g s d) -> p g s d", g=NG, s=1)
                                         .broadcast_to([P, NG, 2, DH]))

                for j in range(EARLY, 16):
                    ada(l, j)
                for i in range(TT, 3 * TT):
                    group, t = i // TT, i % TT
                    if i == 2 * TT:
                        for j in range(16, 18):
                            ada(l, j)
                    projected(dve, l, group, t)
                    ps = bank[i % PB]
                    if group == 1:
                        doubled(J_X, t, ps[:, 0:128])
                        doubled(J_X + 2, t, ps[:, 128:256])
                        doubled(J_K, t, ps[:, 256:384])
                        last = v.tensor_copy(v_sw[:, t, 0, :, 0:DH],
                                             ps[:, 384:512].rearrange("p (g d) -> p g d", g=NG))
                    else:
                        doubled(J_K + 2, t, ps[:, 0:128])
                        v.tensor_copy(v_sw[:, t, 1, :, 0:DH], ps[:, 128:256].rearrange("p (g d) -> p g d", g=NG))
                        last = v.tensor_copy(gif[:, t, :], ps[:, 256:288])
                    last.then_inc(s_pev, 1)
                dve.drain()
                dve.wait_ge(s_sin, 1)
                dve.wait_ge(s_qev, l * TT + TT)
                heads = tok[:, 0:14].rearrange("p j t (s d) -> p j (t s) d", d=DH)
                x1, x2 = heads[:, :, :, 0:HALF], heads[:, :, :, HALF:2 * HALF]
                cosb, sinb = (m[:].rearrange("p t s d -> p (t s) d").unsqueeze(1)
                              .broadcast_to([P, 14, 2 * TT, HALF]) for m in (cos, sin))
                v.tensor_tensor(rt[:, 0], x1, sinb, ALU.mult)
                v.tensor_tensor(rt[:, 1], x2, sinb, ALU.mult)
                dve.drain()
                v.tensor_tensor(x1, x1, cosb, ALU.mult)
                v.tensor_tensor(x2, x2, cosb, ALU.mult)
                dve.drain()
                v.tensor_tensor(x1, x1, rt[:, 1], ALU.subtract)
                v.tensor_tensor(x2, x2, rt[:, 0], ALU.add)
                dve.drain().then_inc(s_rope, 1)
                for j in range(18, AUNITS):
                    ada(l, j)
                dve.wait_ge(s_ag, l * (AUNITS // 2) + AUNITS // 2)
                v.tensor_tensor(mod[:, 16:48], bank[6][:, 16:48], par[:, AB + 16:AB + 48], ALU.add)
                v.memset(hidk[:], 0.0)
                v.memset(hidv[:], 0.0)
                v.memset(vcmp[:], 0.0)
                dve.drain()
                v.scalar_tensor_tensor(out=am[:, 1, :], in0=mod[:, 32:40], scalar=1.0, in1=par[:, N2:N2 + KD],
                                       op0=ALU.add, op1=ALU.mult)
                dve.drain().then_inc(s_mod, 1)
                dve.wait_ge(s_ift, l + 1)
                v.tensor_scalar(ib[:], bank[5][0:MH, :], gate_b[:, bass.ds(l, 1), 0:1].rearrange("h a b -> h (a b)"),
                                None, ALU.add)
                v.tensor_scalar(fb[:], bank[7][0:MH, :], gate_b[:, bass.ds(l, 1), 1:2].rearrange("h a b -> h (a b)"),
                                None, ALU.add)
                dve.drain()
                v.scalar_tensor_tensor(out=fe[:], in0=fb[:], scalar=-1.0, in1=fb[:], op0=ALU.mult, op1=ALU.max)
                dve.drain().then_inc(s_ib, 1)
                for n in range(4):
                    dve.wait_ge(s_tp, l * NJ + n + 1)
                    for half in range(2):
                        p0, p1 = half * DH, (half + 1) * DH
                        src = bank[T_BANK[n]][p0:p1, :].rearrange("p (n c s) -> p n c s", s=2, c=CS // 2)
                        for ab in range(2):
                            col = CP + n // 2 * CS + ab * (CS // 2)
                            last = v.tensor_tensor(
                                xab[p0:p1, n, ab, :].rearrange("p (n c) -> p n c", c=CS // 2), src[:, :, :, half],
                                par[p0:p1, col:col + CS // 2].unsqueeze(1).broadcast_to([DH, NCP, CS // 2]),
                                ALU.add)
                    last.then_inc(s_tev, 1)
                for n in range(4):
                    dve.wait_ge(s_thi, l * (NJ - 4) + n + 1)
                    v.tensor_tensor(qk[0:DH, J_X + n, :], bank[T_BANK[n]][0:DH, :], qk[0:DH, J_K + n, :].bitcast(F32),
                                    ALU.subtract)
                    row = DH + n // NG
                    v.tensor_copy(qk[DH:DH + 2, J_X + n, :], ident[DH:DH + 2, row:row + 1].broadcast_to([2, T]))\
                        .then_inc(s_tev, 1)
                for h in range(NH):
                    dve.wait_ge(s_thi, l * (NJ - 4) + 4 + h + 1)
                    low = qk[DH:P, h, :]
                    v.scalar_tensor_tensor(out=low, in0=bank[T_BANK[h % 4]][DH:P, :], scalar=DH ** -0.5,
                                           in1=low.bitcast(F32), op0=ALU.mult, op1=ALU.subtract).then_inc(s_tev, 1)

                def conv_rest(c0):
                    for k in (2, 1, 0):
                        sh = MC - 1 - k
                        for c8 in (c0, c0 + 1):
                            if k == 2 and c0 >= MH:
                                dve.wait_ge(s_craw, l * MH + c8 - MH + 1)
                            elif k == 2:
                                dve.wait_ge(s_cv1, l * 2 * MH + c8 + 1)
                            last = v.scalar_tensor_tensor(
                                out=mqk[:, c8, sh:T], in0=(bank[c8 % 4] if c0 < MH else craw[c8 - MH])[:, 0:T - sh],
                                scalar=par[:, MW + k * KD + c8:MW + k * KD + c8 + 1], in1=mqk[:, c8, sh:T],
                                op0=ALU.mult, op1=ALU.add)
                            if k == 0:
                                last.then_inc(s_cv2, 1)
                        if k:
                            dve.drain()

                conv_rest(0)
                dve.wait_ge(s_cmp, l + 1)
                v.tensor_copy(kcmp[:].rearrange("p g n -> p (g n)"), bank[5][:, 0:NG * NCP])
                for r in range(R):
                    last = v.tensor_copy(vcmp[r * NCP:(r + 1) * NCP, :, r, :],
                                         bank[5][r * NCP:(r + 1) * NCP, 64:64 + NG * DH]
                                         .rearrange("p (g d) -> p g d", g=NG))
                last.then_inc(s_cmpev, 1)
                for t in range(TT):
                    dve.wait_ge(s_cS, l * TT + t + 1)
                    v.tensor_tensor(csc[:, t], bank[4 + t][:, 0:NH * NCP].rearrange("p (h n) -> p h n", h=NH),
                                    cmask[:, t, :].unsqueeze(1).broadcast_to([P, NH, NCP]), ALU.add)
                dve.drain()
                v.tensor_reduce(out=cmx[:], in_=csc[:], axis=AX.X, op=ALU.max)
                dve.drain()
                v.tensor_scalar(cmx[:], cmx[:], NEG / 10, None, ALU.max)
                dve.drain()
                for t in range(TT):
                    v.tensor_tensor(csc[:, t], csc[:, t], cmx[:, t, :].unsqueeze(2).broadcast_to([P, NH, NCP]),
                                    ALU.subtract).then_inc(s_csub, 1)
                conv_rest(2)
                dve.wait_ge(s_ln, l + 1)
                one = ones[0:MH, 0:1].broadcast_to([MH, T])
                v.scalar_tensor_tensor(out=fb[:], in0=fb[:], scalar=0.0, in1=fe[:], op0=ALU.min, op1=ALU.subtract)
                dve.drain()
                v.tensor_tensor_scan(brow[:], one, fb[:], 0.0, ALU.mult, ALU.add)
                dve.drain()
                v.tensor_tensor(ib[:], ib[:], brow[:], ALU.subtract)
                dve.drain()
                v.tensor_tensor_scan(fb[:], one, ib[:], -3.0e38, ALU.mult, ALU.max)
                dve.drain()
                v.tensor_tensor(mrow[:], brow[:], fb[:], ALU.add)
                v.tensor_scalar(a_hi[:], fb[:], -1.0, None, ALU.mult)
                dve.drain()
                v.scalar_tensor_tensor(out=a_lo[:], in0=fb[:], scalar=-1.0, in1=a_hi[:].bitcast(F32),
                                       op0=ALU.mult, op1=ALU.subtract)
                dve.drain().then_inc(s_rows, 1)
                dve.wait_ge(s_cexp, l * TT + TT)
                v.tensor_reduce(out=csum[:], in_=csc[:], axis=AX.X, op=ALU.add)
                dve.drain()
                v.tensor_scalar(csum[:], csum[:], TINY, None, ALU.max)
                dve.drain()
                v.reciprocal(csum[:], csum[:])
                dve.drain()
                dve.wait_ge(s_gat, l + 1)
                gates = gat[:].rearrange("p t (h b) -> p t h b", b=3)
                v.tensor_tensor(csum[:], csum[:], gates[:, :, :, 0], ALU.mult)
                dve.drain()
                for i in range(2):
                    dve.wait_ge(s_cT, l * TT + 2 * i + 2)
                    v.tensor_copy(pT[:, 2 * i:2 * i + 2].rearrange("p t g q -> p (t g q)"), bank[4 + i])\
                        .then_inc(s_cTev, 1)
                for t in range(TT):
                    dve.wait_ge(s_cO, l * TT + t + 1)
                    v.tensor_tensor(mixt[:, t, 0:T].rearrange("p (h d) -> p h d", h=NH),
                                    bank[C_BANK[t]].rearrange("p (h d) -> p h d", h=NH),
                                    csum[:, t, :].unsqueeze(2).broadcast_to([P, NH, DH]), ALU.mult)\
                        .then_inc(s_cev, 1)
                def maxima(w):
                    h, t = w // TT, w % TT
                    b, n = score_bank(w), (t + 1) * P
                    dve.wait_ge(s_S, l * NW + w + 1)
                    v.tensor_reduce(out=nmx[:, h // BH, t, h % BH, :], in_=psum[:, b:b + 2, 0:n],
                                    axis=AX.X, op=ALU.max, negate=True).then_inc(s_nm, 1)

                for w in range(BW):
                    maxima(w)

                def gated(h):
                    dve.wait_ge(s_oT, l * NH + h + 1)
                    ps = psum[:, 6:8, 0:TT * (DH + 1)].rearrange("p b (t d) -> p b t d", t=TT)
                    v.reciprocal(coef[:], ps[:, :, :, DH])
                    dve.drain()
                    v.tensor_tensor(coef[:], coef[:], gates[:, :, h, 1:3].rearrange("p t b -> p b t"), ALU.mult)
                    dve.drain()
                    if h >= 2:
                        dve.wait_ge(s_comb, l * NH + h - 1)
                    v.tensor_tensor(t12[:, h % 2], ps[:, :, :, 0:DH],
                                    coef[:].unsqueeze(3).broadcast_to([P, 2, TT, DH]), ALU.mult)\
                        .then_inc(s_gated, 1)

                def squares(h):
                    dve.wait_ge(s_comb, l * NH + h + 1)
                    v.tensor_reduce(out=ssq[:, :, h], in_=sqb[:], axis=AX.X, op=ALU.add).then_inc(s_asq, 1)

                for z in range(NW):
                    for w in beside(z):
                        maxima(w)
                    if z in CONV_AT:
                        conv_rest(CONV_AT[z])
                    if z % TT == 0 and z:
                        gated(z // TT - 1)
                        if z > TT:
                            squares(z // TT - 2)

                def mixer_low(c8):
                    dve.wait_ge(s_mhi, l * KD + c8 + 1)
                    v.scalar_tensor_tensor(out=h_lo[:, c8, :], in0=bank[c8 % 4],
                                           scalar=par[:, MG + c8:MG + c8 + 1], in1=h_hi[:, c8, :].bitcast(F32),
                                           op0=ALU.mult, op1=ALU.subtract).then_inc(s_mlo, 1)

                def head_out(h):
                    for e in range(2):
                        dve.wait_ge(s_mO, l * 8 + 2 * h + e + 1)
                        ps = bank[6 + e][:, 0:2 * (MD + 1)].rearrange("p (t d) -> p t d", t=2)
                        v.scalar_tensor_tensor(out=den[:, e, :], in0=ps[:, :, MD], scalar=-1.0,
                                               in1=acol[:, 1, 2 * e:2 * e + 2, h], op0=ALU.mult, op1=ALU.max)
                        dve.drain()
                        v.tensor_tensor(den[:, e, :], ps[:, :, MD], den[:, e, :], ALU.max)
                        dve.drain()
                        v.reciprocal(den[:, e, :], den[:, e, :])
                        dve.drain()
                        for i in range(2):
                            t = 2 * e + i
                            last = v.scalar_tensor_tensor(
                                out=mixt[:, t, T + h * MD:T + (h + 1) * MD], in0=ps[:, i, 0:MD],
                                scalar=den[:, e, i:i + 1], in1=mixt[:, t, T + h * MD:T + (h + 1) * MD],
                                op0=ALU.mult, op1=ALU.mult)
                        last.then_inc(s_mev, 1)

                for h in range(MH):
                    for j in range(TT):
                        z, n = h * TT + j, (TT - j) * P
                        dve.wait_ge(s_mW, l * 16 + z + 1)
                        if h >= 2:
                            dve.wait_ge(s_mO, l * 8 + 2 * (h - 1))
                        v.scalar_tensor_tensor(out=mws[:, h % 2, W_OFF[j]:W_OFF[j] + n],
                                               in0=pair(z % 3)[0][:, 0:n], scalar=MSCALE, in1=mw[:, z % 3, 0:n],
                                               op0=ALU.mult, op1=ALU.mult).then_inc(s_mWS, 1)
                        if z == 1:
                            gated(NH - 1)
                        if z == 3:
                            squares(NH - 2)
                            squares(NH - 1)
                        if j == 1 and h >= 1:
                            head_out(h - 1)
                    if h == 1:
                        dve.wait_ge(s_rt2, l * 2 + 1)
                        v.reciprocal(ssq2[:, :, 0:NH], ssq2[:, :, 0:NH])
                        dve.drain()
                        for t in range(TT):
                            o3 = mixt[:, t, 0:T].rearrange("p (h d) -> p h d", h=NH)
                            last = v.tensor_tensor(o3, o3, ssq2[:, t, 0:NH].unsqueeze(2).broadcast_to([P, NH, DH]),
                                                   ALU.mult)
                        last.then_inc(s_mixa, 1)
                head_out(MH - 1)
                for c8 in range(KD // 2):
                    mixer_low(c8)
                dve.wait_ge(s_rt2, l * 2 + 2)
                v.reciprocal(ssq2[:, :, NH:], ssq2[:, :, NH:])
                dve.drain()
                for h in range(MH):
                    o3 = mixt[:, :, T + h * MD:T + (h + 1) * MD]
                    v.tensor_tensor(o3, o3, ssq2[:, :, NH + h:NH + h + 1].broadcast_to([P, TT, MD]), ALU.mult)\
                        .then_inc(s_mixm, 1)
                for c8 in range(KD // 2, KD):
                    mixer_low(c8)
                x_update(l, 16)
                norm(l, 2 * l + 1, 2 * KD * l + KD, 1)

                def hidden_step(l, f, i, idx):
                    a_ps, v_ps = pair(f % 3)
                    y = fy[:, f % 2, :]
                    dve.wait_ge(s_y1, l * KF + i * BODY + (f + 1))
                    v.scalar_tensor_tensor(out=y[:, 1:T], in0=a_ps[:, 0:T - 1],
                                           scalar=par[:, bass.ds(idx + FW + KF, 1)], in1=y[:, 1:T],
                                           op0=ALU.mult, op1=ALU.add)
                    dve.drain()
                    v.scalar_tensor_tensor(out=y[:, 2:T], in0=a_ps[:, 0:T - 2],
                                           scalar=par[:, bass.ds(idx + FW, 1)], in1=y[:, 2:T],
                                           op0=ALU.mult, op1=ALU.add).then_inc(s_y2, 1)
                    dve.wait_ge(s_z, l * KF + i * BODY + (f + 1))
                    dve.wait_ge(s_flo, l * KF + i * BODY + (f - 1 + CREDIT))
                    v.tensor_tensor(ft[:, f % 2, :], v_ps, y, ALU.mult).then_inc(s_fv, 1)

                with dve.Fori(0, LOOPED // BODY) as i:
                    for f in range(BODY):
                        hidden_step(l, f, i, i * BODY + f)
                for f in range(LOOPED, KF):
                    hidden_step(l, f, 0, f)
                    ada(l, AUNITS + f - LOOPED)
                x_update(l, 40, ada)
            rstd(2 * L)
            for c8 in range(KD):
                if c8 >= 3:
                    dve.wait_ge(s_yT, c8 - 2)
                v.scalar_tensor_tensor(out=hm[:, c8 % 3, :], in0=xT[:, c8, :],
                                       scalar=par_all[:, FROW // P, FROW % P + c8:FROW % P + c8 + 1], in1=bank[7],
                                       op0=ALU.mult, op1=ALU.mult).then_inc(s_fin, 1)

        @block.tensor
        def _(pe):
            m = nc.tensor.matmul

            pe.drain().then_inc(s_used, CREDIT)
            pe.wait_ge(s_const, 1)
            pe.wait_ge(s_par, 16 * len(loads))
            for i in range(4):
                n = tile_rows[i]
                last = nc.tensor.transpose(bank[7][:, i * P:i * P + n], prow[0:n, i, :], ident[0:n, 0:n])
            last.then_inc(s_prT, 1)
            pe.wait_ge(s_x, 16 * TT)
            for c8 in range(KD):
                if c8 >= 6:
                    pe.wait_ge(s_xu, c8 - 5)
                for t in range(TT):
                    last = nc.tensor.transpose(bank[c8 % 6][:, t * P:(t + 1) * P],
                                               xtok[:, t, c8 * P:(c8 + 1) * P], ident[:])
                last.then_inc(s_xT, 1)

            def ada_sums(l, g, src=asum):
                pe.wait_ge(s_asum, l * (AUNITS // 2) + g + 1)
                for i in range(4):
                    at = 4 * (g % (AUNITS // 2)) + i
                    last = m(bank[6][:, at:at + 1], src[:, g % 2, i * P:(i + 1) * P], ones[:, 0:1],
                             start=True, stop=True)
                last.then_inc(s_ag, 1)

            def sum_squares(n):
                pe.wait_ge(s_sqa, n + 1)
                for i, src in enumerate((2, 0, 1)):
                    if i:
                        pe.wait_ge(s_sql, 2 * n + i)
                    for t in range(TT):
                        last = m(bank[7][:, i * TT + t:i * TT + t + 1], hm[:, src, t * P:(t + 1) * P], ones[:, 0:1],
                                 start=True, stop=True)
                last.then_inc(s_ss, 1)

            def spread(n):
                pe.wait_ge(s_dg, n + 1)
                m(bank[7], ones[:], diag[:].rearrange("p t q -> p (t q)"), start=True, stop=True).then_inc(s_rb, 1)

            def three(ps, l_hi, l_lo, r_hi, r_lo, first, last):
                m(ps, l_hi, r_hi, start=first, stop=False)
                m(ps, l_hi, r_lo, start=False, stop=False)
                return m(ps, l_lo, r_hi, start=False, stop=last)

            def tile_free(l, group, t):
                if group < 3:
                    b = group * TT + t - PB
                    if b >= TT:
                        pe.wait_ge(s_pev, l * 2 * TT + b - TT + 1)
                    elif b >= 0:
                        pe.wait_ge(s_qev, l * TT + b + 1)
                elif group == 3:
                    last = max(i for i in range(3 * TT) if i % PB == t)
                    pe.wait_ge(s_pev, l * 2 * TT + last - TT + 1)
                else:
                    pe.wait_ge(s_mvev, l * TT + t + 1)

            def token_unit(l, u, n, between=None):
                group = u // 2
                pe.wait_ge(s_lo, l * UNITS + u + 1)
                for kk in range(4):
                    k = (u % 2) * 4 + kk
                    if u < 2:
                        pe.wait_ge(s_hlo, l * 2 * KD + k + 1)
                    for t in range(TT):
                        if k == 0:
                            tile_free(l, group, t)
                        tile = slice(t * P, (t + 1) * P)
                        b = (group * TT + t) % PB if group < 3 else t
                        last = three(bank[b][:, 0:n], h_hi[:, k, tile], h_lo[:, k, tile],
                                     w_hi[:, u % HI, kk * n:(kk + 1) * n], w_lo[:, slot_of(u), kk * n:(kk + 1) * n],
                                     k == 0, k == KD - 1)
                        if k == KD - 1 and t < TT - 1:
                            last.then_inc(s_proj, 1)
                    if kk == 3:
                        last.then_inc(s_used, 1)
                    if between is not None:
                        between(kk)

            def column_unit(u, banks, nk, rhs, first, last, ready=None, between=None):
                for kk in range(nk):
                    if ready is not None:
                        ready(kk)
                    for e in range(2):
                        at = kk * 256 + e * P
                        hi, lo = rhs(kk)
                        ins = three(banks[e], w_hi[:, u % HI, at:at + P], w_lo[:, slot_of(u), at:at + P], hi, lo,
                                    first and kk == 0, last and kk == nk - 1)
                    if kk == nk - 1:
                        ins.then_inc(s_used, 1)
                    if between is not None:
                        between(kk)

            def h_of(k):
                return h_hi[:, k, :], h_lo[:, k, :]

            pe.wait_ge(s_cact, 1)
            for i in range(4):
                for k in range(KD):
                    if i == 0 and k % 4 == 0:
                        pe.wait_ge(s_e[k // 4], 16)
                    at = k % 4 * T + i * P
                    last = m(bank[6][:, i:i + 1], a_early[k // 4][:, at:at + P], cact[:, k:k + 1],
                             start=(k == 0), stop=(k == KD - 1))
            last.then_inc(s_ag, 1)
            pe.drain().then_inc(s_aused, 2)
            pe.drain().then_inc(s_asum, 1)
            ada_sums(0, 1, asum0)
            sum_squares(0)
            for g in range(2, EARLY // 2):
                ada_sums(0, g, asum0)
            with pe.Fori(0, L) as l:
                spread(2 * l)
                ada_at_step = {(1, 3): 4, (2, 1): 5, (2, 3): 6, (3, 1): 7, (5, 3): 8, (7, 1): 9, (7, 3): 10,
                               (8, 0): 11}

                def beside_ada(u):
                    def between(kk):
                        if (u, kk) in ada_at_step:
                            ada_sums(l, ada_at_step[u, kk])
                    return between

                for u in range(U_MV):
                    token_unit(l, u, 512 if u < 4 else 288, beside_ada(u))

                def transpose_chunk(n):
                    j = (J_X + n, J_K + n - 4, n - 8, n - 8)[n // 4]
                    if n == 0:
                        pe.wait_ge(s_rope, l + 1)
                    elif n in (1, 2):
                        pe.wait_ge(s_ib, l + 1)
                    elif n == 3:
                        pe.wait_ge(s_mod, l * 2 + 2)
                    else:
                        pe.wait_ge(s_tev, l * NJ + n - 3)
                    for t in range(TT):
                        last = nc.tensor.transpose(bank[T_BANK[n % 4]][:, t * P:(t + 1) * P], tok[:, j, t, :],
                                                   ident[:])
                    last.then_inc(s_tp, 1)

                def gate_rows():
                    pe.wait_ge(s_pev, l * 2 * TT + 2 * TT)
                    for i, b in enumerate((5, 7)):
                        for t in range(TT):
                            last = nc.tensor.transpose(bank[b][0:MH, t * P:(t + 1) * P],
                                                       gif[:, t, NGATE + i * MH:NGATE + (i + 1) * MH], ident[:])
                    last.then_inc(s_ift, 1)

                def compress(i):
                    for c16 in range(CB // 2):
                        ab, cc = c16 // (CS // 2), c16 % (CS // 2)
                        x4 = xab[:, NG * i:NG * (i + 1), ab, :].rearrange("p g (n c) -> p g n c", c=CS // 2)
                        at = i * NG * NCP
                        last = m(bank[4][0:DH, at:at + NG * NCP].rearrange("p (g n) -> p g n", g=NG)[:, :, 0:NC],
                                 w1[:, i, c16, :], x4[:, :, ab:ab + NC, cc],
                                 start=(c16 == 0), stop=(c16 == CB // 2 - 1))
                    if i == 1:
                        last.then_inc(s_hid, 1)

                def compressed():
                    pe.wait_ge(s_hids, l + 1)
                    for g in range(NG):
                        m(bank[5][:, 64 + g * DH:64 + (g + 1) * DH], hidv[:, g].rearrange("p r n -> p (r n)"),
                          w2[:, 1, :], start=True, stop=True)
                    for g in range(NG):
                        for half in range(2):
                            last = m(bank[5][half * DH:(half + 1) * DH, g * NCP:(g + 1) * NCP], w2[:, 0, :],
                                     hidk[:, g, :], start=True, stop=True)
                    last.then_inc(s_cmp, 1)

                def compressed_scores(t):
                    if t == 0:
                        pe.wait_ge(s_cmpev, l + 1)
                    for h in range(NH):
                        last = m(bank[4 + t][:, h * NCP:(h + 1) * NCP], qk[:, h, t * P:(t + 1) * P].bitcast(F32),
                                 kcmp[:, h // R, :], start=True, stop=True)
                    last.then_inc(s_cS, 1)

                def compressed_transposes(t):
                    pe.wait_ge(s_cexp, l * TT + TT)
                    for g in range(NG):
                        at = (t % 2) * 256 + g * P
                        last = nc.tensor.transpose(bank[4 + t // 2][:, at:at + P],
                                                   csc[:, t, g * R:(g + 1) * R, :].rearrange("p r n -> p (r n)"),
                                                   ident[:])
                    last.then_inc(s_cT, 1)

                def compressed_outputs(t):
                    pe.wait_ge(s_cTev, l * 2 + (2 if t >= 2 else t // 2 + 1))
                    for g in range(NG):
                        last = m(bank[C_BANK[t]][:, g * R * DH:(g + 1) * R * DH], pT[:, t, g, :],
                                 vcmp[:, g].rearrange("p r d -> p (r d)"), start=True, stop=True)
                    last.then_inc(s_cO, 1)

                def gate_columns():
                    pe.wait_ge(s_rows, l + 1)
                    pe.wait_ge(s_cev, l * TT + 1)
                    for i, rows in enumerate((ib, mrow)):
                        for t in range(TT):
                            last = m(bank[6][:, i * 16 + t * MH:i * 16 + (t + 1) * MH],
                                     rows[:, t * P:(t + 1) * P], ident[0:MH, 0:MH], start=True, stop=True)
                    last.then_inc(s_col, 1)

                def scores(w, after_head=None):
                    h, t = w // TT, w % TT
                    b, n = score_bank(w), (t + 1) * P
                    if w == 0:
                        pe.wait_ge(s_cev, l * TT + TT)
                        pe.wait_ge(s_acol, l + 1)
                    elif after_head is not None:
                        pe.wait_ge(s_gated, l * NH + after_head + 1)
                    elif w >= BW:
                        if w == BW:
                            pe.wait_ge(s_nrow, l * NB + 1)
                        pe.wait_ge(s_nm, l * NW + w)
                    elif w >= 2:
                        pe.wait_ge(s_nm, l * NW + w - 1)
                    for br in range(2):
                        ps = bank[b + br]
                        m(ps[:, 0:n], qk[:, h, t * P:(t + 1) * P], qk[:, J_K + 2 * br + h // R, 0:n],
                          start=True, stop=False)
                        last = m(ps[:, t * P:n], identb[:], tri[:], start=False, stop=True)
                    last.then_inc(s_S, 1)

                def max_rows(b):
                    pe.wait_ge(s_nm, l * NW + (b + 1) * BW)
                    for h in range(BH):
                        for t in range(TT):
                            last = m(bank[6 + h][DH:DH + 2, t * P:(t + 1) * P], nmx[:, b, t, h, :], ident[:],
                                     start=True, stop=True)
                    last.then_inc(s_nr, 1)

                def beside_mo1(kk):
                    if kk == 0:
                        ada_sums(l, ada_at_step[U_MO, 0])
                        gate_rows()
                    for n in ((0,), (), (1, 2), (3, 4))[kk]:
                        transpose_chunk(n)

                def beside_mo2(kk):
                    for n in range(5 + 3 * kk, min(8 + 3 * kk, NJ)):
                        transpose_chunk(n)

                def beside_mqk(i, kk):
                    if i == 0:
                        if kk == 0:
                            pe.wait_ge(s_cw, l * 48 + 48)
                            pe.wait_ge(s_tev, l * NJ + NJ - 3)
                        if kk in (0, 3):
                            compress(kk // 3)
                    elif i == 1:
                        if kk == 3:
                            pe.wait_ge(s_tev, l * NJ + NJ)
                            compressed()
                        if kk >= 4:
                            compressed_scores(kk - 4)
                    elif i == 2:
                        if kk in (6, 7):
                            compressed_transposes(2 * (kk - 6))
                            compressed_transposes(2 * (kk - 6) + 1)
                    else:
                        if kk in (1, 2):
                            compressed_outputs(2 * (kk - 1))
                            compressed_outputs(2 * (kk - 1) + 1)
                        if kk == 3:
                            gate_columns()
                        for w in ((), (), (), (), (0,), (1,), (2, 3), (4, 5))[kk]:
                            scores(w)

                token_unit(l, U_MV, 512, beside_ada(U_MV))
                token_unit(l, U_MV + 1, 512, beside_ada(U_MV + 1))
                token_unit(l, U_MO, 512, beside_mo1)
                token_unit(l, U_MO + 1, 512, beside_mo2)
                for i in range(4):
                    u = U_MQK + i
                    pe.wait_ge(s_lo, l * UNITS + u + 1)
                    if i < 2:
                        pe.wait_ge(s_moev, l * TT + 2 * i + 2)
                    else:
                        pe.wait_ge(s_cv2, l * 2 * MH + 2 * i - 2)
                    column_unit(u, (bank[2 * i % 4], bank[(2 * i + 1) % 4]), KD, h_of, True, True,
                                between=lambda kk: beside_mqk(i, kk))
                for w in range(6, BW):
                    scores(w)
                max_rows(0)

                def key_scores(z):
                    h, kb = z // TT, z % TT
                    n, g = (TT - kb) * P, h // R
                    keys = slice(kb * P, (kb + 1) * P)
                    if z == 0:
                        pe.wait_ge(s_craw, l * MH + MH)
                    if z % BW == 0:
                        pe.wait_ge(s_nrow, l * NB + z // BW + 1)
                    if z == 0:
                        pe.wait_ge(s_qm0, l + 1)
                    elif kb == 0 and h >= BH:
                        pe.wait_ge(s_qm, l * (NH - BH) + h - BH + 1)
                    if z >= 2:
                        pe.wait_ge(s_exp, l * NW + z - 1)
                    for br in range(2):
                        ps = bank[2 * (z % 2) + br]
                        q = qk[:, h, kb * P:T]
                        m(ps[:, 0:n], qk[:, J_K + 2 * br + g, keys], q, start=True, stop=False)
                        m(ps[:, 0:n], qk[0:DH + 2, J_X + 2 * br + g, keys], qm[:, h, kb * P:T],
                          start=False, stop=False)
                        last = m(ps[:, 0:P], identb[:], triT[:], start=False, stop=True)
                    last.then_inc(s_ST, 1)

                def values(z):
                    h, kb = z // TT, z % TT
                    pe.wait_ge(s_exp, l * NW + z + 1)
                    if kb == 0:
                        if h == 0:
                            pe.wait_ge(s_nm, l * NW + BW)
                        else:
                            pe.wait_ge(s_oev, l * NH + h)
                    for br in range(2):
                        last = m(bank[4 + br][0:DH + 1, kb * P:T], v_sw[:, kb, br, h // R, :],
                                 pt[:, z % 2, br, 0:(TT - kb) * P], start=(kb == 0), stop=(kb == TT - 1),
                                 skip_group_check=True)
                    last.then_inc(s_PV, 1)

                def outputs(h):
                    pe.wait_ge(s_oev, l * NH + h + 1)
                    z = TT * (h + 1)
                    if z < NW and len(beside(z)):
                        pe.wait_ge(s_nm, l * NW + done_beside(z))
                    elif z == NW - BW:
                        pe.wait_ge(s_nrow, l * NB + NB)
                    else:
                        pe.wait_ge(s_gated, l * NH + h)
                    for br in range(2):
                        for t in range(TT):
                            last = nc.tensor.transpose(bank[6 + br][:, t * (DH + 1):(t + 1) * (DH + 1)],
                                                       ot[:, br, t * P:(t + 1) * P], ident[0:DH + 1, 0:DH + 1])
                    last.then_inc(s_oT, 1)

                pe.wait_ge(s_vone, l + 1)
                key_scores(0)
                key_scores(1)
                for z in range(NW):
                    ahead = AHEAD[z % BW]
                    for w in beside(z)[:ahead]:
                        scores(w)
                    if z + 2 < NW:
                        key_scores(z + 2)
                    for w in beside(z)[ahead:]:
                        scores(w, z // TT - 1 if z > TT and z % TT == 1 else None)
                    if z // BW + 1 < NB and z % BW == TT + 1:
                        pe.wait_ge(s_gated, l * NH + z // TT)
                        max_rows(z // BW + 1)
                    values(z)
                    if z % TT == 0 and z:
                        outputs(z // TT - 1)

                def sources(z):
                    h, j = z // TT, z % TT
                    n = (TT - j) * P
                    if z >= 3:
                        pe.wait_ge(s_mWS, l * 16 + z - 2)
                    ps, bc = pair(z % 3)
                    m(ps[:, 0:n], mqk[:, MH + h, j * P:(j + 1) * P], mqk[:, h, j * P:T], start=True, stop=True)
                    for i, part in enumerate((a_hi, a_lo)):
                        m(bc[:, 0:n], identr[0:MH, h:h + 1].broadcast_to([MH, P]), part[:, j * P:T],
                          start=(i == 0), stop=False)
                    m(bc[:, 0:P], identb[:], triT[:], start=False, stop=True).then_inc(s_mS, 1)

                def head_values(h):
                    pe.wait_ge(s_mWS, l * 16 + 4 * h + 4)
                    for t in range(TT):
                        e = t // 2
                        if t % 2 == 0:
                            if h >= 1:
                                pe.wait_ge(s_mev, l * 8 + 2 * (h - 1) + e + 1)
                        for j in range(t + 1):
                            at = W_OFF[j] + (t - j) * P
                            last = m(bank[6 + e][:, (t % 2) * (MD + 1):(t % 2 + 1) * (MD + 1)],
                                     mws[:, h % 2, at:at + P], v_m[:, j, h, :], start=(j == 0), stop=(j == t))
                        if t % 2:
                            last.then_inc(s_mO, 1)

                pe.wait_ge(s_cv3, l * 2 * MH + 2 * MH)
                for z in range(MH * TT):
                    if z == 2:
                        outputs(NH - 1)
                    if z == TT + 1:
                        pe.wait_ge(s_gated, l * NH + NH)
                    sources(z)
                    if z % TT == 1 and z > TT:
                        head_values(z // TT - 1)
                head_values(MH - 1)

                def mixed_chunk(c8):
                    if c8 >= 4:
                        pe.wait_ge(s_mixm, l * MH + c8 - 3)
                        pe.wait_ge(s_mlo, l * KD + c8 - 3)
                    for t in range(TT):
                        last = nc.tensor.transpose(bank[c8 % 4][:, t * P:(t + 1) * P],
                                                   mixt[:, t, c8 * P:(c8 + 1) * P], ident[:])
                    last.then_inc(s_mT, 1)

                pe.wait_ge(s_mixa, l + 1)
                for c8 in range(KD // 2):
                    mixed_chunk(c8)
                for q in range(4):
                    u = U_OUT + q
                    pe.wait_ge(s_lo, l * UNITS + u + 1)
                    if q == 3:
                        pe.wait_ge(s_xu, KD + 2 * KD * l + 2)

                    def mixed(kk):
                        if kk == KD // 2:
                            for c8 in range(KD // 2, KD):
                                mixed_chunk(c8)
                        pe.wait_ge(s_mlo, l * KD + kk + 1)

                    column_unit(u, pair((q + 2) % 3), KD, h_of, True, True, mixed if q == 0 else None)
                sum_squares(2 * l + 1)
                spread(2 * l + 1)

                def up(l, f, i):
                    pe.wait_ge(s_lo, l * UNITS + i * BODY + (U_UP + f + 1))
                    pe.wait_ge(s_fv, l * KF + i * BODY + (f - 2 + CREDIT))
                    for kk in range(KD):
                        if f == 0:
                            pe.wait_ge(s_hlo, l * 2 * KD + KD + kk + 1)
                        for e in range(2):
                            at = kk * 256 + e * P
                            last = three(pair(f % 3)[e], w_hi[:, f % HI, at:at + P], w_lo[:, f % RAW, at:at + P],
                                         h_hi[:, kk, :], h_lo[:, kk, :], kk == 0, kk == KD - 1)
                    last.then_inc(s_used, 1)

                with pe.Fori(0, LOOPED // BODY) as i:
                    for f in range(BODY):
                        up(l, f, i)
                for f in range(LOOPED, KF):
                    up(l, f, 0)
                    if f == LOOPED + 3:
                        ada_sums(l, AUNITS // 2)
                for d in range(UNITS - U_DOWN):
                    if d in (2, 5, 8):
                        ada_sums(l, AUNITS // 2 + {2: 1, 5: 2, 8: 3}[d])
                    u, q = U_DOWN + d, d // 3
                    k0, k1 = DOWN_K[d % 3]
                    pe.wait_ge(s_lo, l * UNITS + u + 1)
                    if d % 3 == 0:
                        if q < 3:
                            pe.wait_ge(s_fv, l * KF + 20 + q + CREDIT)
                        else:
                            pe.wait_ge(s_xu, 2 * KD + 2 * KD * l + 2)

                    def made(kk):
                        pe.wait_ge(s_flo, l * KF + k0 + kk + 1 + CREDIT)

                    column_unit(u, pair((q + 1) % 3), k1 - k0,
                                lambda kk: (hid_hi[:, k0 + kk, :], hid_lo[:, k0 + kk, :]),
                                d % 3 == 0, d % 3 == 2, made if q == 0 else None)
                sum_squares(2 * l + 2)
            spread(2 * L)
            for c8 in range(KD):
                pe.wait_ge(s_fin, c8 + 1)
                if c8 >= 4:
                    pe.wait_ge(s_yev, c8 - 3)
                for t in range(TT):
                    last = nc.tensor.transpose(bank[c8 % 4][:, t * P:(t + 1) * P],
                                               hm[:, c8 % 3, t * P:(t + 1) * P], ident[:])
                last.then_inc(s_yT, 1)


NAMES = ["x", "c", "positions", "norm1_g", "norm2_g", "ada_w", "ada_b", "w_in", "cmp_pos", "cmp_w1", "cmp_w2",
         "att_norm_g", "m_conv_w", "m_conv_b", "m_gate_b", "m_norm_g", "w_out", "ffn_up", "ffn_conv_w",
         "ffn_conv_b", "ffn_down", "final_g"]


def kernel(**inputs):
    import concourse.bacc as bacc
    from concourse.bass_utils import run_bass_kernel_spmd

    nc = bacc.Bacc("TRN2", target_bir_lowering=False, num_devices=1)
    arrays, args = {}, []
    for name in NAMES:
        a = np.ascontiguousarray(inputs[name])
        arrays[f"in_{name}"] = a
        args.append(nc.dram_tensor(f"in_{name}", a.shape, dt.from_np(a.dtype), kind="ExternalInput").ap())
    out = nc.dram_tensor("out", (1, T, D), F32, kind="ExternalOutput").ap()
    build(nc, *args, out)
    r = run_bass_kernel_spmd(nc, [arrays], core_ids=[0])
    return r.results[0]["out"]
```
